# Optimizing a Trainium2 kernel written in Bass

```python
import jax, jax.numpy as jnp
from jax import lax
import numpy as np
import math

D_MODEL = 2048
BATCH = 1
SEQ = 256
DEPTH = 1

GRID_W = 64
CTX_LEN = 256
EPS = 1e-6

MLA_HEADS = 8
MLA_NOPE = 128
MLA_ROPE = 64
MLA_V = 128
MLA_Q_RANK = 512
MLA_KV_RANK = 512
MLA_SCALE = (MLA_NOPE + MLA_ROPE) ** -0.5
ROPE_BASE = 10000.0

NA_HEADS = 4
NA_HEAD_DIM = 128
NA_KH = 8
NA_KW = 16
NA_SCALE = NA_HEAD_DIM ** -0.5

FN_GROUPS = 4
FN_CH = 128

MLA_WIDTH = MLA_HEADS * MLA_V
NA_WIDTH = NA_HEADS * NA_HEAD_DIM
FN_WIDTH = FN_GROUPS * FN_CH
MIX_WIDTH = MLA_WIDTH + NA_WIDTH + FN_WIDTH
IN_SPLITS = (MLA_Q_RANK, MLA_KV_RANK, MLA_ROPE, NA_WIDTH, NA_WIDTH, NA_WIDTH, FN_WIDTH)
IN_COLS = sum(IN_SPLITS)

D_FF = 5632
CONV_W = 3
Q_BLOCK = 128


def rmsnorm(x, g):
    xf = x.astype(jnp.float32)
    y = xf * lax.rsqrt(jnp.mean(xf * xf, axis=-1, keepdims=True) + EPS)
    return (y * g.astype(jnp.float32)).astype(x.dtype)

def split_columns(u):
    offs = np.cumsum(IN_SPLITS)[:-1].tolist()
    return jnp.split(u, offs, axis=-1)

def axial_angles(rows, cols):
    n = MLA_ROPE // 4
    freqs = ROPE_BASE ** (-jnp.arange(n, dtype=jnp.float32) / n)
    ang_r = rows.astype(jnp.float32)[:, None, None] * freqs
    ang_c = cols.astype(jnp.float32)[:, None, None] * freqs
    return ang_r, ang_c

def rotate(x, ang):
    n = x.shape[-1] // 2
    x1, x2 = x[..., :n], x[..., n:]
    cos, sin = jnp.cos(ang).astype(x.dtype), jnp.sin(ang).astype(x.dtype)
    return jnp.concatenate([x1 * cos - x2 * sin, x2 * cos + x1 * sin], axis=-1)

def axial_rope(x, ang_r, ang_c):
    h = x.shape[-1] // 2
    return jnp.concatenate([rotate(x[..., :h], ang_r), rotate(x[..., h:], ang_c)], axis=-1)

def mla_qkv(c_q, c_kv, k_r, g_q, w_uq, g_kv, w_ukv, angles):
    B, L, _ = c_q.shape
    q = (rmsnorm(c_q, g_q) @ w_uq).reshape(B, L, MLA_HEADS, MLA_NOPE + MLA_ROPE)
    kv = (rmsnorm(c_kv, g_kv) @ w_ukv).reshape(B, L, MLA_HEADS, MLA_NOPE + MLA_V)
    q_nope, q_rope = q[..., :MLA_NOPE], q[..., MLA_NOPE:]
    k_nope, v = kv[..., :MLA_NOPE], kv[..., MLA_NOPE:]
    k_rope = k_r[:, :, None, :]
    if angles is not None:
        q_rope = axial_rope(q_rope, *angles)
        k_rope = axial_rope(k_rope, *angles)
    q = jnp.concatenate([q_nope, q_rope], axis=-1)
    k = jnp.concatenate([k_nope, jnp.broadcast_to(k_rope, (B, L, MLA_HEADS, MLA_ROPE))], axis=-1)
    return q, k, v

def blocked_attention(q, k, v, scale):
    B, L, H, dq = q.shape
    dv = v.shape[-1]
    nb = L // Q_BLOCK
    qb = q.reshape(B, nb, Q_BLOCK, H, dq).transpose(1, 0, 2, 3, 4)

    def one_block(qi):
        s = jnp.einsum('bqhd,bkhd->bhqk', qi, k, preferred_element_type=jnp.float32) * scale
        p = jax.nn.softmax(s, axis=-1).astype(v.dtype)
        return jnp.einsum('bhqk,bkhd->bqhd', p, v)

    o = lax.map(one_block, qb)
    return o.transpose(1, 0, 2, 3, 4).reshape(B, L, H * dv)

def neighborhood_attention(q, k, v, k_ctx, v_ctx, rpb):
    B, S, H, d = q.shape
    rows = S // GRID_W
    kh = min(NA_KH, rows)
    qg = q.reshape(B, rows, GRID_W, H, d)
    kg = k.reshape(B, rows, GRID_W, H, d)
    vg = v.reshape(B, rows, GRID_W, H, d)
    w_idx = jnp.arange(GRID_W)
    col_start = jnp.clip(w_idx - NA_KW // 2, 0, GRID_W - NA_KW)
    col_idx = col_start[:, None] + jnp.arange(NA_KW)
    rel_col = col_idx - w_idx[:, None] + (NA_KW - 1)
    nwin = kh * NA_KW

    def one_row(r):
        rs = jnp.clip(r - kh // 2, 0, rows - kh)
        q_r = lax.dynamic_index_in_dim(qg, r, axis=1, keepdims=False)
        k_rows = lax.dynamic_slice_in_dim(kg, rs, kh, axis=1)
        v_rows = lax.dynamic_slice_in_dim(vg, rs, kh, axis=1)
        k_win = k_rows[:, :, col_idx]
        v_win = v_rows[:, :, col_idx]
        rel_row = rs + jnp.arange(kh) - r + (NA_KH - 1)
        bias = rpb[:, rel_row[None, :, None], rel_col[:, None, :]]
        s_win = jnp.einsum('bwhd,bawjhd->bhwaj', q_r, k_win, preferred_element_type=jnp.float32) * NA_SCALE
        s_win = s_win + bias.astype(jnp.float32)
        s_ctx = jnp.einsum('bwhd,bchd->bhwc', q_r, k_ctx, preferred_element_type=jnp.float32) * NA_SCALE
        s = jnp.concatenate([s_win.reshape(B, H, GRID_W, nwin), s_ctx], axis=-1)
        p = jax.nn.softmax(s, axis=-1).astype(v.dtype)
        p_win = p[..., :nwin].reshape(B, H, GRID_W, kh, NA_KW)
        p_ctx = p[..., nwin:]
        return (jnp.einsum('bhwaj,bawjhd->bwhd', p_win, v_win)
                + jnp.einsum('bhwc,bchd->bwhd', p_ctx, v_ctx))

    o = lax.map(one_row, jnp.arange(rows))
    return o.transpose(1, 0, 2, 3, 4).reshape(B, S, H * d)

def fourier_mix(f, w_fnet):
    B, L, _ = f.shape
    fg = f.reshape(B, L, FN_GROUPS, FN_CH).astype(jnp.float32)
    spec = jnp.fft.fft2(fg, axes=(1, 3), norm='ortho').real.astype(f.dtype)
    return jnp.einsum('blgc,gcd->blgd', spec, w_fnet).reshape(B, L, FN_WIDTH)

def conv_ffn(h, w_up, conv_w, conv_b, w_down):
    L = h.shape[1]
    u = h @ w_up
    up = jnp.pad(u, ((0, 0), (CONV_W // 2, CONV_W // 2), (0, 0)))
    u = sum(up[:, j:j + L] * conv_w[j] for j in range(CONV_W)) + conv_b
    gate, val = jnp.split(u, 2, axis=-1)
    return (jax.nn.silu(gate) * val) @ w_down

def heads(t, n_heads):
    B, L, _ = t.shape
    return t.reshape(B, L, n_heads, -1)

def first_inputs(seed: int = 0) -> dict:
    key = jax.random.key(seed)
    ks = jax.random.split(key, 24)
    D = D_MODEL

    def nrm(k, shape, scale):
        return jax.random.normal(k, shape, jnp.float32) * scale

    return {
        'x': nrm(ks[0], (BATCH, SEQ, D), 1.0),
        'c': nrm(ks[1], (BATCH, D), 1.0),
        'ctx': nrm(ks[2], (BATCH, CTX_LEN, D), 1.0),
        'c_ctx': nrm(ks[3], (D,), 1.0),
        'w_mod': nrm(ks[4], (DEPTH, D, 6 * D), D ** -0.5),
        'b_mod': nrm(ks[5], (DEPTH, 6 * D), 0.02),
        'g_attn': 1.0 + nrm(ks[6], (DEPTH, D), 0.02),
        'g_ffn': 1.0 + nrm(ks[7], (DEPTH, D), 0.02),
        'w_in': nrm(ks[8], (DEPTH, D, IN_COLS), D ** -0.5),
        'g_q': 1.0 + nrm(ks[9], (DEPTH, MLA_Q_RANK), 0.02),
        'w_uq': nrm(ks[10], (DEPTH, MLA_Q_RANK, MLA_HEADS * (MLA_NOPE + MLA_ROPE)), MLA_Q_RANK ** -0.5),
        'g_kv': 1.0 + nrm(ks[11], (DEPTH, MLA_KV_RANK), 0.02),
        'w_ukv': nrm(ks[12], (DEPTH, MLA_KV_RANK, MLA_HEADS * (MLA_NOPE + MLA_V)), MLA_KV_RANK ** -0.5),
        'na_rpb': nrm(ks[13], (DEPTH, NA_HEADS, 2 * NA_KH - 1, 2 * NA_KW - 1), 0.1),
        'w_fnet': nrm(ks[14], (DEPTH, FN_GROUPS, FN_CH, FN_CH), FN_CH ** -0.5),
        'w_out': nrm(ks[15], (DEPTH, MIX_WIDTH, D), MIX_WIDTH ** -0.5),
        'w_up': nrm(ks[16], (DEPTH, D, 2 * D_FF), D ** -0.5),
        'conv_w': nrm(ks[17], (DEPTH, CONV_W, 2 * D_FF), CONV_W ** -0.5),
        'conv_b': nrm(ks[18], (DEPTH, 2 * D_FF), 0.02),
        'w_down': nrm(ks[19], (DEPTH, D_FF, D), D_FF ** -0.5),
        'g_final': 1.0 + nrm(ks[20], (D,), 0.02),
    }

def first_block(x, c, ctx, c_ctx, w_mod, b_mod, g_attn, g_ffn, w_in, g_q, w_uq, g_kv, w_ukv,
              na_rpb, w_fnet, w_out, w_up, conv_w, conv_b, w_down, g_final):
    S = x.shape[1]
    pos = jnp.arange(S)
    angles = axial_angles(pos // GRID_W, pos % GRID_W)
    xc = ctx
    mod_in = jax.nn.silu(c)
    modc_in = jax.nn.silu(c_ctx)

    for l in range(DEPTH):
        ctx_out = l < DEPTH - 1
        sh1, sc1, gt1, sh2, sc2, gt2 = jnp.split((mod_in @ w_mod[l] + b_mod[l])[:, None, :], 6, axis=-1)
        csh1, csc1, cgt1, csh2, csc2, cgt2 = jnp.split(modc_in @ w_mod[l] + b_mod[l], 6, axis=-1)

        h = rmsnorm(x, g_attn[l]) * (1 + sc1) + sh1
        hc = rmsnorm(xc, g_attn[l]) * (1 + csc1) + csh1
        cq, ckv, kr, qn, kn, vn, f = split_columns(h @ w_in[l])
        cq_c, ckv_c, kr_c, qn_c, kn_c, vn_c, f_c = split_columns(hc @ w_in[l])

        q_m, k_m, v_m = mla_qkv(cq, ckv, kr, g_q[l], w_uq[l], g_kv[l], w_ukv[l], angles)
        q_mc, k_mc, v_mc = mla_qkv(cq_c, ckv_c, kr_c, g_q[l], w_uq[l], g_kv[l], w_ukv[l], None)
        o_mla = blocked_attention(q_m, jnp.concatenate([k_m, k_mc], axis=1),
                                  jnp.concatenate([v_m, v_mc], axis=1), MLA_SCALE)
        kn_c, vn_c = heads(kn_c, NA_HEADS), heads(vn_c, NA_HEADS)
        o_na = neighborhood_attention(heads(qn, NA_HEADS), heads(kn, NA_HEADS), heads(vn, NA_HEADS),
                                      kn_c, vn_c, na_rpb[l])
        o_fn = fourier_mix(f, w_fnet[l])
        x = x + gt1 * (jnp.concatenate([o_mla, o_na, o_fn], axis=-1) @ w_out[l])

        if ctx_out:
            o_mla_c = blocked_attention(q_mc, k_mc, v_mc, MLA_SCALE)
            o_na_c = blocked_attention(heads(qn_c, NA_HEADS), kn_c, vn_c, NA_SCALE)
            o_fn_c = fourier_mix(f_c, w_fnet[l])
            xc = xc + cgt1 * (jnp.concatenate([o_mla_c, o_na_c, o_fn_c], axis=-1) @ w_out[l])

        h2 = rmsnorm(x, g_ffn[l]) * (1 + sc2) + sh2
        x = x + gt2 * conv_ffn(h2, w_up[l], conv_w[l], conv_b[l], w_down[l])
        if ctx_out:
            h2c = rmsnorm(xc, g_ffn[l]) * (1 + csc2) + csh2
            xc = xc + cgt2 * conv_ffn(h2c, w_up[l], conv_w[l], conv_b[l], w_down[l])

    return rmsnorm(x, g_final)


HEAD_DIM = 64
A_Q_HEADS = 16
A_KV_HEADS = 4
A_GROUP = A_Q_HEADS // A_KV_HEADS
WINDOW = 128
B_HEADS = 16
BLOCK = 128
D_FF_2 = ((8 * D_MODEL // 3 + 255) // 256) * 256

A_Q_W = A_Q_HEADS * HEAD_DIM
A_KV_W = A_KV_HEADS * HEAD_DIM
B_W = B_HEADS * HEAD_DIM
IN_SPLITS_2 = (A_Q_W, A_KV_W, A_KV_W, B_W, B_W, B_W, D_MODEL, D_MODEL)
IN_WIDTH = sum(IN_SPLITS_2)
IN_OFFSETS = tuple(int(o) for o in np.cumsum(IN_SPLITS_2)[:-1])


def rmsnorm_2(x, g):
    xf = x.astype(jnp.float32)
    inv = lax.rsqrt(jnp.mean(xf * xf, axis=-1, keepdims=True) + EPS)
    return (xf * inv * g.astype(jnp.float32)).astype(x.dtype)

def alibi_slopes(n_heads):
    h = jnp.arange(1, n_heads + 1, dtype=jnp.float32)
    return jnp.exp2(-8.0 * h / n_heads)

def sliding_window_attention(q, k, v, sinks):
    B, S = q.shape[0], q.shape[1]
    nb = S // BLOCK
    qb = q.reshape(B, nb, BLOCK, A_KV_HEADS, A_GROUP, HEAD_DIM)
    kb = k.reshape(B, nb, BLOCK, A_KV_HEADS, HEAD_DIM)
    vb = v.reshape(B, nb, BLOCK, A_KV_HEADS, HEAD_DIM)
    pad_k = jnp.zeros_like(kb[:, :1])
    pad_v = jnp.zeros_like(vb[:, :1])
    kk = jnp.concatenate([jnp.concatenate([pad_k, kb[:, :-1]], axis=1), kb], axis=2)
    vv = jnp.concatenate([jnp.concatenate([pad_v, vb[:, :-1]], axis=1), vb], axis=2)

    scale = 1.0 / math.sqrt(HEAD_DIM)
    s = jnp.einsum('bnqhgd,bnkhd->bnhgqk', qb, kk).astype(jnp.float32) * scale

    qi = jnp.arange(BLOCK)[:, None]
    ki = jnp.arange(2 * BLOCK)[None, :]
    dist = (BLOCK + qi - ki)
    blk = jnp.arange(nb)[:, None, None]
    valid = (dist >= 0) & (dist < WINDOW)
    valid = valid[None] & ((blk > 0) | (ki[None] >= BLOCK))

    slopes = alibi_slopes(A_Q_HEADS).reshape(A_KV_HEADS, A_GROUP)
    s = s - slopes[:, :, None, None] * dist.astype(jnp.float32)[None, None]
    s = jnp.where(valid[None, :, None, None], s, -jnp.inf)

    sink = sinks.astype(jnp.float32).reshape(A_KV_HEADS, A_GROUP)[None, None, :, :, None, None]
    sink = jnp.broadcast_to(sink, s.shape[:-1] + (1,))
    p = jax.nn.softmax(jnp.concatenate([s, sink], axis=-1), axis=-1)[..., :-1]
    o = jnp.einsum('bnhgqk,bnkhd->bnqhgd', p.astype(v.dtype), vv)
    return o.reshape(B, S, A_Q_W)

def stick_breaking_attention(q, k, v):
    B, S = q.shape[0], q.shape[1]
    nb = S // BLOCK
    scale = 1.0 / math.sqrt(HEAD_DIM)
    qb = q.reshape(B, nb, BLOCK, B_HEADS, HEAD_DIM).transpose(1, 0, 2, 3, 4)
    kpos = jnp.arange(S)

    def one_block(args):
        qblk, i = args
        z = jnp.einsum('bqhd,bkhd->bhqk', qblk, k).astype(jnp.float32) * scale
        tpos = i * BLOCK + jnp.arange(BLOCK)
        causal = kpos[None, :] < tpos[:, None]
        log_beta = jax.nn.log_sigmoid(z)
        log_fail = jnp.where(causal, jax.nn.log_sigmoid(-z), 0.0)
        suffix = lax.cumsum(log_fail, axis=3, reverse=True) - log_fail
        a = jnp.where(causal, jnp.exp(log_beta + suffix), 0.0)
        return jnp.einsum('bhqk,bkhd->bqhd', a.astype(v.dtype), v)

    o = lax.map(one_block, (qb, jnp.arange(nb)))
    return o.transpose(1, 0, 2, 3, 4).reshape(B, S, B_W)

def swiglu(h, w_in, w_down):
    gu = h @ w_in
    gate, up = jnp.split(gu, 2, axis=-1)
    return (jax.nn.silu(gate) * up) @ w_down

def second_inputs(seed: int = 0) -> dict:
    key = jax.random.key(seed)
    ks = jax.random.split(key, 12)
    f32 = jnp.float32

    def w(k, shape, fan_in):
        return jax.random.normal(k, shape, f32) * (fan_in ** -0.5)

    def gain(k, shape):
        return 1.0 + 0.02 * jax.random.normal(k, shape, f32)

    return {
        "x": jax.random.normal(ks[0], (BATCH, SEQ, D_MODEL), f32),
        "norm_mix_g": gain(ks[1], (DEPTH, D_MODEL)),
        "w_in": w(ks[2], (DEPTH, D_MODEL, IN_WIDTH), D_MODEL),
        "sink_logits": 0.5 * jax.random.normal(ks[3], (DEPTH, A_Q_HEADS), f32),
        "w_branch_a": w(ks[4], (DEPTH, A_Q_W, D_MODEL), A_Q_W),
        "w_branch_b": w(ks[5], (DEPTH, B_W, D_MODEL), B_W),
        "w_out": w(ks[6], (DEPTH, D_MODEL, D_MODEL), D_MODEL),
        "norm_ffn_g": gain(ks[7], (DEPTH, D_MODEL)),
        "w_ffn_in": w(ks[8], (DEPTH, D_MODEL, 2 * D_FF_2), D_MODEL),
        "w_ffn_down": w(ks[9], (DEPTH, D_FF_2, D_MODEL), D_FF_2),
        "norm_final_g": gain(ks[10], (D_MODEL,)),
    }

def second_block(x, norm_mix_g, w_in, sink_logits, w_branch_a, w_branch_b, w_out,
              norm_ffn_g, w_ffn_in, w_ffn_down, norm_final_g):
    B, S, _ = x.shape
    for layer in range(DEPTH):
        h = rmsnorm_2(x, norm_mix_g[layer])
        proj = h @ w_in[layer]
        qa, ka, va, qb, kb, vb, ga, gb = jnp.split(proj, IN_OFFSETS, axis=-1)

        ya = sliding_window_attention(
            qa.reshape(B, S, A_Q_HEADS, HEAD_DIM),
            ka.reshape(B, S, A_KV_HEADS, HEAD_DIM),
            va.reshape(B, S, A_KV_HEADS, HEAD_DIM),
            sink_logits[layer]) @ w_branch_a[layer]
        yb = stick_breaking_attention(
            qb.reshape(B, S, B_HEADS, HEAD_DIM),
            kb.reshape(B, S, B_HEADS, HEAD_DIM),
            vb.reshape(B, S, B_HEADS, HEAD_DIM)) @ w_branch_b[layer]

        merged = jax.nn.sigmoid(ga) * ya + jax.nn.sigmoid(gb) * yb
        x = x + merged @ w_out[layer]
        x = x + swiglu(rmsnorm_2(x, norm_ffn_g[layer]), w_ffn_in[layer], w_ffn_down[layer])
    return rmsnorm_2(x, norm_final_g)


def setup_inputs(seed=0):
    out = dict(first_inputs(seed))
    for name, value in second_inputs(seed + 1).items():
        if name != "x":
            out[name + "_2"] = value
    return out


def reference(
    x, c, ctx, c_ctx, w_mod, b_mod, g_attn, g_ffn, w_in, g_q, w_uq, g_kv, w_ukv, na_rpb, w_fnet,
    w_out, w_up, conv_w, conv_b, w_down, g_final, norm_mix_g_2, w_in_2, sink_logits_2,
    w_branch_a_2, w_branch_b_2, w_out_2, norm_ffn_g_2, w_ffn_in_2, w_ffn_down_2, norm_final_g_2,
):
    x = first_block(
        x, c, ctx, c_ctx, w_mod, b_mod, g_attn, g_ffn, w_in, g_q, w_uq, g_kv, w_ukv, na_rpb,
        w_fnet, w_out, w_up, conv_w, conv_b, w_down, g_final,
    )
    return second_block(
        x, norm_mix_g_2, w_in_2, sink_logits_2, w_branch_a_2, w_branch_b_2, w_out_2,
        norm_ffn_g_2, w_ffn_in_2, w_ffn_down_2, norm_final_g_2,
    )


_drawn_inputs = setup_inputs


def setup_inputs(seed=0):
    import zlib

    import numpy as np

    out = dict(_drawn_inputs(seed))
    spreads = {}
    factors = {'g_attn': 7.577,
     'g_ffn': 3.292,
     'g_q': 8.0,
     'g_kv': 8.0,
     'na_rpb': 8.0,
     'conv_b': 4.058,
     'norm_mix_g_2': 5.144,
     'sink_logits_2': 17.777,
     'norm_ffn_g_2': 4.065,
     'norm_final_g_2': 7.653}
    for name, (base, spread) in spreads.items():
        noise = np.random.default_rng([zlib.crc32(name.encode()), seed]).standard_normal(out[name].shape)
        drawn = base * np.exp(spread * noise) if base else spread * noise
        out[name] = __import__('jax').numpy.asarray(drawn.astype(out[name].dtype))
    for name, factor in factors.items():
        out[name] = (out[name] * factor).astype(out[name].dtype)
    return out
```

```python
from contextlib import ExitStack

import numpy as np

import concourse.bass as bass
from concourse import mybir

F32 = mybir.dt.float32
F32R = mybir.dt.float32r
ALU = mybir.AluOpType
ACT = mybir.ActivationFunctionType
AX_X = mybir.AxisListType.X

P = 128
D = 2048
T = 256
KT = D // P
FF = 5632
FT = FF // P
R = 4
LEAD = R
CH = 1024
GW = 512
CPG = KT // 2
EPS = 1e-6
BIG = 1e30

MLA_H, NOPE, ROPE, VD, RANK = 8, 128, 64, 128, 512
RT = RANK // P
MLA_SCALE = (NOPE + ROPE) ** -0.5
NA_H, NA_ROWS, GRID_W, NA_KH, NA_KW = 4, 4, 64, 8, 16
NA_SCALE = 128 ** -0.5
FN_G = 4
HEADS = MLA_H + NA_H

A_H, A_KV, B_H, HD = 16, 4, 16, 64
PAIRS = A_H // 2
SLOPES = [2.0 ** (-8.0 * (h + 1) / A_H) for h in range(A_H)]

VEC = {}


def _vec(name, n):
    VEC[name] = (VEC["_n"] if "_n" in VEC else 0, n)
    VEC["_n"] = VEC[name][0] + n


for _name, _n in (("c", KT), ("c_ctx", KT), ("b_mod", 6 * KT), ("g_attn", KT), ("g_ffn", KT),
                  ("g_q", RT), ("g_kv", RT), ("conv_w", 3 * 2 * FT), ("conv_b", 2 * FT),
                  ("g_final", KT), ("g_mix2", KT), ("g_ffn2", KT), ("g_final2", KT),
                  ("sink", 2 * A_H), ("eps", 1)):
    _vec(_name, _n)
NV = VEC["_n"]

STAGES = [("cq", 1, CPG), ("ckv", 1, CPG), ("kr", 1, 2), ("qn", 1, CPG), ("kn", 1, CPG),
          ("vn", 1, CPG), ("f", 1, CPG), ("uq", 4, 2), ("ukv", 4, 2), ("out", 4, CPG),
          ("up", 22, CPG), ("down", 4, FT // 2),
          ("qa", 2, CPG), ("kva", 1, CPG), ("qkb", 4, CPG), ("vb", 2, CPG), ("gates", 8, CPG),
          ("bra", 4, 4), ("brb", 4, 4), ("out2", 4, CPG), ("up2", 22, CPG), ("down2", 4, FT // 2)]
BASE = {}
N_CHUNKS = 0
for _s, _g, _n in STAGES:
    BASE[_s] = N_CHUNKS
    N_CHUNKS += _g * _n
MOD_G = 6 * D // GW
MOD_CHUNKS = MOD_G * CPG
assert MOD_CHUNKS % R == 0

SUMS = {}
N_SUMS = 0
for _s, _n in (("cq", 4), ("ckv", 8), ("kr", 2), ("qn", 4), ("kn", 8), ("uq", 12), ("ukv", 16),
               ("out", 16), ("up", 88), ("down", 16), ("qa", 8), ("kva", 2), ("qkb", 16),
               ("gates", 32), ("bra", 16), ("brb", 16), ("out2", 16), ("up2", 88), ("down2", 16)):
    SUMS[_s] = N_SUMS
    N_SUMS += _n
ROWS = {}
N_ROWS = 0
for _s, _n in (("vn", 4), ("f", 2), ("ukv", 16), ("kva", 2), ("vb", 4)):
    ROWS[_s] = N_ROWS
    N_ROWS += _n

NORM = {}
_t = 0
for _i, (_s, _n) in enumerate((("x", KT), ("ctx", KT), ("cq", RT), ("ckv", RT), ("ckvc", RT),
                               ("ffn", KT), ("fin", KT), ("mix2", KT), ("ffn2", KT), ("fin2", KT))):
    NORM[_s] = (_t, _t // 2, _i, _n)
    _t += _n


def plus(base, it, per):
    return base if it is None else it * per + base


def host_tables():
    f = np.float32
    n = ROPE // 4
    freqs = (f(10000.0) ** (-np.arange(n, dtype=f) / f(n))).astype(f)
    pos = np.arange(T)
    ang = np.zeros((ROPE, T), f)
    rot = np.zeros((ROPE, ROPE), f)
    for half, where in enumerate((pos // GRID_W, pos % GRID_W)):
        for i in range(n):
            a, b = half * 2 * n + i, half * 2 * n + n + i
            ang[a] = ang[b] = where.astype(f) * freqs[i]
            rot[b, a] = -1.0
            rot[a, b] = 1.0
    rope = np.zeros((P, 2 * T + P), f)
    for s in range(2):
        rope[s * ROPE:(s + 1) * ROPE, 0:T] = np.cos(ang)
        rope[s * ROPE:(s + 1) * ROPE, T:2 * T] = np.sin(ang)
        rope[s * ROPE:(s + 1) * ROPE, 2 * T + s * ROPE:2 * T + (s + 1) * ROPE] = rot
    base = np.concatenate([np.eye(P, dtype=f), np.ones((P, P), f)], axis=1)
    l = np.arange(T)
    angl = 2 * np.pi * ((l[:, None] * l[None, :]) % T) / T
    cl = np.concatenate([np.cos(angl), np.sin(angl)], axis=1)
    c = np.arange(P)
    angc = 2 * np.pi * ((c[:, None] * c[None, :]) % P) / P
    ortho = 1.0 / np.sqrt(T * P)
    dft = np.concatenate([cl[:P], cl[P:], np.cos(angc) * ortho, -np.sin(angc) * ortho], axis=1).astype(f)
    w = np.arange(P) % GRID_W
    start = np.clip(w - NA_KW // 2, 0, GRID_W - NA_KW)[:, None]
    col = np.arange(GRID_W)[None, :]
    na_mask = np.where((col >= start) & (col < start + NA_KW), 0.0, -BIG).astype(f)
    k, q = np.arange(P)[:, None], np.arange(P)[None, :]
    strict = np.where(k < q, 0.0, -BIG).astype(f)
    tri = (k >= q).astype(f)
    stick = np.concatenate([strict, np.zeros((P, P), f), strict, tri], axis=1)
    qi, ki = np.arange(P)[:, None], np.arange(2 * P)[None, :]
    dist = P + qi - ki
    dist = np.where((dist >= 0) & (dist < P), dist, BIG).astype(f)
    return dict(base_tab=base, rope_tab=rope, dft_tab=dft, na_mask=na_mask, stick_tab=stick, dist_tab=dist)


def two_blocks(nc, xT, ctxT, vecs_d, w_mod, w_in, w_uq, w_ukv, rpb, w_fnet, w_out, w_up, w_down,
               w_in2, w_bra, w_brb, w_out2, w_up2, w_down2,
               base_tab, rope_tab, dft_tab, na_mask, stick_tab, dist_tab, outT):
    ctx = ExitStack()
    with ctx:
        def sem(name):
            return ctx.enter_context(nc.semaphore(name))

        top = [-(-nc.sbuf_base // 32) * 32]

        def place(name, shape, dt=F32, at=None):
            size = 4 * int(np.prod(shape[1:]))
            if at is None:
                at = top[0]
                top[0] += -(-size // 32) * 32
            assert at + size <= nc.sbuf_usable_end, (name, at + size - nc.sbuf_usable_end)
            return nc.alloc_sbuf_tensor_at(name, shape, dt, offset=at), at

        raw, _ = place("raw", [P, R, CH])
        hi, _ = place("hi", [P, R, CH], F32R)
        lo, _ = place("lo", [P, R, CH], F32R)
        x, _ = place("x", [P, KT, T])
        pair, _ = place("pair", [P, KT, 2, T], F32R)
        tmp, tmp_at = place("tmp", [P, 4, T])
        base, _ = place("base", [P, 2 * P])
        ident, ones = base[:, 0:P], base[:, P:2 * P]
        vecs, _ = place("vecs", [P, NV])
        mod, _ = place("mod", [P, 2, 6 * KT])
        csil, _ = place("csil", [P, KT, 2])
        gain, _ = place("gain", [P, 3, KT])
        std, _ = place("std", [P, T])
        rinv, _ = place("rinv", [P, 2, T])
        small, _ = place("small", [P, 8 * 24])
        rope, rope_at = place("rope", [P, 2 * T + P])
        cos, sin, rot = rope[:, 0:T], rope[:, T:2 * T], rope[:, 2 * T:2 * T + P]
        reg = top[0]
        K1 = 1024
        ctxpair, _ = place("ctxpair", [P, KT, 2, T], F32R, reg)
        cq, _ = place("cq", [P, RT, T], at=reg + 32 * K1)
        ckv, _ = place("ckv", [P, RT, 2, T], at=reg + 36 * K1)
        cqn, _ = place("cqn", [P, RT, 2, T], F32R, reg + 44 * K1)
        ckvn, _ = place("ckvn", [P, 2, RT, 2, T], F32R, reg + 52 * K1)
        kre, _ = place("kre", [P, 2, T], at=reg + 68 * K1)
        kro, _ = place("kro", [P, 2, T], at=reg + 70 * K1)
        qn, _ = place("qn", [P, NA_H, T], at=reg + 72 * K1)
        kn, _ = place("kn", [P, NA_H, 2, T], at=reg + 76 * K1)
        vn, _ = place("vn", [P, 4, GW], at=reg + 84 * K1)
        f_sb, _ = place("f_sb", [P, 2, GW], at=reg + 92 * K1)
        ctx_x, _ = place("ctx_x", [P, KT, T], at=reg + 76 * K1)
        dft, _ = place("dft", [P, 4 * T + 2 * P], at=reg)
        wfn, _ = place("wfn", [P, FN_G, P], at=reg + 5 * K1)
        uv, _ = place("uv", [P, FN_G, 2 * T], at=reg + 7 * K1)
        spec, _ = place("spec", [P, FN_G, T], at=reg + 15 * K1)
        knope, _ = place("knope", [P, MLA_H, 2, T], at=reg)
        v_sb, _ = place("v_sb", [P, 4, MLA_H * VD], at=reg + 16 * K1)
        qnope, _ = place("qnope", [P, MLA_H, T], at=reg + 32 * K1)
        qrope, _ = place("qrope", [P, MLA_H // 2, T], at=reg + 40 * K1)
        prob, _ = place("prob", [P, 2, 2, 2 * T], at=reg + 44 * K1)
        probT, _ = place("probT", [P, 2, 4, T], at=reg + 52 * K1)
        bias, _ = place("bias", [P, NA_H, 2, T], at=reg + 60 * K1)
        hid, _ = place("hid", [P, FT, 2, T], F32R, reg)
        gate, _ = place("gate", [P, 4, T], at=reg + 88 * K1)
        val, _ = place("val", [P, 4, T], at=reg + 92 * K1)
        qa, _ = place("qa", [P, PAIRS, T], at=reg)
        ka, _ = place("ka", [P, 2, T], at=reg + 8 * K1)
        va, _ = place("va", [P, 2, A_KV * HD], at=reg + 10 * K1)
        qkb, _ = place("qkb", [P, 2 * PAIRS, T], at=reg + 12 * K1)
        vb, _ = place("vb", [P, 2, B_H * HD], at=reg + 28 * K1)
        gates, _ = place("gates", [P, 2 * KT, T], at=reg + 36 * K1)
        W3 = 3 * P
        sa, _ = place("sa", [P, 2, 2, W3], at=reg + 68 * K1)
        saT, _ = place("saT", [P, 2, 2, W3], at=reg + 74 * K1)
        sp_, _ = place("sp_", [P, 2, 2, W3], at=reg + 80 * K1)
        zb, _ = place("zb", [P, 3, 2, W3], at=reg + 86 * K1)
        lnb, _ = place("lnb", [P, 2, W3], at=tmp_at)
        dist, _ = place("dist", [P, 2 * P], at=tmp_at + 3 * K1)
        stick, _ = place("stick", [P, 4 * P], at=rope_at)
        pair2, _ = place("pair2", [P, KT, 2, T], F32R, reg)

        ps = ctx.enter_context(nc.psum_tensor("ps", [P, 8, 512], F32))

        def vec(name, i=0, n=1, it=None, per=0):
            o = VEC[name][0] + i
            if it is None:
                return vecs[:, o:o + n]
            return vecs[:, bass.ds(it * per + o, n)]

        landed = [sem(f"landed{i}") for i in range(R)]
        s_x, s_ctx, s_vecs, s_tabs = sem("x_landed"), sem("ctx_landed"), sem("vecs_landed"), sem("tabs_landed")
        s_dft, s_bias, s_stick, s_dist = sem("dft_landed"), sem("bias_landed"), sem("stick_landed"), sem("dist_landed")
        mod_used, hi_ready, lo_ready, weights_used = sem("mod_used"), sem("hi_ready"), sem("lo_ready"), sem("weights_used")
        sums_ready, rows_copied = sem("sums_ready"), sem("rows_copied")
        silu_c, mod_ready, gain_ready = sem("silu_c"), sem("mod_ready"), sem("gain_ready")
        sq_ready, sq_used, std_ready, rinv_ready = sem("sq_ready"), sem("sq_used"), sem("std_ready"), sem("rinv_ready")
        scaled, norm_hi, norm_lo = sem("scaled"), sem("norm_hi"), sem("norm_lo")
        zeroed = sem("zeroed")
        turned, rope_mul, roped = sem("turned"), sem("rope_mul"), sem("roped")
        uv_done, uv_copied, spec_done, spec_copied, fn_done = (sem("uv_done"), sem("uv_copied"), sem("spec_done"),
                                                              sem("spec_copied"), sem("fn_done"))
        o_hi, o_lo = sem("o_hi"), sem("o_lo")
        scores, biased, maxed, negmax = sem("scores"), sem("biased"), sem("maxed"), sem("negmax")
        exps, recips, probs = sem("exps"), sem("recips"), sem("probs")
        flipped, flips_copied, mixed = sem("flipped"), sem("flips_copied"), sem("mixed")
        bias_masked = sem("bias_masked")
        resid = sem("resid")
        centre, sides, silu_done, prod = sem("centre"), sem("sides"), sem("silu_done"), sem("prod")
        hid_hi, hid_lo = sem("hid_hi"), sem("hid_lo")
        tmp_read, qb_scaled, gated, merged = (sem("tmp_read"), sem("qb_scaled"),
                                                         sem("gated"), sem("merged"))
        m_hi, m_lo = sem("m_hi"), sem("m_lo")
        sw_scores, sw_biased, sw_max, sw_neg = sem("sw_scores"), sem("sw_biased"), sem("sw_max"), sem("sw_neg")
        sw_exps, sw_sum, sw_probs, sw_flip, sw_flipc = (sem("sw_exps"), sem("sw_sum"), sem("sw_probs"),
                                                       sem("sw_flip"), sem("sw_flipc"))
        sb_z, sb_zb, sb_ln, sb_sp, sb_suffix, sb_d, sb_a = (sem("sb_z"), sem("sb_zb"), sem("sb_ln"), sem("sb_sp"),
                                                           sem("sb_suffix"), sem("sb_d"), sem("sb_a"))
        sb_step = sem("sb_step")
        mixed2, o2_hi, o2_lo = sem("mixed2"), sem("o2_hi"), sem("o2_lo")
        stored = sem("stored")

        block = ctx.enter_context(nc.Block())

        def load(e, c, dst, src, it=None, per=0):
            prev = c - R
            if prev >= MOD_CHUNKS:
                e.wait_ge(lo_ready, plus(prev - MOD_CHUNKS + 1, it, per))
            elif prev >= 0:
                e.wait_ge(mod_used, plus(prev + 1, it, per))
            e.dma_start(dst, src).then_inc(landed[c % R], 16)

        def raw_view(c, k, n):
            return raw[:, c % R, 0:k * n].rearrange("p (k n) -> p k n", k=k)

        def split_view(part, c, k, n):
            return part[:, c % R, 0:k * n].rearrange("p (k n) -> p k n", k=k)

        def pieces(c, *parts):
            r = raw[:, c % R, :]
            ds = [p[:, c % R, :] for p in parts]
            if BASE["kr"] <= c < BASE["kr"] + 2:
                src = r[:, 0:CH // 2].rearrange("p (k n) -> p k n", n=ROPE)
                ds = [d.rearrange("p (k j n) -> p k j n", j=2, n=ROPE) for d in ds]
                return [[d[:, :, j] for d in ds] + [src] for j in range(2)]
            if BASE["uq"] <= c < BASE["ukv"]:
                n = 2 * 2 * (NOPE + ROPE)
                src = r[:, 0:n].rearrange("p (k m n) -> p k m n", k=2, m=2)
                ds = [d[:, 0:n].rearrange("p (k n) -> p k n", k=2) for d in ds]
                plain = [d[:, :, 0:2 * NOPE].rearrange("p k (m n) -> p k m n", m=2) for d in ds]
                rotary = [d[:, :, 2 * NOPE:].rearrange("p k (m n) -> p k m n", m=2) for d in ds]
                return [plain + [src[:, :, :, 0:NOPE]], rotary + [src[:, :, :, NOPE:]]]
            if BASE["qa"] <= c < BASE["kva"]:
                return [[d[:, k * GW:(k + 1) * GW].rearrange("p (i a d) -> p i a d", i=4, a=2) for d in ds]
                        + [r[:, k * GW:(k + 1) * GW].rearrange("p (a i d) -> p i a d", i=4, a=2)] for k in range(2)]
            return [ds + [r]]

        def split_hi(e, a, b, it=None, per=0):
            for c in range(a, min(b, N_CHUNKS)):
                e.wait_ge(landed[c % R], plus(16 * ((c + MOD_CHUNKS) // R + 1), it, 16 * per // R))
                if c >= R:
                    e.wait_ge(weights_used, plus(c - R + 1, it, per))
                for h, r in pieces(c, hi):
                    m = e.activation(h, r, ACT.Copy)
                m.then_inc(hi_ready, 1)

        def split_lo(e, a, b, it=None, per=0):
            for c in range(a, min(b, N_CHUNKS)):
                e.wait_ge(hi_ready, plus(c + 1, it, per))
                for l, h, r in pieces(c, lo, hi):
                    m = e.tensor_tensor(l, r, h.bitcast(F32), ALU.subtract)
                m.then_inc(lo_ready, 1)

        def group(e, c0, n_chunks, kpc, w, jobs, it=None, per=0, need=None):
            for ch in range(n_chunks):
                c = c0 + ch
                e.wait_ge(lo_ready, plus(c + 1, it, per))
                for k in range(kpc):
                    kt = ch * kpc + k
                    if need is not None:
                        need(kt)
                    last = jobs(kt, split_view(hi, c, kpc, w)[:, k], split_view(lo, c, kpc, w)[:, k],
                                kt == 0, kt == n_chunks * kpc - 1)
                last.then_inc(weights_used, 1)

        def features(e, bank, whi, wlo, act, first, last):
            out = ps[:, bank, :]
            both = act.rearrange("p s t -> p (s t)")
            if first:
                e.matmul(out, whi, both, start=True, stop=False)
                return e.matmul(out[:, T:2 * T], wlo, act[:, 0, :], start=False, stop=False)
            m = e.matmul(out[:, T:2 * T], wlo, act[:, 0, :], start=False, stop=False)
            return e.matmul(out, whi, both, start=False, stop=last)

        def tokens(e, out, whi, wlo, act, tt, first, last):
            ahi, alo = act[:, 0, tt * P:(tt + 1) * P], act[:, 1, tt * P:(tt + 1) * P]
            e.matmul(out, alo, whi, start=first, stop=False)
            e.matmul(out, ahi, wlo, start=False, stop=False)
            return e.matmul(out, ahi, whi, start=False, stop=last)

        @block.sync
        def _(e):
            e.dma_start(vecs[:], vecs_d).then_inc(s_vecs, 16)
            wm = w_mod.rearrange("(t p) n -> p t n", p=P)
            for ch in range(CPG):
                load(e, ch, raw_view(ch, 2, GW), wm[:, 2 * ch:2 * ch + 2, 0:GW])
                if ch == 1:
                    e.dma_start(x[:], xT.rearrange("(t p) n -> p t n", p=P)).then_inc(s_x, 16)
                if ch == 3:
                    e.dma_start(ctx_x[:], ctxT.rearrange("(t p) n -> p t n", p=P)).then_inc(s_ctx, 16)
            with e.Fori(1, MOD_G) as g:
                for ch in range(CPG):
                    e.wait_ge(mod_used, g * CPG + (ch - R + 1))
                    e.dma_start(raw_view(ch, 2, GW), wm[:, 2 * ch:2 * ch + 2, bass.ds(g * GW, GW)])\
                        .then_inc(landed[ch % R], 16)

            def stream(w, stage, col, g=0, it=None, per=0, col_per=0, kts=2, n=GW, chunks=CPG):
                wv = w.rearrange("(t p) n -> p t n", p=P)
                for ch in range(chunks):
                    c = MOD_CHUNKS + BASE[stage] + g * chunks + ch
                    cols = slice(col, col + n) if it is None else bass.ds(it * col_per + col, n)
                    load(e, c, raw_view(c, kts, n), wv[:, kts * ch:kts * (ch + 1), cols], it, per)

            for stage, col in (("cq", 0), ("ckv", 512), ("kr", 1024), ("qn", 1088), ("kn", 1600), ("vn", 2112),
                               ("f", 2624)):
                if stage == "kr":
                    stream(w_in, stage, col, kts=8, n=ROPE, chunks=2)
                else:
                    stream(w_in, stage, col)
            for g in range(4):
                stream(w_uq, "uq", g * 384, g, n=384, chunks=2)
            for g in range(4):
                stream(w_ukv, "ukv", g * GW, g, chunks=2)
            for g in range(4):
                stream(w_out, "out", g * GW, g)

            def ffn_stream(up, down, s_up, s_down):
                with e.Fori(0, 11) as j:
                    stream(up, s_up, 0, 0, j, 2 * CPG, GW)
                    stream(up, s_up, FF, 1, j, 2 * CPG, GW)
                with e.Fori(0, 2) as j:
                    for g in range(2):
                        stream(down, s_down, g * GW, g, j, FT, 2 * GW, chunks=FT // 2)

            ffn_stream(w_up, w_down, "up", "down")
            for g in range(2):
                stream(w_in2, "qa", g * GW, g)
            stream(w_in2, "kva", 1024)
            with e.Fori(0, 2) as j:
                for g in range(2):
                    stream(w_in2, "qkb", 1536 + g * GW, g, j, 2 * CPG, 2 * GW)
            for g in range(2):
                stream(w_in2, "vb", 3584 + g * GW, g)
            with e.Fori(0, 4) as j:
                for g in range(2):
                    stream(w_in2, "gates", 4608 + g * GW, g, j, 2 * CPG, 2 * GW)
            for g in range(4):
                stream(w_bra, "bra", g * GW, g, chunks=4)
            for g in range(4):
                stream(w_brb, "brb", g * GW, g, chunks=4)
            with e.Fori(0, 2) as j:
                for g in range(2):
                    stream(w_out2, "out2", g * GW, g, j, 2 * CPG, 2 * GW)
            ffn_stream(w_up2, w_down2, "up2", "down2")

            ov = outT.rearrange("(t p) n -> p t n", p=P)
            for i in range(4):
                e.wait_ge(scaled, NORM["fin2"][0] + 4 * (i + 1))
                e.dma_start(ov[:, 4 * i:4 * i + 4, :], x[:, 4 * i:4 * i + 4, :]).then_inc(stored, 16)
            e.wait_ge(stored, 64)

        @block.gpsimd
        def _(e):
            e.dma_start(base[:], base_tab).then_inc(s_tabs, 16)
            e.dma_start(rope[:], rope_tab).then_inc(s_tabs, 16)
            e.memset(kre[64:P, :, :], 0.0).then_inc(zeroed, 1)
            e.memset(kro[0:64, :, :], 0.0).then_inc(zeroed, 1)
            e.wait_ge(weights_used, BASE["f"])
            e.dma_start(dft[:], dft_tab).then_inc(s_dft, 16)
            e.dma_start(wfn[:], w_fnet.rearrange("g c d -> c g d")).then_inc(s_dft, 16)
            e.wait_ge(weights_used, BASE["out"])
            e.dma_start(tmp[:, 3, 0:GRID_W], na_mask).then_inc(s_dft, 16)
            for r in range(NA_ROWS):
                a0 = NA_KH - 1 - r
                src = rpb[:, :, a0:a0 + NA_ROWS, :].rearrange("w h a c -> w h (a c)")
                e.dma_start(bias[(r % 2) * GRID_W:(r % 2 + 1) * GRID_W, :, r // 2, :], src).then_inc(s_bias, 16)
            e.wait_ge(weights_used, BASE["gates"])
            e.dma_start(stick[:], stick_tab).then_inc(s_stick, 16)

        def squares(e, name, src, bank_free=None):
            t0, s0, idx, n = NORM[name]
            if name not in ("x", "ctx"):
                e.wait_ge(norm_lo, sum(NORM[q][3] for q in PAIRED if NORM[q][2] < idx))
            for s in range(n // 2):
                if s0 + s >= 2:
                    e.wait_ge(sq_used, s0 + s - 1)
                e.activation(tmp[:, 2 * ((s0 + s) % 2):2 * ((s0 + s) % 2) + 2, :], src(2 * s), ACT.Square)\
                    .then_inc(sq_ready, 1)
            e.wait_ge(sq_used, s0 + n // 2)
            if idx >= 1:
                e.wait_ge(rinv_ready, idx)
            e.activation(std[:], ps[:, STAT[name], 0:T], ACT.Sqrt, bias=vec("eps"), scale=1.0 / (n * P))\
                .then_inc(std_ready, 1)

        STAT = {"x": 2, "ctx": 3, "cq": 0, "ckv": 5, "ckvc": 6, "ffn": 0, "fin": 0, "mix2": 1, "ffn2": 0, "fin2": 0}

        def stats(e, name):
            t0, s0, idx, n = NORM[name]
            for s in range(n // 2):
                e.wait_ge(sq_ready, s0 + s + 1)
                for k in range(2):
                    last = e.matmul(ps[:, STAT[name], 0:T], ones, tmp[:, 2 * ((s0 + s) % 2) + k, :],
                                    start=(s == 0 and k == 0), stop=(s == n // 2 - 1 and k == 1))
                last.then_inc(sq_used, 1)

        def inv_rms(e, name, slot=0):
            idx = NORM[name][2]
            e.wait_ge(std_ready, idx + 1)
            e.reciprocal(rinv[:, slot, :], std[:]).then_inc(rinv_ready, 1)
            e.wait_ge(rinv_ready, idx + 1)

        def norm_scale(e, name, t, src, g, slot=0, out=None):
            n = NORM[name][0] + t
            if out is None:
                out = tmp[:, t % 4, :]
            e.scalar_tensor_tensor(out=out, in0=src, scalar=g, in1=rinv[:, slot, :], op0=ALU.mult, op1=ALU.mult)\
                .then_inc(scaled, 1)

        PAIRED = {}
        _n = 0
        for _s in ("x", "ctx", "cq", "ckv", "ckvc", "ffn", "mix2", "ffn2"):
            PAIRED[_s] = _n
            _n += NORM[_s][3]

        def norm_hi_part(e, name, dst, shift=None):
            for t in range(NORM[name][3]):
                e.wait_ge(scaled, NORM[name][0] + t + 1)
                b = 0.0 if shift is None else shift(t)
                e.activation(dst(t)[:, 0, :], tmp[:, t % 4, :], ACT.Copy if shift is None else ACT.Identity, bias=b)\
                    .then_inc(norm_hi, 1)

        def norm_lo_part(e, name, t, dst, shift=None):
            e.wait_ge(norm_hi, PAIRED[name] + t + 1)
            h = dst(t)[:, 0, :].bitcast(F32)
            if shift is None:
                e.tensor_tensor(dst(t)[:, 1, :], tmp[:, t % 4, :], h, ALU.subtract).then_inc(norm_lo, 1)
            else:
                e.scalar_tensor_tensor(out=dst(t)[:, 1, :], in0=tmp[:, t % 4, :], scalar=shift(t), in1=h,
                                       op0=ALU.add, op1=ALU.subtract).then_inc(norm_lo, 1)

        def norm_apply(e, name, src, g, dst, shift=None, slot=0, after=None):
            n = NORM[name][3]
            for t in range(n + 2):
                if t < n:
                    if t >= 4:
                        e.wait_ge(norm_lo, PAIRED[name] + t - 3)
                    norm_scale(e, name, t, src(t), g(t), slot)
                if t >= 2:
                    norm_lo_part(e, name, t - 2, dst, shift)
                if after is not None:
                    after(t)

        SH1, SC1, GT1, SH2, SC2, GT2 = (KT * i for i in range(6))

        def modv(which, off, t, n=1):
            return mod[:, which, off + t:off + t + n]

        SRC = {
            "x": (lambda t: x[:, t, :], lambda t: gain[:, 0, t:t + 1], lambda t: pair[:, t], lambda t: modv(0, SH1, t)),
            "ctx": (lambda t: ctx_x[:, t, :], lambda t: gain[:, 1, t:t + 1], lambda t: ctxpair[:, t],
                    lambda t: modv(1, SH1, t)),
            "cq": (lambda t: cq[:, t, :], lambda t: vec("g_q", t), lambda t: cqn[:, t], None),
            "ckv": (lambda t: ckv[:, t, 0, :], lambda t: vec("g_kv", t), lambda t: ckvn[:, 0, t], None),
            "ckvc": (lambda t: ckv[:, t, 1, :], lambda t: vec("g_kv", t), lambda t: ckvn[:, 1, t], None),
            "ffn": (lambda t: x[:, t, :], lambda t: gain[:, 2, t:t + 1], lambda t: pair[:, t], lambda t: modv(0, SH2, t)),
            "mix2": (lambda t: x[:, t, :], lambda t: vec("g_mix2", t), lambda t: pair[:, t], None),
            "ffn2": (lambda t: x[:, t, :], lambda t: vec("g_ffn2", t), lambda t: pair[:, t], None),
        }

        def sq_src(v):
            return lambda t: v[:, t:t + 2, :]

        RES = {"out": 0, "down": 16, "out2": 32, "down2": 48}

        @block.scalar
        def _(e):
            e.wait_ge(s_vecs, 16)
            for v, name in enumerate(("c", "c_ctx")):
                e.activation(csil[:, :, v], vec(name, 0, KT), ACT.Silu).then_inc(silu_c, 1)
            e.wait_ge(s_x, 16)
            squares(e, "x", sq_src(x))
            e.wait_ge(s_ctx, 16)
            squares(e, "ctx", sq_src(ctx_x))
            norm_hi_part(e, "x", SRC["x"][2], SRC["x"][3])
            split_hi(e, 0, LEAD)
            e_ctx = NORM["ctx"][0]
            for i in range(CPG):
                split_hi(e, LEAD + i, LEAD + i + 1)
                for t in (2 * i, 2 * i + 1):
                    e.wait_ge(scaled, e_ctx + t + 1)
                    e.activation(ctxpair[:, t, 0, :], tmp[:, t % 4, :], ACT.Identity, bias=modv(1, SH1, t))\
                        .then_inc(norm_hi, 1)

            def upto(a, stage, n):
                b = BASE[stage] + n + LEAD
                split_hi(e, a, b)
                return b

            at = LEAD + CPG
            at = upto(at, "ckv", CPG)
            e.wait_ge(sums_ready, SUMS["cq"] + 4)
            squares(e, "cq", sq_src(cq))
            norm_hi_part(e, "cq", SRC["cq"][2])
            at = upto(at, "kr", 2)
            at = upto(at, "qn", CPG)
            e.wait_ge(sums_ready, SUMS["ckv"] + 8)
            squares(e, "ckv", lambda t: ckv[:, t:t + 2, 0, :])
            norm_hi_part(e, "ckv", SRC["ckv"][2])
            squares(e, "ckvc", lambda t: ckv[:, t:t + 2, 1, :])
            norm_hi_part(e, "ckvc", SRC["ckvc"][2])
            at = upto(at, "kn", CPG)
            at = upto(at, "vn", CPG)
            e.wait_ge(weights_used, BASE["vn"] + CPG)
            for tt in range(4):
                e.activation(vn[:, tt, :], ps[:, 4 + tt, :], ACT.Copy).then_inc(rows_copied, 1)
            at = upto(at, "f", CPG)
            e.wait_ge(weights_used, BASE["f"] + CPG)
            for tt in range(2):
                e.activation(f_sb[:, tt, :], ps[:, tt, :], ACT.Copy).then_inc(rows_copied, 1)
            at = upto(at, "uq", 8)
            for g in range(FN_G):
                e.wait_ge(uv_done, g + 1)
                e.activation(uv[:, g, :], ps[:, 4 + g, :], ACT.Copy).then_inc(uv_copied, 1)
            for g in range(FN_G):
                e.wait_ge(fn_done, g + 1)
                e.activation(pair[:, HEADS + g, 0, :], ps[:, 4 + g, 0:T], ACT.Copy).then_inc(o_hi, 1)
            for g in range(4):
                at = upto(at, "ukv", 2 * (g + 1))
                e.wait_ge(weights_used, BASE["ukv"] + 2 * (g + 1))
                for tt in range(4):
                    e.activation(v_sb[:, tt, g * 2 * VD:(g + 1) * 2 * VD], ps[:, 4 + tt, 0:2 * VD], ACT.Copy)\
                        .then_inc(rows_copied, 1)
            for i in range(HEADS + 2):
                if 1 <= i <= HEADS:
                    h = i - 1
                    for t in range(2):
                        e.wait_ge(flipped, 2 * h + t + 1)
                        if h >= 2:
                            e.wait_ge(mixed, h - 1)
                        e.activation(probT[:, h % 2, :, t * P:(t + 1) * P],
                                     ps[:, 4 + t, :].rearrange("p (k q) -> p k q", k=4), ACT.Copy)\
                            .then_inc(flips_copied, 1)
                if i < HEADS:
                    for t in range(2):
                        n = 2 * i + t
                        e.wait_ge(negmax, n + 1)
                        if i >= 2:
                            e.wait_ge(flipped, n - 3)
                        src = ps[:, 2 * (i % 2) + t, :] if i < MLA_H else prob[:, i % 2, t, :]
                        e.activation(prob[:, i % 2, t, :], src, ACT.Exp, bias=small[:, 24 + n:25 + n],
                                     scale=MLA_SCALE if i < MLA_H else 1.0,
                                     accum_out=small[:, 48 + n:49 + n]).then_inc(exps, 1)
                if i >= 2:
                    h = i - 2
                    e.wait_ge(mixed, h + 1)
                    e.activation(pair[:, h, 0, :], ps[:, 6 + h % 2, 0:T], ACT.Copy).then_inc(o_hi, 1)
            for g in range(4):
                at = upto(at, "out", (g + 1) * CPG)
            e.wait_ge(resid, RES["out"] + 16)
            squares(e, "ffn", sq_src(x))
            norm_hi_part(e, "ffn", SRC["ffn"][2], SRC["ffn"][3])

            def ffn(s_up, s_down, n_ffn, conv):
                b = BASE[s_up]
                with e.Fori(0, 11) as j:
                    def tile_acts(group, buf):
                        for m in range(4):
                            e.wait_ge(sums_ready, plus(SUMS[s_up] + 4 * group + m + 1, j, 8))
                            if conv:
                                e.activation(buf[:, m, :], tmp[:, m, :], ACT.Identity,
                                             bias=vec("conv_b", FT * group + m, 1, j, 4),
                                             scale=vec("conv_w", 2 * FT + FT * group + m, 1, j, 4)).then_inc(centre, 1)
                            elif group == 0:
                                e.activation(gate[:, m, :], tmp[:, m, :], ACT.Silu).then_inc(silu_done, 1)
                    split_hi(e, b + LEAD, b + LEAD + CPG, j, 2 * CPG)
                    tile_acts(0, gate)
                    if conv:
                        for m in range(4):
                            e.wait_ge(sides, plus(2 * m + 2, j, 16))
                            e.activation(gate[:, m, :], gate[:, m, :], ACT.Silu).then_inc(silu_done, 1)
                    split_hi(e, b + LEAD + CPG, b + LEAD + 2 * CPG, j, 2 * CPG)
                    tile_acts(1, val)
                    for m in range(4):
                        e.wait_ge(prod, plus(44 * n_ffn + m + 1, j, 4))
                        e.activation(hid[:, bass.ds(j * 4 + m, 1), 0, :].rearrange("p a t -> p (a t)"), val[:, m, :],
                                     ACT.Copy).then_inc(hid_hi, 1)
                b = BASE[s_down] + LEAD
                split_hi(e, b, b + 2 * FT)

            ffn("up", "down", 0, True)
            e.wait_ge(resid, RES["down"] + 16)
            squares(e, "fin", sq_src(x))
            e.wait_ge(scaled, NORM["fin"][0] + KT)
            squares(e, "mix2", sq_src(x))
            norm_hi_part(e, "mix2", SRC["mix2"][2])
            for g in range(2):
                b = BASE["qa"] + g * CPG + LEAD
                split_hi(e, b, b + CPG)
                for m in range(4):
                    e.wait_ge(sums_ready, SUMS["qa"] + 4 * g + m + 1)
                    e.activation(qa[:, 4 * g + m, :], tmp[:, m, :], ACT.Copy, scale=HD ** -0.5).then_inc(tmp_read, 1)
            b = BASE["kva"] + LEAD
            split_hi(e, b, b + CPG)
            e.wait_ge(weights_used, BASE["kva"] + CPG)
            for tt in range(2):
                e.activation(va[:, tt, :], ps[:, 2 + tt, 0:A_KV * HD], ACT.Copy).then_inc(rows_copied, 1)
            b = BASE["qkb"] + LEAD
            with e.Fori(0, 2) as j:
                split_hi(e, b, b + 2 * CPG, j, 2 * CPG)
            e.wait_ge(sums_ready, SUMS["qkb"] + 16)
            e.activation(qkb[:, 0:PAIRS, :], qkb[:, 0:PAIRS, :], ACT.Copy, scale=HD ** -0.5).then_inc(qb_scaled, 1)
            for g in range(2):
                b = BASE["vb"] + g * CPG + LEAD
                split_hi(e, b, b + CPG)
                e.wait_ge(weights_used, BASE["vb"] + (g + 1) * CPG)
                for tt in range(2):
                    e.activation(vb[:, tt, g * GW:(g + 1) * GW], ps[:, 4 * g + tt, :], ACT.Copy).then_inc(rows_copied, 1)
            b = BASE["gates"] + LEAD
            with e.Fori(0, 4) as j:
                for g in range(2):
                    split_hi(e, b + g * CPG, b + (g + 1) * CPG, j, 2 * CPG)
                    for m in range(4):
                        e.wait_ge(sums_ready, plus(SUMS["gates"] + 4 * g + m + 1, j, 8))
                        e.activation(gates[:, bass.ds(j * 8 + 4 * g + m, 1), :].rearrange("p a t -> p (a t)"),
                                     tmp[:, m, :], ACT.Sigmoid).then_inc(tmp_read, 1)
            e.wait_ge(tmp_read, 8 + 2 * KT)
            e.dma_start(dist[:], dist_tab).then_inc(s_dist, 16)
            for i in range(PAIRS + 2):
                if i < PAIRS:
                    e.wait_ge(sb_zb, i + 1)
                    if i >= 1:
                        e.wait_ge(sb_sp, i)
                    e.activation(lnb[:], zb[:, i % 3], ACT.Abs).then_inc(sb_step, 1)
                    e.wait_ge(sb_step, 2 * i + 1)
                    e.activation(lnb[:], lnb[:], ACT.Exp, scale=-1.0).then_inc(sb_step, 1)
                    e.wait_ge(sb_step, 2 * i + 2)
                    e.activation(lnb[:], lnb[:], ACT.Ln, bias=1.0).then_inc(sb_ln, 1)
                if 1 <= i <= PAIRS:
                    n = i - 1
                    e.wait_ge(sw_flip, i)
                    if n >= 2:
                        e.wait_ge(mixed2, 4 * (n - 1))
                    e.activation(saT[:, n % 2], ps[:, 0:2, 0:W3], ACT.Copy).then_inc(sw_flipc, 1)
                    e.wait_ge(sb_d, i)
                    e.activation(zb[:, n % 3], zb[:, n % 3], ACT.Exp).then_inc(sb_a, 1)
                if i < PAIRS:
                    e.wait_ge(sw_neg, 2 * (i + 1))
                    o = 4 * i
                    e.activation(small[:, 128:132], small[:, 132:136], ACT.Exp).then_inc(sw_exps, 1)
                    for h in range(2):
                        for b_ in range(2):
                            q = slice(0, P) if b_ == 0 else slice(P, W3)
                            k = 2 * h + b_
                            e.activation(sa[:, i % 2, h, q], sa[:, i % 2, h, q], ACT.Exp,
                                         bias=small[:, 136 + k:137 + k],
                                         accum_out=small[:, 140 + k:141 + k]).then_inc(sw_exps, 1)
                if i >= 2:
                    n = i - 2
                    for br in range(2):
                        e.wait_ge(mixed2, 2 * (2 * n + br + 1))
                        e.activation(pair[:, 8 * br + n, 0, :], ps[:, 6 + br, 0:T], ACT.Copy)\
                            .then_inc(o2_hi, 1)
            for g in range(4):
                b = BASE["bra"] + g * 4 + LEAD
                split_hi(e, b, b + 4)
            for g in range(4):
                b = BASE["brb"] + g * 4 + LEAD
                split_hi(e, b, b + 4)
                for m in range(4):
                    t = 4 * g + m
                    e.wait_ge(merged, t + 1)
                    e.activation(pair2[:, t, 0, :], gates[:, t, :], ACT.Copy).then_inc(m_hi, 1)
            b = BASE["out2"] + LEAD
            with e.Fori(0, 2) as j:
                split_hi(e, b, b + 2 * CPG, j, 2 * CPG)
            e.wait_ge(resid, RES["out2"] + 16)
            squares(e, "ffn2", sq_src(x))
            norm_hi_part(e, "ffn2", SRC["ffn2"][2])
            ffn("up2", "down2", 1, False)
            e.wait_ge(resid, RES["down2"] + 16)
            squares(e, "fin2", sq_src(x))

        @block.vector
        def _(e):
            e.wait_ge(s_vecs, 16)

            e.sem_inc(mod_ready, 1)
            inv_rms(e, "x", 0)
            inv_rms(e, "ctx", 1)
            with e.Fori(0, MOD_G // 2) as g:
                for s in range(2):
                    e.wait_ge(mod_used, g * (2 * CPG) + (s + 1) * CPG)
                    v = ps[:, s, 0:8].rearrange("p (m v) -> p v m", v=2)
                    for w in range(2):
                        e.tensor_tensor(mod[:, w, bass.ds(g * 8 + 4 * s, 4)], v[:, w, :],
                                        vecs[:, bass.ds(g * 8 + VEC["b_mod"][0] + 4 * s, 4)], ALU.add)\
                            .then_inc(mod_ready, 1)
            e.wait_ge(mod_ready, 2 * MOD_G + 1)
            for i, (w, off, gname) in enumerate(((0, SC1, "g_attn"), (1, SC1, "g_attn"), (0, SC2, "g_ffn"))):
                e.scalar_tensor_tensor(out=gain[:, i, :], in0=mod[:, w, off:off + KT], scalar=1.0,
                                       in1=vec(gname, 0, KT), op0=ALU.add, op1=ALU.mult).then_inc(gain_ready, 1)
            e.wait_ge(gain_ready, 3)
            src, g_, dst, shift = SRC["x"]
            norm_apply(e, "x", src, g_, dst, shift)
            split_lo(e, 0, LEAD)
            src, g_, dst, shift = SRC["ctx"]
            for i in range(CPG):
                split_lo(e, LEAD + i, LEAD + i + 1)
                for t in (2 * i, 2 * i + 1):
                    if t >= 4:
                        e.wait_ge(norm_lo, PAIRED["ctx"] + t - 3)
                    norm_scale(e, "ctx", t, src(t), g_(t), 1)
                for t in (2 * i, 2 * i + 1):
                    norm_lo_part(e, "ctx", t, dst, shift)

            def upto(a, stage, n):
                b = BASE[stage] + n + LEAD
                split_lo(e, a, b)
                return b

            def sum_out(bank, out):
                e.tensor_reduce(out, ps[:, bank, :].rearrange("p (s t) -> p t s", s=2), AX_X, ALU.add)\
                    .then_inc(sums_ready, 1)

            at = LEAD + CPG
            e.wait_ge(weights_used, BASE["cq"] + CPG)
            for m in range(4):
                sum_out(m, cq[:, m, :])
            at = upto(at, "ckv", CPG)
            e.wait_ge(weights_used, BASE["ckv"] + CPG)
            for s in range(2):
                for m in range(4):
                    sum_out(4 * (1 - s) + m, ckv[:, m, s, :])
            inv_rms(e, "cq")
            norm_apply(e, "cq", SRC["cq"][0], SRC["cq"][1], SRC["cq"][2])
            at = upto(at, "kr", 2)
            e.wait_ge(weights_used, BASE["kr"] + 2)
            e.wait_ge(s_tabs, 32)
            e.wait_ge(zeroed, 2)
            sum_out(4, rinv[:, 1, :])
            sum_out(7, qn[:, 0, :])
            e.wait_ge(sums_ready, SUMS["kr"] + 2)
            e.tensor_copy(kre[0:64, 1, :], qn[0:64, 0, :]).then_inc(roped, 1)
            e.tensor_copy(kro[64:P, 1, :], qn[64:P, 0, :]).then_inc(roped, 1)
            at = upto(at, "qn", CPG)
            e.wait_ge(turned, 1)
            e.tensor_tensor(qn[:, 1, :], rinv[:, 1, :], cos, ALU.mult).then_inc(rope_mul, 1)
            e.tensor_tensor(qn[:, 2, :], ps[:, 7, 0:T], sin, ALU.mult).then_inc(rope_mul, 1)
            e.wait_ge(rope_mul, 2)
            e.tensor_tensor(kre[0:64, 0, :], qn[0:64, 1, :], qn[0:64, 2, :], ALU.add).then_inc(roped, 1)
            e.tensor_tensor(kro[64:P, 0, :], qn[64:P, 1, :], qn[64:P, 2, :], ALU.add).then_inc(roped, 1)
            e.wait_ge(roped, 4)
            e.wait_ge(weights_used, BASE["qn"] + CPG)
            for m in range(4):
                sum_out(m, qn[:, m, :])
            for name in ("ckv", "ckvc"):
                inv_rms(e, name)
                norm_apply(e, name, SRC[name][0], SRC[name][1], SRC[name][2])
            at = upto(at, "kn", CPG)
            e.wait_ge(weights_used, BASE["kn"] + CPG)
            for s in range(2):
                for m in range(4):
                    sum_out(4 * (1 - s) + m, kn[:, m, s, :])
            at = upto(at, "vn", CPG)
            at = upto(at, "f", CPG)
            for g in range(4):
                at = upto(at, "uq", 2 * (g + 1))
                e.wait_ge(weights_used, BASE["uq"] + 2 * (g + 1))
                b = 4 * (g % 2)
                sum_out(b, qnope[:, 2 * g, :])
                sum_out(b + 1, qnope[:, 2 * g + 1, :])
                sum_out(b + 2, qrope[:, g, :])
            for g in range(4):
                e.wait_ge(turned, 2 + g)
                if g >= 2:
                    e.wait_ge(roped, 4 + 2 * (g - 1))
                e.tensor_tensor(tmp[:, g % 2, :], ps[:, g, 0:T], sin, ALU.mult).then_inc(rope_mul, 1)
                e.tensor_tensor(qrope[:, g, :], qrope[:, g, :], cos, ALU.mult).then_inc(roped, 1)
                e.wait_ge(rope_mul, 3 + g)
                e.wait_ge(roped, 5 + 2 * g)
                e.tensor_tensor(qrope[:, g, :], qrope[:, g, :], tmp[:, g % 2, :], ALU.add).then_inc(roped, 1)
            for g in range(FN_G):
                e.wait_ge(spec_done, g + 1)
                e.tensor_copy(spec[:, g, :], ps[:, g, 0:T]).then_inc(spec_copied, 1)
            for g in range(FN_G):
                e.wait_ge(o_hi, g + 1)
                e.tensor_tensor(pair[:, HEADS + g, 1, :], ps[:, 4 + g, 0:T], pair[:, HEADS + g, 0, :].bitcast(F32),
                                ALU.subtract).then_inc(o_lo, 1)
            for g in range(4):
                at = upto(at, "ukv", 2 * (g + 1))
                e.wait_ge(weights_used, BASE["ukv"] + 2 * (g + 1))
                for m in range(2):
                    for s in range(2):
                        sum_out(2 * m + s, knope[:, 2 * g + m, s, :])
            for i in range(HEADS + 2):
                if i == 1:
                    e.wait_ge(s_bias, 16 * NA_ROWS)
                    e.wait_ge(s_dft, 48)
                    for h in range(NA_H):
                        v = bias[:, h].rearrange("p t (a c) -> p (t a) c", c=GRID_W)
                        mk = tmp[:, 3, 0:GRID_W].unsqueeze(1).to_broadcast([P, 2 * NA_ROWS, GRID_W])
                        e.tensor_tensor(v, v, mk, ALU.add).then_inc(bias_masked, 1)
                if i < HEADS:
                    for t in range(2):
                        n = 2 * i + t
                        e.wait_ge(scores, n + 1)
                        if i >= MLA_H:
                            if i == MLA_H and t == 0:
                                e.wait_ge(bias_masked, NA_H)
                            e.wait_ge(flipped, n - 3)
                            pb, bk = prob[:, i % 2, t, :], ps[:, 2 * (i % 2) + t, :]
                            e.scalar_tensor_tensor(out=pb[:, 0:T], in0=bk[:, 0:T], scalar=NA_SCALE,
                                                   in1=bias[:, i - MLA_H, t, :], op0=ALU.mult, op1=ALU.add)\
                                .then_inc(biased, 1)
                            e.tensor_scalar(pb[:, T:2 * T], bk[:, T:2 * T], NA_SCALE, None, ALU.mult).then_inc(biased, 1)
                            e.wait_ge(biased, 2 * (n - 2 * MLA_H + 1))
                            e.tensor_reduce(small[:, n:n + 1], pb, AX_X, ALU.max).then_inc(maxed, 1)
                        else:
                            e.tensor_reduce(small[:, n:n + 1], ps[:, 2 * (i % 2) + t, :], AX_X, ALU.max)\
                                .then_inc(maxed, 1)
                        e.wait_ge(maxed, n + 1)
                        e.tensor_scalar(small[:, 24 + n:25 + n], small[:, n:n + 1],
                                        -(MLA_SCALE if i < MLA_H else 1.0), None, ALU.mult).then_inc(negmax, 1)
                if i >= 2:
                    h = i - 2
                    e.wait_ge(o_hi, FN_G + h + 1)
                    e.tensor_tensor(pair[:, h, 1, :], ps[:, 6 + h % 2, 0:T], pair[:, h, 0, :].bitcast(F32),
                                    ALU.subtract).then_inc(o_lo, 1)
                if i < HEADS:
                    for t in range(2):
                        n = 2 * i + t
                        e.wait_ge(exps, n + 1)
                        e.reciprocal(small[:, 72 + n:73 + n], small[:, 48 + n:49 + n]).then_inc(recips, 1)
                        e.wait_ge(recips, n + 1)
                        pb = prob[:, i % 2, t, :]
                        e.tensor_scalar(pb, pb, small[:, 72 + n:73 + n], None, ALU.mult).then_inc(probs, 1)

            def residual(stage, g, gt, it=None, per_t=0, bank=None):
                for m in range(4):
                    t = 4 * g + m
                    if it is None:
                        xt = x[:, t, :]
                        gv = None if gt is None else modv(0, gt, t)
                    else:
                        xt = x[:, bass.ds(it * per_t + t, 1), :].rearrange("p a t -> p (a t)")
                        gv = None if gt is None else mod[:, 0, bass.ds(it * per_t + gt + t, 1)]
                    e.wait_ge(sums_ready, plus(SUMS[stage] + t + 1, it, per_t))
                    e.scalar_tensor_tensor(out=xt, in0=tmp[:, m, :], scalar=1.0 if gv is None else gv, in1=xt,
                                           op0=ALU.mult, op1=ALU.add).then_inc(resid, 1)

            for g in range(4):
                at = upto(at, "out", (g + 1) * CPG)
                e.wait_ge(weights_used, BASE["out"] + (g + 1) * CPG)
                for m in range(4):
                    sum_out(4 * (g % 2) + m, tmp[:, m, :])
                residual("out", g, GT1)
            e.wait_ge(resid, RES["out"] + 16)
            inv_rms(e, "ffn")
            norm_apply(e, "ffn", *SRC["ffn"])

            def ffn(s_up, s_down, n_ffn, conv, gt):
                b, u = BASE[s_up], SUMS[s_up]
                with e.Fori(0, 11) as j:
                    def taps(group, buf, first):
                        for m in range(4):
                            e.wait_ge(centre, plus(4 * group + m + 1, j, 8))
                            e.scalar_tensor_tensor(out=buf[:, m, 1:T], in0=tmp[:, m, 0:T - 1],
                                                   scalar=vec("conv_w", FT * group + m, 1, j, 4),
                                                   in1=buf[:, m, 1:T], op0=ALU.mult, op1=ALU.add).then_inc(sides, 1)
                            e.wait_ge(sides, plus(first + 2 * m + 1, j, 16))
                            e.scalar_tensor_tensor(out=buf[:, m, 0:T - 1], in0=tmp[:, m, 1:T],
                                                   scalar=vec("conv_w", 4 * FT + FT * group + m, 1, j, 4),
                                                   in1=buf[:, m, 0:T - 1], op0=ALU.mult, op1=ALU.add)\
                                .then_inc(sides, 1)
                    split_lo(e, b + LEAD, b + LEAD + CPG, j, 2 * CPG)
                    e.wait_ge(weights_used, plus(b + CPG, j, 2 * CPG))
                    for m in range(4):
                        sum_out(m, tmp[:, m, :])
                    if conv:
                        taps(0, gate, 0)
                    split_lo(e, b + LEAD + CPG, b + LEAD + 2 * CPG, j, 2 * CPG)
                    e.wait_ge(weights_used, plus(b + 2 * CPG, j, 2 * CPG))
                    if conv:
                        e.wait_ge(silu_done, plus(4, j, 4))
                    else:
                        e.wait_ge(silu_done, plus(44 * n_ffn + 4, j, 4))
                    for m in range(4):
                        sum_out(4 + m, tmp[:, m, :])
                    if conv:
                        taps(1, val, 8)
                        e.wait_ge(sides, plus(16, j, 16))
                    else:
                        e.wait_ge(sums_ready, plus(u + 8, j, 8))
                    for m in range(4):
                        e.tensor_tensor(val[:, m, :], val[:, m, :] if conv else tmp[:, m, :], gate[:, m, :],
                                        ALU.mult).then_inc(prod, 1)
                    for m in range(4):
                        e.wait_ge(hid_hi, plus(44 * n_ffn + m + 1, j, 4))
                        hv = hid[:, bass.ds(j * 4 + m, 1), :, :].rearrange("p a s t -> p (a s) t")
                        e.tensor_tensor(hv[:, 1, :], val[:, m, :], hv[:, 0, :].bitcast(F32), ALU.subtract)\
                            .then_inc(hid_lo, 1)
                b = BASE[s_down]
                for g in range(4):
                    split_lo(e, b + LEAD + g * FT // 2, b + LEAD + (g + 1) * FT // 2)
                    e.wait_ge(weights_used, b + (g + 1) * FT // 2)
                    for m in range(4):
                        sum_out(4 * (g % 2) + m, tmp[:, m, :])
                    residual(s_down, g, gt)

            ffn("up", "down", 0, True, GT2)
            e.wait_ge(resid, RES["down"] + 16)
            inv_rms(e, "fin")
            for t in range(KT):
                norm_scale(e, "fin", t, x[:, t, :], vec("g_final", t), out=x[:, t, :])
            e.wait_ge(scaled, NORM["fin"][0] + KT)
            inv_rms(e, "mix2")
            norm_apply(e, "mix2", SRC["mix2"][0], SRC["mix2"][1], SRC["mix2"][2])
            for g in range(2):
                b = BASE["qa"] + g * CPG + LEAD
                split_lo(e, b, b + CPG)
                e.wait_ge(weights_used, BASE["qa"] + (g + 1) * CPG)
                if g:
                    e.wait_ge(tmp_read, 4)
                for m in range(4):
                    sum_out(4 * g + m, tmp[:, m, :])
            b = BASE["kva"] + LEAD
            split_lo(e, b, b + CPG)
            e.wait_ge(weights_used, BASE["kva"] + CPG)
            for m in range(2):
                sum_out(m, ka[:, m, :])
            b = BASE["qkb"]
            with e.Fori(0, 2) as j:
                for g in range(2):
                    split_lo(e, b + LEAD + g * CPG, b + LEAD + (g + 1) * CPG, j, 2 * CPG)
                    e.wait_ge(weights_used, plus(b + (g + 1) * CPG, j, 2 * CPG))
                    for m in range(4):
                        sum_out(4 + m if g == 0 else m,
                                qkb[:, bass.ds(j * 8 + 4 * g + m, 1), :].rearrange("p a t -> p (a t)"))
            b = BASE["vb"] + LEAD
            split_lo(e, b, b + 2 * CPG)
            b = BASE["gates"]
            with e.Fori(0, 4) as j:
                for g in range(2):
                    split_lo(e, b + LEAD + g * CPG, b + LEAD + (g + 1) * CPG, j, 2 * CPG)
                    e.wait_ge(weights_used, plus(b + (g + 1) * CPG, j, 2 * CPG))
                    e.wait_ge(tmp_read, plus(8 + 4 * g, j, 8))
                    for m in range(4):
                        sum_out(4 * g + m, tmp[:, m, :])
            e.wait_ge(tmp_read, 8 + 2 * KT)
            e.wait_ge(s_dist, 16)
            e.wait_ge(s_stick, 16)
            for i in range(PAIRS + 2):
                if i < PAIRS:
                    e.wait_ge(sw_scores, 2 * (i + 1))
                    if i >= 2:
                        e.wait_ge(sw_flip, i - 1)
                    for h in range(2):
                        s = -SLOPES[2 * i + h]
                        o = sa[:, i % 2, h]
                        e.scalar_tensor_tensor(out=o[:, 0:P], in0=dist[:, P:2 * P], scalar=s, in1=ps[:, h, 0:P],
                                               op0=ALU.mult, op1=ALU.add).then_inc(sw_biased, 1)
                        e.scalar_tensor_tensor(out=o[:, P:W3], in0=dist[:], scalar=s, in1=ps[:, h, P:W3],
                                               op0=ALU.mult, op1=ALU.add).then_inc(sw_biased, 1)
                    e.wait_ge(sb_z, 2 * (i + 1))
                    if i >= 3:
                        e.wait_ge(mixed2, 4 * (i - 2))
                    mk = stick[:, 0:W3].unsqueeze(1).to_broadcast([P, 2, W3])
                    e.tensor_tensor(zb[:, i % 3], ps[:, 2:4, 0:W3], mk, ALU.add).then_inc(sb_zb, 1)
                if 1 <= i <= PAIRS:
                    n = i - 1
                    e.wait_ge(sb_suffix, i)
                    e.tensor_tensor(zb[:, n % 3], zb[:, n % 3], ps[:, 4:6, 0:W3], ALU.subtract).then_inc(sb_d, 1)
                if i < PAIRS:
                    e.wait_ge(sw_biased, 4 * (i + 1))
                    if i:
                        e.wait_ge(sw_probs, 4 * i)
                    mx = small[:, 144:148].rearrange("p (h b) -> p h b", b=2)
                    e.tensor_reduce(mx[:, :, 0], sa[:, i % 2, :, 0:P], AX_X, ALU.max).then_inc(sw_max, 1)
                    e.tensor_reduce(mx[:, :, 1], sa[:, i % 2, :, P:W3], AX_X, ALU.max).then_inc(sw_max, 1)
                    e.wait_ge(sw_max, 3 * i + 2)
                    sk = vec("sink", 4 * i, 4)
                    e.tensor_tensor(small[:, 144:148], small[:, 144:148], sk, ALU.max).then_inc(sw_max, 1)
                    e.wait_ge(sw_max, 3 * i + 3)
                    e.tensor_tensor(small[:, 132:136], sk, small[:, 144:148], ALU.subtract).then_inc(sw_neg, 1)
                    e.tensor_scalar(small[:, 136:140], small[:, 144:148], -1.0, None, ALU.mult).then_inc(sw_neg, 1)
                    e.wait_ge(sb_ln, i + 1)
                    if i >= 2:
                        e.wait_ge(sb_suffix, i - 1)
                    e.scalar_tensor_tensor(out=sp_[:, i % 2], in0=zb[:, i % 3], scalar=0.0, in1=lnb[:],
                                           op0=ALU.max, op1=ALU.add).then_inc(sb_sp, 1)
                    e.wait_ge(sw_exps, 5 * (i + 1))
                    e.tensor_tensor(small[:, 148:152], small[:, 140:144], small[:, 128:132], ALU.add).then_inc(sw_sum, 1)
                    e.wait_ge(sw_sum, 2 * i + 1)
                    e.reciprocal(small[:, 152:156], small[:, 148:152]).then_inc(sw_sum, 1)
                    e.wait_ge(sw_sum, 2 * i + 2)
                    for h in range(2):
                        for b_ in range(2):
                            q = slice(0, P) if b_ == 0 else slice(P, W3)
                            k = 2 * h + b_
                            e.tensor_scalar(sa[:, i % 2, h, q], sa[:, i % 2, h, q], small[:, 152 + k:153 + k], None,
                                            ALU.mult).then_inc(sw_probs, 1)
                if i >= 2:
                    n = i - 2
                    for br in range(2):
                        e.wait_ge(o2_hi, 2 * n + br + 1)
                        e.tensor_tensor(pair[:, 8 * br + n, 1, :], ps[:, 6 + br, 0:T],
                                        pair[:, 8 * br + n, 0, :].bitcast(F32), ALU.subtract).then_inc(o2_lo, 1)
            for br, stage in enumerate(("bra", "brb")):
                for g in range(4):
                    b = BASE[stage] + g * 4
                    split_lo(e, b + LEAD, b + LEAD + 4)
                    e.wait_ge(weights_used, b + 4)
                    if br or g:
                        e.wait_ge(gated, 16 * br + 4 * g)
                    for m in range(4):
                        sum_out(4 * (g % 2) + m, tmp[:, m, :])
                    for m in range(4):
                        t = 16 * br + 4 * g + m
                        e.wait_ge(sums_ready, SUMS[stage] + 4 * g + m + 1)
                        e.tensor_tensor(gates[:, t, :], gates[:, t, :], tmp[:, m, :], ALU.mult).then_inc(gated, 1)
                    if br:
                        for m in range(4):
                            t = 4 * g + m
                            e.wait_ge(gated, 16 + t + 1)
                            e.tensor_tensor(gates[:, t, :], gates[:, t, :], gates[:, 16 + t, :], ALU.add)\
                                .then_inc(merged, 1)
                        for m in range(4):
                            t = 4 * g + m
                            e.wait_ge(m_hi, t + 1)
                            e.tensor_tensor(pair2[:, t, 1, :], gates[:, t, :], pair2[:, t, 0, :].bitcast(F32),
                                            ALU.subtract).then_inc(m_lo, 1)
            b = BASE["out2"]
            with e.Fori(0, 2) as j:
                for g in range(2):
                    split_lo(e, b + LEAD + g * CPG, b + LEAD + (g + 1) * CPG, j, 2 * CPG)
                    e.wait_ge(weights_used, plus(b + (g + 1) * CPG, j, 2 * CPG))
                    for m in range(4):
                        sum_out(4 * g + m, tmp[:, m, :])
                    residual("out2", g, None, j, 8)
            e.wait_ge(resid, RES["out2"] + 16)
            inv_rms(e, "ffn2")
            norm_apply(e, "ffn2", SRC["ffn2"][0], SRC["ffn2"][1], SRC["ffn2"][2])
            ffn("up2", "down2", 1, False, None)
            e.wait_ge(resid, RES["down2"] + 16)
            inv_rms(e, "fin2")
            for t in range(KT):
                norm_scale(e, "fin2", t, x[:, t, :], vec("g_final2", t), out=x[:, t, :])

        @block.tensor
        def _(e):
            e.wait_ge(s_tabs, 32)
            stats(e, "x")
            stats(e, "ctx")
            e.wait_ge(silu_c, 2)
            with e.Fori(0, MOD_G // 2) as g:
                for s in range(2):
                    for ch in range(CPG):
                        c = s * CPG + ch
                        e.wait_ge(landed[c % R], g * (16 * 2 * CPG // R) + 16 * (c // R + 1))
                        if ch == 0:
                            e.wait_ge(mod_ready, g * 4 + 1)
                        for k in range(2):
                            for m in range(4):
                                last = e.matmul(ps[:, s, 2 * m:2 * m + 2],
                                                raw_view(c, 2, GW)[:, k, m * P:(m + 1) * P], csil[:, 2 * ch + k, :],
                                                start=(ch == 0 and k == 0 and m == 0),
                                                stop=(ch == CPG - 1 and k == 1), skip_group_check=True)
                        last.then_inc(mod_used, 1)

            def wide(banks, acts, n=4):
                def jobs(kt, whi, wlo, first, last):
                    for m in range(n):
                        for bk, act in zip(banks, acts):
                            r = features(e, bk + m, whi[:, m * P:(m + 1) * P], wlo[:, m * P:(m + 1) * P], act(kt),
                                         first, last)
                    return r
                return jobs

            def px(kt):
                return pair[:, kt]

            def pc(kt):
                return ctxpair[:, kt]

            def normed(name):
                return lambda kt: e.wait_ge(norm_lo, PAIRED[name] + kt + 1)

            e.wait_ge(std_ready, 2)
            e.wait_ge(mod_ready, 2 * MOD_G + 1)
            group(e, BASE["cq"], CPG, 2, GW, wide([0], [px]), need=normed("x"))
            e.wait_ge(sums_ready, SUMS["cq"] + 4)
            group(e, BASE["ckv"], CPG, 2, GW, wide([4, 0], [px, pc]), need=normed("ctx"))
            e.wait_ge(sums_ready, SUMS["ckv"] + 8)
            stats(e, "cq")
            def kr_jobs(kt, whi, wlo, first, last):
                features(e, 4, whi, wlo, px(kt), first, last)
                return features(e, 7, whi, wlo, pc(kt), first, last)
            group(e, BASE["kr"], 2, 8, P, kr_jobs)
            e.wait_ge(std_ready, 3)
            group(e, BASE["qn"], CPG, 2, GW, wide([0], [px]))
            stats(e, "ckv")
            e.wait_ge(sums_ready, SUMS["kr"] + 2)
            e.matmul(ps[:, 7, 0:T], rot, rinv[:, 1, :], start=True, stop=True).then_inc(turned, 1)
            stats(e, "ckvc")
            e.wait_ge(sums_ready, SUMS["qn"] + 4)
            e.wait_ge(std_ready, 5)
            e.wait_ge(roped, 4)
            group(e, BASE["kn"], CPG, 2, GW, wide([4, 0], [px, pc]))
            e.wait_ge(sums_ready, SUMS["kn"] + 8)

            def vn_jobs(kt, whi, wlo, first, last):
                for tt in range(4):
                    r = tokens(e, ps[:, 4 + tt, :], whi, wlo, px(kt) if tt < 2 else pc(kt), tt % 2, first, last)
                return r
            group(e, BASE["vn"], CPG, 2, GW, vn_jobs)

            def f_jobs(kt, whi, wlo, first, last):
                for tt in range(2):
                    r = tokens(e, ps[:, tt, :], whi, wlo, px(kt), tt, first, last)
                return r
            group(e, BASE["f"], CPG, 2, GW, f_jobs)
            e.wait_ge(norm_lo, PAIRED["cq"] + RT)
            e.wait_ge(rows_copied, ROWS["f"] + 2)
            for g in range(4):
                if g >= 2:
                    e.wait_ge(sums_ready, SUMS["uq"] + 3 * (g - 1))

                def uq_jobs(kt, whi, wlo, first, last, b=4 * (g % 2)):
                    for m in range(2):
                        s = slice(m * NOPE, (m + 1) * NOPE)
                        features(e, b + m, whi[:, s], wlo[:, s], cqn[:, kt], first, last)
                    s = slice(2 * NOPE, 2 * (NOPE + ROPE))
                    return features(e, b + 2, whi[:, s], wlo[:, s], cqn[:, kt], first, last)
                group(e, BASE["uq"] + 2 * g, 2, 2, 2 * (NOPE + ROPE), uq_jobs)
            e.wait_ge(sums_ready, SUMS["uq"] + 12)
            for g in range(4):
                e.matmul(ps[:, g, 0:T], rot, qrope[:, g, :], start=True, stop=True).then_inc(turned, 1)
            e.wait_ge(s_dft, 32)
            for g in range(FN_G):
                for tt in range(2):
                    m = e.matmul(ps[:, 4 + g, :], f_sb[:, tt, g * P:(g + 1) * P], dft[:, 2 * T * tt:2 * T * (tt + 1)],
                                 start=(tt == 0), stop=(tt == 1))
                m.then_inc(uv_done, 1)
            e.wait_ge(roped, 12)
            for g in range(FN_G):
                e.wait_ge(uv_copied, g + 1)
                for s in range(2):
                    m = e.matmul(ps[:, g, 0:T], dft[:, 4 * T + s * P:4 * T + (s + 1) * P], uv[:, g, s * T:(s + 1) * T],
                                 start=(s == 0), stop=(s == 1))
                m.then_inc(spec_done, 1)
            for g in range(FN_G):
                e.wait_ge(spec_copied, g + 1)
                e.matmul(ps[:, 4 + g, 0:T], wfn[:, g, :], spec[:, g, :], start=True, stop=True).then_inc(fn_done, 1)
            e.wait_ge(o_lo, FN_G)
            e.wait_ge(norm_lo, PAIRED["ckvc"] + RT)
            for g in range(4):
                if g:
                    e.wait_ge(sums_ready, SUMS["ukv"] + 4 * g)
                    e.wait_ge(rows_copied, ROWS["ukv"] + 4 * g)

                def ukv_jobs(kt, whi, wlo, first, last):
                    for m in range(2):
                        s = slice(m * (NOPE + VD), m * (NOPE + VD) + NOPE)
                        for st in range(2):
                            features(e, 2 * m + st, whi[:, s], wlo[:, s], ckvn[:, st, kt], first, last)
                    wv = [w.rearrange("p (m n) -> p m n", m=2)[:, :, NOPE:] for w in (whi, wlo)]
                    for tt in range(4):
                        out = ps[:, 4 + tt, 0:2 * VD].rearrange("p (m n) -> p m n", m=2)
                        r = tokens(e, out, wv[0], wv[1], ckvn[:, tt // 2, kt], tt % 2, first, last)
                    return r
                group(e, BASE["ukv"] + 2 * g, 2, 2, GW, ukv_jobs)
            e.wait_ge(sums_ready, SUMS["ukv"] + 16)
            e.wait_ge(rows_copied, ROWS["ukv"] + 16)
            for i in range(HEADS + 2):
                if i < HEADS:
                    if i >= 2:
                        e.wait_ge(exps, 2 * (i - 1))
                    for t in range(2):
                        q, out = slice(t * P, (t + 1) * P), ps[:, 2 * (i % 2) + t, :]
                        if i < MLA_H:
                            e.matmul(out, qnope[:, i, q], knope[:, i].rearrange("p s t -> p (s t)"), start=True,
                                     stop=False)
                            kr = kro if i % 2 else kre
                            m = e.matmul(out, qrope[:, i // 2, q], kr[:].rearrange("p s t -> p (s t)"), start=False,
                                         stop=True)
                        else:
                            h = i - MLA_H
                            m = e.matmul(out, qn[:, h, q], kn[:, h].rearrange("p s t -> p (s t)"), start=True,
                                         stop=True)
                        m.then_inc(scores, 1)
                if 1 <= i <= HEADS:
                    h = i - 1
                    for t in range(2):
                        e.wait_ge(probs, 2 * h + t + 1)
                        if h >= 1:
                            e.wait_ge(flips_copied, 2 * h + t - 1)
                        for k in range(4):
                            m = e.transpose(ps[:, 4 + t, k * P:(k + 1) * P], prob[:, h % 2, t, k * P:(k + 1) * P],
                                            ident)
                        m.then_inc(flipped, 1)
                if i >= 2:
                    h = i - 2
                    e.wait_ge(flips_copied, 2 * h + 2)
                    if h >= 2:
                        e.wait_ge(o_lo, FN_G + h - 1)
                    for k in range(4):
                        v = v_sb[:, k, h * VD:(h + 1) * VD] if h < MLA_H else vn[:, k, (h - MLA_H) * P:(h - MLA_H + 1) * P]
                        m = e.matmul(ps[:, 6 + h % 2, 0:T], v, probT[:, h % 2, k, :], start=(k == 0), stop=(k == 3))
                    m.then_inc(mixed, 1)
            e.wait_ge(o_lo, FN_G + HEADS)
            for g in range(4):
                if g >= 2:
                    e.wait_ge(sums_ready, SUMS["out"] + 4 * (g - 1))
                group(e, BASE["out"] + g * CPG, CPG, 2, GW, wide([4 * (g % 2)], [px]))
            e.wait_ge(sums_ready, SUMS["out"] + 16)
            stats(e, "ffn")

            def ffn(s_up, s_down, n_ffn, name, stat_no):
                e.wait_ge(std_ready, stat_no)
                e.wait_ge(norm_lo, PAIRED[name] + KT)
                with e.Fori(0, 11) as j:
                    for g in range(2):
                        e.wait_ge(sums_ready, plus(SUMS[s_up] - 4 + 4 * g, j, 8))
                        group(e, BASE[s_up] + g * CPG, CPG, 2, GW, wide([4 * g], [px]), j, 2 * CPG)
                e.wait_ge(hid_lo, 44 * (n_ffn + 1))
                with e.Fori(0, 2) as j:
                    for g in range(2):
                        e.wait_ge(sums_ready, plus(SUMS[s_down] - 4 + 4 * g, j, 8))
                        group(e, BASE[s_down] + g * FT // 2, FT // 2, 2, GW,
                              wide([4 * g], [lambda kt: hid[:, kt]]), j, FT)
                e.wait_ge(sums_ready, SUMS[s_down] + 16)

            ffn("up", "down", 0, "ffn", NORM["ffn"][2] + 1)
            stats(e, "fin")
            stats(e, "mix2")
            e.wait_ge(norm_lo, PAIRED["mix2"] + KT)
            for g in range(2):
                group(e, BASE["qa"] + g * CPG, CPG, 2, GW, wide([4 * g], [px]))
            e.wait_ge(sums_ready, SUMS["qa"] + 4)

            def kva_jobs(kt, whi, wlo, first, last):
                for m in range(2):
                    features(e, m, whi[:, m * P:(m + 1) * P], wlo[:, m * P:(m + 1) * P], px(kt), first, last)
                for tt in range(2):
                    r = tokens(e, ps[:, 2 + tt, 0:T], whi[:, T:2 * T], wlo[:, T:2 * T], px(kt), tt, first, last)
                return r
            group(e, BASE["kva"], CPG, 2, GW, kva_jobs)
            e.wait_ge(rows_copied, ROWS["kva"] + 2)
            e.wait_ge(sums_ready, SUMS["kva"] + 2)
            with e.Fori(0, 2) as j:
                for g in range(2):
                    e.wait_ge(sums_ready, plus(SUMS["qkb"] - 4 + 4 * g, j, 8))
                    group(e, BASE["qkb"] + g * CPG, CPG, 2, GW, wide([4 - 4 * g], [px]), j, 2 * CPG)
            e.wait_ge(sums_ready, SUMS["qkb"] + 16)
            for g in range(2):
                def vb_jobs(kt, whi, wlo, first, last, g=g):
                    for tt in range(2):
                        r = tokens(e, ps[:, 4 * g + tt, :], whi, wlo, px(kt), tt, first, last)
                    return r
                group(e, BASE["vb"] + g * CPG, CPG, 2, GW, vb_jobs)
            e.wait_ge(rows_copied, ROWS["vb"] + 4)
            with e.Fori(0, 4) as j:
                for g in range(2):
                    e.wait_ge(sums_ready, plus(SUMS["gates"] - 4 + 4 * g, j, 8))
                    group(e, BASE["gates"] + g * CPG, CPG, 2, GW, wide([4 * g], [px]), j, 2 * CPG)
            e.wait_ge(sums_ready, SUMS["gates"] + 32)
            e.wait_ge(qb_scaled, 1)
            e.wait_ge(s_stick, 16)
            tri = stick[:, W3:W3 + P]
            for i in range(PAIRS + 2):
                if i < PAIRS:
                    if i == 1:
                        e.wait_ge(sw_biased, 4)
                    if i >= 2:
                        e.wait_ge(sw_flipc, i - 1)
                    for h in range(2):
                        hq = 2 * i + h
                        kv = hq // 4
                        r = slice(HD * (kv % 2), HD * (kv % 2 + 1))
                        qt = qa[r, 4 * (kv // 2) + hq % 4, :]
                        kt_ = ka[r, kv // 2, :]
                        e.matmul(ps[:, h, 0:P], qt[:, 0:P], kt_[:, 0:P], start=True, stop=True)
                        e.matmul(ps[:, h, P:W3], qt[:, P:2 * P], kt_, start=True, stop=True).then_inc(sw_scores, 1)
                    if i:
                        e.wait_ge(sb_zb, i)
                    for h in range(2):
                        r = slice(HD * h, HD * (h + 1))
                        q, k = qkb[r, i, :], qkb[r, PAIRS + i, :]
                        e.matmul(ps[:, 2 + h, 0:T], k[:, 0:P], q, start=True, stop=True)
                        e.matmul(ps[:, 2 + h, T:W3], k[:, P:2 * P], q[:, P:2 * P], start=True, stop=True)\
                            .then_inc(sb_z, 1)
                if 1 <= i <= PAIRS:
                    n = i - 1
                    e.wait_ge(sb_sp, i)
                    if n:
                        e.wait_ge(sb_d, n)
                    for h in range(2):
                        s = sp_[:, n % 2, h]
                        out = ps[:, 4 + h, :]
                        e.matmul(out[:, 0:P], tri, s[:, 0:P], start=True, stop=True)
                        e.matmul(out[:, P:T], tri, s[:, P:T], start=True, stop=False)
                        e.matmul(out[:, P:T], ones, s[:, T:W3], start=False, stop=True)
                        m = e.matmul(out[:, T:W3], tri, s[:, T:W3], start=True, stop=True)
                    m.then_inc(sb_suffix, 1)
                    e.wait_ge(sw_probs, 4 * i)
                    if i < PAIRS:
                        e.wait_ge(sw_biased, 4 * (i + 1))
                    if n:
                        e.wait_ge(sw_flipc, n)
                    for h in range(2):
                        for dst, src in ((0, 0), (1, 1), (2, 2)):
                            m = e.transpose(ps[:, h, dst * P:(dst + 1) * P], sa[:, n % 2, h, src * P:(src + 1) * P],
                                            ident)
                    m.then_inc(sw_flip, 1)
                if i >= 2:
                    n = i - 2
                    c0 = slice(0, P)
                    c1 = slice(P, T)
                    for br in range(2):
                        if br == 0:
                            e.wait_ge(sw_flipc, n + 1)
                        else:
                            e.wait_ge(sb_a, n + 1)
                        if n:
                            e.wait_ge(o2_lo, 2 * (n - 1) + br + 1)
                        for h in range(2):
                            hq = 2 * n + h
                            r = slice(HD * h, HD * (h + 1))
                            pt = saT[:, n % 2, h] if br == 0 else zb[:, n % 3, h]
                            vv = va if br == 0 else vb
                            hv = hq // 4 if br == 0 else hq
                            v = [vv[:, tt, hv * HD:(hv + 1) * HD] for tt in range(2)]
                            e.matmul(ps[r, 6 + br, c0], v[0], pt[:, 0:P], start=True, stop=True)
                            e.matmul(ps[r, 6 + br, c1], v[0], pt[:, P:T], start=True, stop=False)
                            e.matmul(ps[r, 6 + br, c1], v[1], pt[:, T:W3], start=False, stop=True)\
                                .then_inc(mixed2, 1)
            e.wait_ge(o2_lo, 2 * PAIRS)
            for br, stage in enumerate(("bra", "brb")):
                for g in range(4):
                    if br or g >= 2:
                        e.wait_ge(sums_ready, SUMS[stage] + 4 * (g - 1))
                    group(e, BASE[stage] + 4 * g, 4, 2, GW, wide([4 * (g % 2)], [lambda kt: pair[:, 8 * br + kt]]))
            e.wait_ge(m_lo, KT)
            with e.Fori(0, 2) as j:
                for g in range(2):
                    e.wait_ge(sums_ready, plus(SUMS["out2"] - 4 + 4 * g, j, 8))
                    group(e, BASE["out2"] + g * CPG, CPG, 2, GW, wide([4 * g], [lambda kt: pair2[:, kt]]), j, 2 * CPG)
            e.wait_ge(sums_ready, SUMS["out2"] + 16)
            stats(e, "ffn2")
            ffn("up2", "down2", 1, "ffn2", NORM["ffn2"][2] + 1)
            stats(e, "fin2")


_ORDER = ("xT", "ctxT", "vecs", "w_mod", "w_in", "w_uq", "w_ukv", "rpb", "w_fnet", "w_out", "w_up", "w_down",
          "w_in2", "w_bra", "w_brb", "w_out2", "w_up2", "w_down2",
          "base_tab", "rope_tab", "dft_tab", "na_mask", "stick_tab", "dist_tab")


def toeplitz(rpb):
    wide = np.zeros(rpb.shape[:2] + (2 * GRID_W - 1,), rpb.dtype)
    o = GRID_W - NA_KW
    wide[:, :, o:o + 2 * NA_KW - 1] = rpb
    return np.stack([wide[:, :, GRID_W - 1 - w:2 * GRID_W - 1 - w] for w in range(GRID_W)])


def lay_out(inputs):
    g = {k: np.asarray(v) for k, v in inputs.items()}

    def cols(v):
        return np.ascontiguousarray(v.reshape(-1, P).T)

    vecs = np.zeros((P, NV), np.float32)

    def put(name, v):
        o, n = VEC[name]
        vecs[:, o:o + n] = v

    put("c", cols(g["c"]))
    put("c_ctx", cols(g["c_ctx"]))
    put("b_mod", cols(g["b_mod"]))
    put("g_attn", cols(g["g_attn"]))
    put("g_ffn", cols(g["g_ffn"]))
    put("g_q", cols(g["g_q"]))
    put("g_kv", cols(g["g_kv"]))
    put("conv_w", cols(g["conv_w"]))
    put("conv_b", cols(g["conv_b"]))
    put("g_final", cols(g["g_final"]))
    put("g_mix2", cols(g["norm_mix_g_2"]))
    put("g_ffn2", cols(g["norm_ffn_g_2"]))
    put("g_final2", cols(g["norm_final_g_2"]))
    put("sink", np.broadcast_to(np.repeat(g["sink_logits_2"].reshape(-1), 2), (P, 2 * A_H)))
    put("eps", np.float32(EPS))
    out = dict(
        xT=np.ascontiguousarray(g["x"][0].T), ctxT=np.ascontiguousarray(g["ctx"][0].T), vecs=vecs,
        w_mod=g["w_mod"][0], w_in=g["w_in"][0], w_uq=g["w_uq"][0], w_ukv=g["w_ukv"][0], rpb=toeplitz(g["na_rpb"][0]),
        w_fnet=g["w_fnet"][0], w_out=g["w_out"][0], w_up=g["w_up"][0], w_down=g["w_down"][0],
        w_in2=g["w_in_2"][0], w_bra=g["w_branch_a_2"][0], w_brb=g["w_branch_b_2"][0], w_out2=g["w_out_2"][0],
        w_up2=g["w_ffn_in_2"][0], w_down2=g["w_ffn_down_2"][0])
    out.update(host_tables())
    return out


def kernel(**inputs):
    import concourse.bacc as bacc
    from concourse.bass_utils import run_bass_kernel_spmd

    arrays = lay_out(inputs)
    nc = bacc.Bacc("TRN2", target_bir_lowering=False, num_devices=1)
    maps, args = {}, []
    for name in _ORDER:
        a = np.ascontiguousarray(arrays[name])
        maps[f"in_{name}"] = a
        args.append(nc.dram_tensor(f"in_{name}", a.shape, mybir.dt.from_np(a.dtype), kind="ExternalInput").ap())
    args.append(nc.dram_tensor("outT", (D, T), F32, kind="ExternalOutput").ap())
    two_blocks(nc, *args)
    r = run_bass_kernel_spmd(nc, [maps], core_ids=[0])
    return np.ascontiguousarray(r.results[0]["outT"].T)[None]
```

```python
from contextlib import ExitStack

import numpy as np

import concourse.bass as bass
from concourse import mybir

F32 = mybir.dt.float32
F32R = mybir.dt.float32r
ALU = mybir.AluOpType
ACT = mybir.ActivationFunctionType
AX_X = mybir.AxisListType.X

P = 128
D = 2048
T = 256
KT = D // P
FF = 5632
FT = FF // P
R = 4
LEAD = R
CH = 1024
GW = 512
CPG = KT // 2
EPS = 1e-6
BIG = 1e30

MLA_H, NOPE, ROPE, VD, RANK = 8, 128, 64, 128, 512
RT = RANK // P
MLA_SCALE = (NOPE + ROPE) ** -0.5
NA_H, NA_ROWS, GRID_W, NA_KH, NA_KW = 4, 4, 64, 8, 16
NA_SCALE = 128 ** -0.5
FN_G = 4
HEADS = MLA_H + NA_H

A_H, A_KV, B_H, HD = 16, 4, 16, 64
PAIRS = A_H // 2
SLOPES = [2.0 ** (-8.0 * (h + 1) / A_H) for h in range(A_H)]

VEC = {}


def _vec(name, n):
    VEC[name] = (VEC["_n"] if "_n" in VEC else 0, n)
    VEC["_n"] = VEC[name][0] + n


for _name, _n in (("c", KT), ("c_ctx", KT), ("b_mod", 6 * KT), ("g_attn", KT), ("g_ffn", KT),
                  ("g_q", RT), ("g_kv", RT), ("conv_w", 3 * 2 * FT), ("conv_b", 2 * FT),
                  ("g_final", KT), ("g_mix2", KT), ("g_ffn2", KT), ("g_final2", KT),
                  ("sink", 2 * A_H), ("eps", 1)):
    _vec(_name, _n)
NV = VEC["_n"]

STAGES = [("mod1", 8, CPG), ("cq", 1, CPG), ("ckv", 1, CPG), ("kr", 1, 2), ("qn", 1, CPG), ("kn", 1, CPG),
          ("vn", 1, CPG), ("f", 1, CPG), ("uq", 4, 2), ("ukv", 4, 2), ("out", 4, CPG),
          ("up", 22, CPG), ("down", 4, FT // 2),
          ("qa", 2, CPG), ("kva", 1, CPG), ("qkb", 4, CPG), ("vb", 2, CPG), ("gates", 8, CPG),
          ("bra", 4, 4), ("brb", 4, 4), ("out2", 4, CPG), ("up2", 22, CPG), ("down2", 4, FT // 2)]
BASE = {}
N_CHUNKS = 0
for _s, _g, _n in STAGES:
    BASE[_s] = N_CHUNKS
    N_CHUNKS += _g * _n
N_EXTRA = 4 * D // GW * CPG
EXTRA = {}
for _s, _k in (("ckv", 2), ("qn", 1), ("kn", 2), ("vn", 2), ("f", 1), ("ukv", 2)):
    for _i in range(CPG):
        EXTRA[BASE[_s] + _i] = _k
ATT_EXTRA = 16
for _i in range(R, 28):
    EXTRA[BASE["out"] + _i] = 2 if _i % 3 == 0 else 1
SEQ = []
for _c in range(BASE["up"]):
    SEQ.append(("weights", _c))
    for _ in range(EXTRA.get(_c, 0) + (ATT_EXTRA if _c == BASE["out"] + R - 1 else 0)):
        SEQ.append(("extra", sum(q[0] == "extra" for q in SEQ)))
assert SEQ[-1][0] == "weights" and len(SEQ) == BASE["up"] + N_EXTRA and N_EXTRA % R == 0
POS = {q: i for i, q in enumerate(SEQ)}


def position(c):
    return POS[("weights", c)] if c < BASE["up"] else c + N_EXTRA


SUMS = {}
N_SUMS = 0
for _s, _n in (("cq", 4), ("ckv", 8), ("kr", 2), ("qn", 4), ("kn", 8), ("uq", 12), ("ukv", 16),
               ("out", 16), ("up", 88), ("down", 16), ("qa", 8), ("kva", 2), ("qkb", 16),
               ("gates", 32), ("bra", 16), ("brb", 16), ("out2", 16), ("up2", 88), ("down2", 16)):
    SUMS[_s] = N_SUMS
    N_SUMS += _n
ROWS = {}
N_ROWS = 0
for _s, _n in (("vn", 4), ("f", 2), ("ukv", 16), ("kva", 2), ("vb", 4)):
    ROWS[_s] = N_ROWS
    N_ROWS += _n

NORM = {}
_t = 0
for _i, (_s, _n) in enumerate((("x", KT), ("ctx", KT), ("cq", RT), ("ckv", RT), ("ckvc", RT),
                               ("ffn", KT), ("fin", KT), ("mix2", KT), ("ffn2", KT), ("fin2", KT))):
    NORM[_s] = (_t, {"cq": 0, "ckv": RT // 2, "ckvc": RT}.get(_s), _i, _n)
    _t += 0 if _s == "fin" else _n


def plus(base, it, per):
    return base if it is None else it * per + base


def host_tables():
    f = np.float32
    n = ROPE // 4
    freqs = (f(10000.0) ** (-np.arange(n, dtype=f) / f(n))).astype(f)
    pos = np.arange(T)
    ang = np.zeros((ROPE, T), f)
    rot = np.zeros((ROPE, ROPE), f)
    for half, where in enumerate((pos // GRID_W, pos % GRID_W)):
        for i in range(n):
            a, b = half * 2 * n + i, half * 2 * n + n + i
            ang[a] = ang[b] = where.astype(f) * freqs[i]
            rot[b, a] = -1.0
            rot[a, b] = 1.0
    rope = np.zeros((P, 2 * T + P), f)
    for s in range(2):
        rope[s * ROPE:(s + 1) * ROPE, 0:T] = np.cos(ang)
        rope[s * ROPE:(s + 1) * ROPE, T:2 * T] = np.sin(ang)
        rope[s * ROPE:(s + 1) * ROPE, 2 * T + s * ROPE:2 * T + (s + 1) * ROPE] = rot
    pick = np.zeros((P, 2), f)
    pick[0:4] = np.tile(np.eye(2, dtype=f), (2, 1))
    base = np.concatenate([np.eye(P, dtype=f), np.ones((P, P), f), pick], axis=1)
    l = np.arange(T)
    angl = 2 * np.pi * ((l[:, None] * l[None, :]) % T) / T
    cl = np.concatenate([np.cos(angl), np.sin(angl)], axis=1)
    c = np.arange(P)
    angc = 2 * np.pi * ((c[:, None] * c[None, :]) % P) / P
    ortho = 1.0 / np.sqrt(T * P)
    dft = np.concatenate([cl[:P], cl[P:], np.cos(angc) * ortho, -np.sin(angc) * ortho], axis=1).astype(f)
    w = np.arange(P) % GRID_W
    start = np.clip(w - NA_KW // 2, 0, GRID_W - NA_KW)[:, None]
    col = np.arange(GRID_W)[None, :]
    na_mask = np.where((col >= start) & (col < start + NA_KW), 0.0, -BIG).astype(f)
    k, q = np.arange(P)[:, None], np.arange(P)[None, :]
    strict = np.where(k < q, 0.0, -BIG).astype(f)
    tri = (k >= q).astype(f)
    stick = np.concatenate([strict, np.zeros((P, P), f), strict, tri], axis=1)
    qi, ki = np.arange(P)[:, None], np.arange(2 * P)[None, :]
    dist = P + qi - ki
    dist = np.where((dist >= 0) & (dist < P), dist, BIG).astype(f)
    return dict(base_tab=base, rope_tab=rope, dft_tab=dft, na_mask=na_mask, stick_tab=stick, dist_tab=dist)


def two_blocks(nc, xT, ctxT, vecs_d, w_mod, w_in, w_uq, w_ukv, rpb, w_fnet, w_out, w_up, w_down,
               w_in2, w_bra, w_brb, w_out2, w_up2, w_down2,
               base_tab, rope_tab, dft_tab, na_mask, stick_tab, dist_tab, outT):
    ctx = ExitStack()
    with ctx:
        def sem(name):
            return ctx.enter_context(nc.semaphore(name))

        top = [-(-nc.sbuf_base // 32) * 32]

        def place(name, shape, dt=F32, at=None):
            size = 4 * int(np.prod(shape[1:]))
            if at is None:
                at = top[0]
                top[0] += -(-size // 32) * 32
            assert at + size <= nc.sbuf_usable_end, (name, at + size - nc.sbuf_usable_end)
            return nc.alloc_sbuf_tensor_at(name, shape, dt, offset=at), at

        raw, _ = place("raw", [P, R, CH])
        hi, _ = place("hi", [P, R, CH], F32R)
        lo, _ = place("lo", [P, R, CH], F32R)
        x, _ = place("x", [P, KT, T])
        pair, _ = place("pair", [P, KT, 2, T], F32R)
        tmp, tmp_at = place("tmp", [P, 4, T])
        base, _ = place("base", [P, 2 * P + 2])
        ident, ones, pick = base[:, 0:P], base[:, P:2 * P], base[0:4, 2 * P:2 * P + 2]
        vecs, _ = place("vecs", [P, NV])
        mod, _ = place("mod", [P, 2, 6 * KT])
        csil, _ = place("csil", [P, KT, 2])
        csplit, _ = place("csplit", [P, KT, 4], F32R)
        gain, _ = place("gain", [P, 3, KT])
        std, _ = place("std", [P, T])
        rinv, _ = place("rinv", [P, 2, T])
        small, _ = place("small", [P, 8 * 24])
        rope, rope_at = place("rope", [P, 2 * T + P])
        cos, sin, rot = rope[:, 0:T], rope[:, T:2 * T], rope[:, 2 * T:2 * T + P]
        reg = top[0]
        K1 = 1024
        ctxpair, _ = place("ctxpair", [P, KT, 2, T], F32R, reg)
        cq, _ = place("cq", [P, RT, T], at=reg + 32 * K1)
        mrows, _ = place("mrows", [P, 2, GW], at=reg + 32 * K1)
        ckv, _ = place("ckv", [P, RT, 2, T], at=reg + 36 * K1)
        cqn, _ = place("cqn", [P, RT, 2, T], F32R, reg + 44 * K1)
        ckvn, _ = place("ckvn", [P, 2, RT, 2, T], F32R, reg + 52 * K1)
        kre, _ = place("kre", [P, 2, T], at=reg + 68 * K1)
        kro, _ = place("kro", [P, 2, T], at=reg + 70 * K1)
        qn, _ = place("qn", [P, NA_H, T], at=reg + 72 * K1)
        kn, _ = place("kn", [P, NA_H, 2, T], at=reg + 76 * K1)
        vn, _ = place("vn", [P, 4, GW], at=reg + 84 * K1)
        f_sb, _ = place("f_sb", [P, 2, GW], at=reg + 92 * K1)
        ctx_x, _ = place("ctx_x", [P, KT, T], at=reg + 76 * K1)
        dft, _ = place("dft", [P, 4 * T + 2 * P], at=reg)
        wfn, _ = place("wfn", [P, FN_G, P], at=reg + 5 * K1)
        uv, _ = place("uv", [P, FN_G, 2 * T], at=reg + 7 * K1)
        spec, _ = place("spec", [P, FN_G, T], at=reg + 15 * K1)
        knope, _ = place("knope", [P, MLA_H, 2, T], at=reg)
        v_sb, _ = place("v_sb", [P, 4, MLA_H * VD], at=reg + 16 * K1)
        qnope, _ = place("qnope", [P, MLA_H, T], at=reg + 32 * K1)
        qrope, _ = place("qrope", [P, MLA_H // 2, T], at=reg + 40 * K1)
        prob, _ = place("prob", [P, 2, 2, 2 * T], at=reg + 44 * K1)
        probT, _ = place("probT", [P, 2, 4, T], at=reg + 52 * K1)
        bias, _ = place("bias", [P, NA_H, 2, T], at=reg + 60 * K1)
        late, _ = place("late", [P, 4, GW], at=reg + 80 * K1)
        hid, _ = place("hid", [P, FT, 2, T], F32R, reg)
        sq_acc, _ = place("sq_acc", [P, 2, 2, T], at=reg + 88 * K1)
        sq_slot, _ = place("sq_slot", [P, 2, 2, T], at=reg + 92 * K1)
        gate, _ = place("gate", [P, 4, T], at=reg + 88 * K1)
        val, _ = place("val", [P, 4, T], at=reg + 92 * K1)
        qa, _ = place("qa", [P, PAIRS, T], at=reg)
        ka, _ = place("ka", [P, 2, T], at=reg + 8 * K1)
        va, _ = place("va", [P, 2, A_KV * HD], at=reg + 10 * K1)
        qkb, _ = place("qkb", [P, 2 * PAIRS, T], at=reg + 12 * K1)
        vb, _ = place("vb", [P, 2, B_H * HD], at=reg + 28 * K1)
        gates, _ = place("gates", [P, 2 * KT, T], at=reg + 36 * K1)
        W3 = 3 * P
        sa, _ = place("sa", [P, 2, 2, W3], at=reg + 68 * K1)
        saT, _ = place("saT", [P, 2, 2, W3], at=reg + 74 * K1)
        sp_, _ = place("sp_", [P, 2, 2, W3], at=reg + 80 * K1)
        zb, _ = place("zb", [P, 3, 2, W3], at=reg + 86 * K1)
        lnb, _ = place("lnb", [P, 2, W3], at=tmp_at)
        dist, _ = place("dist", [P, 2 * P], at=tmp_at + 3 * K1)
        stick, _ = place("stick", [P, 4 * P], at=rope_at)
        pair2, _ = place("pair2", [P, KT, 2, T], F32R, reg)

        ps = ctx.enter_context(nc.psum_tensor("ps", [P, 8, 512], F32))

        def vec(name, i=0, n=1, it=None, per=0):
            o = VEC[name][0] + i
            if it is None:
                return vecs[:, o:o + n]
            return vecs[:, bass.ds(it * per + o, n)]

        landed = [sem(f"landed{i}") for i in range(R)]
        s_x, s_ctx, s_vecs, s_tabs = sem("x_landed"), sem("ctx_landed"), sem("vecs_landed"), sem("tabs_landed")
        s_dft, s_bias, s_stick, s_dist = sem("dft_landed"), sem("bias_landed"), sem("stick_landed"), sem("dist_landed")
        mod_rows, mod_turned, hi_ready, lo_ready, weights_used = sem("mod_rows"), sem("mod_turned"), sem("hi_ready"), sem("lo_ready"), sem("weights_used")
        sums_ready, rows_copied = sem("sums_ready"), sem("rows_copied")
        csplit_hi, csplit_lo = sem("csplit_hi"), sem("csplit_lo")
        extra_used, mod_sum, late_mod, x_again = sem("extra_used"), sem("mod_sum"), sem("late_mod"), sem("x_again")
        silu_c, mod_ready, gain_ready = sem("silu_c"), sem("mod_ready"), sem("gain_ready")
        sq_ready, sq_used, std_ready, rinv_ready = sem("sq_ready"), sem("sq_used"), sem("std_ready"), sem("rinv_ready")
        scaled, norm_hi, norm_lo = sem("scaled"), sem("norm_hi"), sem("norm_lo")
        zeroed = sem("zeroed")
        turned, rope_mul, roped = sem("turned"), sem("rope_mul"), sem("roped")
        uv_done, uv_copied, spec_done, spec_copied, fn_done = (sem("uv_done"), sem("uv_copied"), sem("spec_done"),
                                                              sem("spec_copied"), sem("fn_done"))
        o_hi, o_lo = sem("o_hi"), sem("o_lo")
        scores, biased, maxed, negmax = sem("scores"), sem("biased"), sem("maxed"), sem("negmax")
        exps, recips, probs = sem("exps"), sem("recips"), sem("probs")
        flipped, flips_copied, mixed = sem("flipped"), sem("flips_copied"), sem("mixed")
        bias_masked = sem("bias_masked")
        resid = sem("resid")
        centre, sides, silu_done, prod = sem("centre"), sem("sides"), sem("silu_done"), sem("prod")
        hid_hi, hid_lo = sem("hid_hi"), sem("hid_lo")
        tmp_read, qb_scaled, gated, merged = (sem("tmp_read"), sem("qb_scaled"),
                                                         sem("gated"), sem("merged"))
        m_hi, m_lo = sem("m_hi"), sem("m_lo")
        sw_scores, sw_biased, sw_max, sw_neg = sem("sw_scores"), sem("sw_biased"), sem("sw_max"), sem("sw_neg")
        sw_exps, sw_sum, sw_probs, sw_flip, sw_flipc = (sem("sw_exps"), sem("sw_sum"), sem("sw_probs"),
                                                       sem("sw_flip"), sem("sw_flipc"))
        sb_z, sb_zb, sb_ln, sb_sp, sb_suffix, sb_d, sb_a = (sem("sb_z"), sem("sb_zb"), sem("sb_ln"), sem("sb_sp"),
                                                           sem("sb_suffix"), sem("sb_d"), sem("sb_a"))
        sb_step = sem("sb_step")
        sq_piece, sq_added, sq_sum, mix_ms, x_between = (sem("sq_piece"), sem("sq_added"), sem("sq_sum"), sem("mix_ms"),
                                                         sem("x_between"))
        mixed2, o2_hi, o2_lo = sem("mixed2"), sem("o2_hi"), sem("o2_lo")
        stored = sem("stored")

        block = ctx.enter_context(nc.Block())

        def slot(c):
            return position(c) % R

        def load(e, p, dst, src, it=None, per=0):
            prev = p - R
            if prev >= len(SEQ):
                e.wait_ge(lo_ready, plus(prev - N_EXTRA + 1, it, per))
            elif prev >= 0:
                kind, i = SEQ[prev]
                if kind == "weights":
                    e.wait_ge(lo_ready, plus(i + 1, it, per))
                else:
                    e.wait_ge(extra_used, 2 * (i + 1))
            e.dma_start(dst, src).then_inc(landed[p % R], 16)

        def raw_view(p, k, n):
            return raw[:, p % R, 0:k * n].rearrange("p (k n) -> p k n", k=k)

        def split_view(part, c, k, n):
            return part[:, c % R, 0:k * n].rearrange("p (k n) -> p k n", k=k)

        def pieces(c, *parts):
            r = raw[:, slot(c), :]
            ds = [p[:, c % R, :] for p in parts]
            if BASE["kr"] <= c < BASE["kr"] + 2:
                src = r[:, 0:CH // 2].rearrange("p (k n) -> p k n", n=ROPE)
                ds = [d.rearrange("p (k j n) -> p k j n", j=2, n=ROPE) for d in ds]
                return [[d[:, :, j] for d in ds] + [src] for j in range(2)]
            if BASE["uq"] <= c < BASE["ukv"]:
                n = 2 * 2 * (NOPE + ROPE)
                src = r[:, 0:n].rearrange("p (k m n) -> p k m n", k=2, m=2)
                ds = [d[:, 0:n].rearrange("p (k n) -> p k n", k=2) for d in ds]
                plain = [d[:, :, 0:2 * NOPE].rearrange("p k (m n) -> p k m n", m=2) for d in ds]
                rotary = [d[:, :, 2 * NOPE:].rearrange("p k (m n) -> p k m n", m=2) for d in ds]
                return [plain + [src[:, :, :, 0:NOPE]], rotary + [src[:, :, :, NOPE:]]]
            if BASE["qa"] <= c < BASE["kva"]:
                return [[d[:, k * GW:(k + 1) * GW].rearrange("p (i a d) -> p i a d", i=4, a=2) for d in ds]
                        + [r[:, k * GW:(k + 1) * GW].rearrange("p (a i d) -> p i a d", i=4, a=2)] for k in range(2)]
            return [ds + [r]]

        def split_hi(e, a, b, it=None, per=0):
            for c in range(a, min(b, N_CHUNKS)):
                e.wait_ge(landed[slot(c)], plus(16 * (position(c) // R + 1), it, 16 * per // R))
                if c >= R:
                    e.wait_ge(weights_used, plus(c - R + 1, it, per))
                for h, r in pieces(c, hi):
                    m = e.activation(h, r, ACT.Copy)
                m.then_inc(hi_ready, 1)

        def split_lo(e, a, b, it=None, per=0):
            for c in range(a, min(b, N_CHUNKS)):
                e.wait_ge(hi_ready, plus(c + 1, it, per))
                for l, h, r in pieces(c, lo, hi):
                    m = e.tensor_tensor(l, r, h.bitcast(F32), ALU.subtract)
                m.then_inc(lo_ready, 1)
                if EXTRA.get(c, 0):
                    i = SEQ[position(c) + 1][1]
                    accumulate(e, i, i + EXTRA[c])

        def late_acc(i):
            if i < 12:
                return x[:, 2 * (i % 8):2 * (i % 8) + 2, :].rearrange("p a t -> p (a t)")
            return late[:, i - 12, :]

        def accumulate(e, a, b):
            for i in range(a, b):
                p = POS[("extra", i)]
                e.wait_ge(landed[p % R], 16 * (p // R + 1))
                acc = late_acc(i // CPG)
                for k in range(2):
                    kt = 2 * (i % CPG) + k
                    w, c = raw_view(p, 2, GW)[:, k, :], csil[:, kt, 0:1]
                    if kt == 0:
                        if 8 <= i // CPG < 12:
                            e.wait_ge(mod_sum, 1)
                        e.tensor_scalar(acc, w, c, None, ALU.mult).then_inc(extra_used, 1)
                    else:
                        e.wait_ge(extra_used, 2 * i + k)
                        e.scalar_tensor_tensor(out=acc, in0=w, scalar=c, in1=acc, op0=ALU.mult, op1=ALU.add)\
                            .then_inc(extra_used, 1)

        def late_sums(e, a, b, bank):
            e.wait_ge(extra_used, 2 * CPG * b)
            for i in range(a, b):
                for m in range(4):
                    col = 4 * (i - a) + m
                    r = e.matmul(ps[:, bank, col:col + 1], late_acc(i)[:, m * P:(m + 1) * P], ones[:, 0:1],
                                 start=True, stop=True)
            r.then_inc(mod_sum, 1)

        def late_bias(e, n, a, b, bank):
            e.wait_ge(mod_sum, n)
            o = 2 * KT + 4 * a
            k = 4 * (b - a)
            e.tensor_tensor(mod[:, 0, o:o + k], ps[:, bank, 0:k], vec("b_mod", o, k), ALU.add).then_inc(late_mod, 1)

        def group(e, c0, n_chunks, kpc, w, jobs, it=None, per=0, need=None):
            for ch in range(n_chunks):
                c = c0 + ch
                e.wait_ge(lo_ready, plus(c + 1, it, per))
                for k in range(kpc):
                    kt = ch * kpc + k
                    if need is not None:
                        need(kt)
                    last = jobs(kt, split_view(hi, c, kpc, w)[:, k], split_view(lo, c, kpc, w)[:, k],
                                kt == 0, kt == n_chunks * kpc - 1)
                last.then_inc(weights_used, 1)

        def features(e, bank, whi, wlo, act, first, last):
            out = ps[:, bank, :]
            both = act.rearrange("p s t -> p (s t)")
            if first:
                e.matmul(out, whi, both, start=True, stop=False)
                return e.matmul(out[:, T:2 * T], wlo, act[:, 0, :], start=False, stop=False)
            m = e.matmul(out[:, T:2 * T], wlo, act[:, 0, :], start=False, stop=False)
            return e.matmul(out, whi, both, start=False, stop=last)

        def tokens(e, out, whi, wlo, act, tt, first, last):
            ahi, alo = act[:, 0, tt * P:(tt + 1) * P], act[:, 1, tt * P:(tt + 1) * P]
            e.matmul(out, alo, whi, start=first, stop=False)
            e.matmul(out, ahi, wlo, start=False, stop=False)
            return e.matmul(out, ahi, whi, start=False, stop=last)

        @block.sync
        def _(e):
            e.dma_start(vecs[:], vecs_d).then_inc(s_vecs, 16)
            wm = w_mod.rearrange("(t p) n -> p t n", p=P)

            def extras(p):
                while p + 1 < len(SEQ) and SEQ[p + 1][0] == "extra":
                    p += 1
                    i = SEQ[p][1]
                    ch, col = i % CPG, 2 * D + i // CPG * GW
                    load(e, p, raw_view(p, 2, GW), wm[:, 2 * ch:2 * ch + 2, col:col + GW])

            for c in range(8 * CPG):
                g, ch = c // CPG, c % CPG
                col = (D + g * GW) % (2 * D)
                load(e, c, raw_view(c, 2, GW), wm[:, 2 * ch:2 * ch + 2, col:col + GW])
                if c == 6:
                    e.dma_start(x[:], xT.rearrange("(t p) n -> p t n", p=P)).then_inc(s_x, 16)
                if c == 22:
                    e.dma_start(ctx_x[:], ctxT.rearrange("(t p) n -> p t n", p=P)).then_inc(s_ctx, 16)

            def stream(w, stage, col, g=0, it=None, per=0, col_per=0, kts=2, n=GW, chunks=CPG):
                wv = w.rearrange("(t p) n -> p t n", p=P)
                for ch in range(chunks):
                    p = position(BASE[stage] + g * chunks + ch)
                    cols = slice(col, col + n) if it is None else bass.ds(it * col_per + col, n)
                    load(e, p, raw_view(p, kts, n), wv[:, kts * ch:kts * (ch + 1), cols], it, per)
                    extras(p)

            for stage, col in (("cq", 0), ("ckv", 512), ("kr", 1024), ("qn", 1088), ("kn", 1600), ("vn", 2112),
                               ("f", 2624)):
                if stage == "kr":
                    stream(w_in, stage, col, kts=8, n=ROPE, chunks=2)
                else:
                    stream(w_in, stage, col)
            for g in range(4):
                stream(w_uq, "uq", g * 384, g, n=384, chunks=2)
            for g in range(4):
                stream(w_ukv, "ukv", g * GW, g, chunks=2)
            for g in range(4):
                stream(w_out, "out", g * GW, g)

            def ffn_stream(up, down, s_up, s_down):
                with e.Fori(0, 11) as j:
                    stream(up, s_up, 0, 0, j, 2 * CPG, GW)
                    stream(up, s_up, FF, 1, j, 2 * CPG, GW)
                with e.Fori(0, 2) as j:
                    for g in range(2):
                        stream(down, s_down, g * GW, g, j, FT, 2 * GW, chunks=FT // 2)

            ffn_stream(w_up, w_down, "up", "down")
            for g in range(2):
                stream(w_in2, "qa", g * GW, g)
            stream(w_in2, "kva", 1024)
            with e.Fori(0, 2) as j:
                for g in range(2):
                    stream(w_in2, "qkb", 1536 + g * GW, g, j, 2 * CPG, 2 * GW)
            for g in range(2):
                stream(w_in2, "vb", 3584 + g * GW, g)
            with e.Fori(0, 4) as j:
                for g in range(2):
                    stream(w_in2, "gates", 4608 + g * GW, g, j, 2 * CPG, 2 * GW)
            for g in range(4):
                stream(w_bra, "bra", g * GW, g, chunks=4)
            for g in range(4):
                stream(w_brb, "brb", g * GW, g, chunks=4)
            with e.Fori(0, 2) as j:
                for g in range(2):
                    stream(w_out2, "out2", g * GW, g, j, 2 * CPG, 2 * GW)
            ffn_stream(w_up2, w_down2, "up2", "down2")

            ov = outT.rearrange("(t p) n -> p t n", p=P)
            for i in range(4):
                e.wait_ge(scaled, NORM["fin2"][0] + 4 * (i + 1))
                e.dma_start(ov[:, 4 * i:4 * i + 4, :], x[:, 4 * i:4 * i + 4, :]).then_inc(stored, 16)
            e.wait_ge(stored, 64)

        @block.gpsimd
        def _(e):
            e.dma_start(base[:], base_tab).then_inc(s_tabs, 16)
            e.dma_start(rope[:], rope_tab).then_inc(s_tabs, 16)
            e.memset(kre[64:P, :, :], 0.0).then_inc(zeroed, 1)
            e.memset(kro[0:64, :, :], 0.0).then_inc(zeroed, 1)
            e.wait_ge(weights_used, BASE["f"])
            e.dma_start(dft[:], dft_tab).then_inc(s_dft, 16)
            e.dma_start(wfn[:], w_fnet.rearrange("g c d -> c g d")).then_inc(s_dft, 16)
            e.wait_ge(weights_used, BASE["out"])
            e.dma_start(tmp[:, 3, 0:GRID_W], na_mask).then_inc(s_dft, 16)
            for r in range(NA_ROWS):
                a0 = NA_KH - 1 - r
                src = rpb[:, :, a0:a0 + NA_ROWS, :].rearrange("w h a c -> w h (a c)")
                e.dma_start(bias[(r % 2) * GRID_W:(r % 2 + 1) * GRID_W, :, r // 2, :], src).then_inc(s_bias, 16)
            e.wait_ge(mod_sum, 2)
            e.dma_start(x[:], xT.rearrange("(t p) n -> p t n", p=P)).then_inc(x_again, 16)
            e.wait_ge(weights_used, BASE["gates"])
            e.dma_start(stick[:], stick_tab).then_inc(s_stick, 16)

        def squares(e, name, src, bank_free=None):
            t0, s0, idx, n = NORM[name]
            if name not in ("x", "ctx"):
                e.wait_ge(norm_lo, sum(NORM[q][3] for q in PAIRED if NORM[q][2] < idx))
            for s in range(n // 2):
                if s0 + s >= 2:
                    e.wait_ge(sq_used, s0 + s - 1)
                e.activation(tmp[:, 2 * ((s0 + s) % 2):2 * ((s0 + s) % 2) + 2, :], src(2 * s), ACT.Square)\
                    .then_inc(sq_ready, 1)
            e.wait_ge(sq_used, s0 + n // 2)
            if idx >= 1:
                e.wait_ge(rinv_ready, idx)
            e.activation(std[:], ps[:, STAT[name], 0:T], ACT.Sqrt, bias=vec("eps"), scale=1.0 / (n * P))\
                .then_inc(std_ready, 1)

        STAT = {"x": 2, "ctx": 3, "cq": 0, "ckv": 5, "ckvc": 6, "ffn": 0, "fin": 0, "mix2": 1, "ffn2": 0, "fin2": 0}

        def stats(e, name):
            t0, s0, idx, n = NORM[name]
            for s in range(n // 2):
                e.wait_ge(sq_ready, s0 + s + 1)
                for k in range(2):
                    last = e.matmul(ps[:, STAT[name], 0:T], ones, tmp[:, 2 * ((s0 + s) % 2) + k, :],
                                    start=(s == 0 and k == 0), stop=(s == n // 2 - 1 and k == 1))
                last.then_inc(sq_used, 1)

        SQ = {"x": 0, "ctx": 8, "ffn": 16, "fin": 24, "ffn2": 40, "fin2": 48}

        def square(e, n, src, scale=None):
            if n >= 2:
                e.wait_ge(sq_added, n - 1)
            if scale is None:
                e.activation(sq_slot[:, n % 2], src, ACT.Square).then_inc(sq_piece, 1)
            else:
                e.activation(sq_slot[:, n % 2, 0], src[:, 0], ACT.Square, scale=scale[:, 0:1])
                e.activation(sq_slot[:, n % 2, 1], src[:, 1], ACT.Square, scale=scale[:, 1:2]).then_inc(sq_piece, 1)

        def add_square(e, n, acc, first, apart=1):
            e.wait_ge(sq_piece, n + 1)
            if first:
                e.tensor_copy(acc, sq_slot[:, n % 2]).then_inc(sq_added, 1)
            else:
                e.wait_ge(sq_added, n + 1 - apart)
                e.tensor_tensor(acc, acc, sq_slot[:, n % 2], ALU.add).then_inc(sq_added, 1)

        def sum_squares(e, n, acc, bank):
            e.wait_ge(sq_added, n)
            for k in range(2):
                m = e.matmul(ps[:, bank, 0:T], ones, acc[:, k, :], start=(k == 0), stop=(k == 1))
            m.then_inc(sq_sum, 1)

        def root(e, name):
            t0, s0, idx, n = NORM[name]
            e.wait_ge(sq_sum, {"x": 1, "ctx": 2, "ffn": 3, "fin": 4, "ffn2": 6, "fin2": 7}[name])
            if idx >= 1:
                e.wait_ge(rinv_ready, idx)
            e.activation(std[:], ps[:, STAT[name], 0:T], ACT.Sqrt, bias=vec("eps"), scale=1.0 / (n * P))\
                .then_inc(std_ready, 1)

        def inv_rms(e, name, slot=0):
            idx = NORM[name][2]
            e.wait_ge(std_ready, idx + 1)
            e.reciprocal(rinv[:, slot, :], std[:]).then_inc(rinv_ready, 1)
            e.wait_ge(rinv_ready, idx + 1)

        def norm_scale(e, name, t, src, g, slot=0, out=None):
            n = NORM[name][0] + t
            if out is None:
                out = tmp[:, t % 4, :]
            e.scalar_tensor_tensor(out=out, in0=src, scalar=g, in1=rinv[:, slot, :], op0=ALU.mult, op1=ALU.mult)\
                .then_inc(scaled, 1)

        PAIRED = {}
        _n = 0
        for _s in ("x", "ctx", "cq", "ckv", "ckvc", "ffn", "mix2", "ffn2"):
            PAIRED[_s] = _n
            _n += NORM[_s][3]

        def norm_hi_part(e, name, dst, shift=None):
            for t in range(NORM[name][3]):
                e.wait_ge(scaled, NORM[name][0] + t + 1)
                b = 0.0 if shift is None else shift(t)
                e.activation(dst(t)[:, 0, :], tmp[:, t % 4, :], ACT.Copy if shift is None else ACT.Identity, bias=b)\
                    .then_inc(norm_hi, 1)

        def norm_lo_part(e, name, t, dst, shift=None):
            e.wait_ge(norm_hi, PAIRED[name] + t + 1)
            h = dst(t)[:, 0, :].bitcast(F32)
            if shift is None:
                e.tensor_tensor(dst(t)[:, 1, :], tmp[:, t % 4, :], h, ALU.subtract).then_inc(norm_lo, 1)
            else:
                e.scalar_tensor_tensor(out=dst(t)[:, 1, :], in0=tmp[:, t % 4, :], scalar=shift(t), in1=h,
                                       op0=ALU.add, op1=ALU.subtract).then_inc(norm_lo, 1)

        def norm_apply(e, name, src, g, dst, shift=None, slot=0, after=None):
            n = NORM[name][3]
            for t in range(n + 2):
                if t < n:
                    if t >= 4:
                        e.wait_ge(norm_lo, PAIRED[name] + t - 3)
                    norm_scale(e, name, t, src(t), g(t), slot)
                if t >= 2:
                    norm_lo_part(e, name, t - 2, dst, shift)
                if after is not None:
                    after(t)

        SH1, SC1, GT1, SH2, SC2, GT2 = (KT * i for i in range(6))

        def modv(which, off, t, n=1):
            return mod[:, which, off + t:off + t + n]

        SRC = {
            "x": (lambda t: x[:, t, :], lambda t: gain[:, 0, t:t + 1], lambda t: pair[:, t], lambda t: modv(0, SH1, t)),
            "ctx": (lambda t: ctx_x[:, t, :], lambda t: gain[:, 1, t:t + 1], lambda t: ctxpair[:, t],
                    lambda t: modv(1, SH1, t)),
            "cq": (lambda t: cq[:, t, :], lambda t: vec("g_q", t), lambda t: cqn[:, t], None),
            "ckv": (lambda t: ckv[:, t, 0, :], lambda t: vec("g_kv", t), lambda t: ckvn[:, 0, t], None),
            "ckvc": (lambda t: ckv[:, t, 1, :], lambda t: vec("g_kv", t), lambda t: ckvn[:, 1, t], None),
            "ffn": (lambda t: x[:, t, :], lambda t: gain[:, 2, t:t + 1], lambda t: pair[:, t], lambda t: modv(0, SH2, t)),
            "mix2": (lambda t: x[:, t, :], lambda t: vec("g_mix2", t), lambda t: pair[:, t], None),
            "ffn2": (lambda t: x[:, t, :], lambda t: vec("g_ffn2", t), lambda t: pair[:, t], None),
        }

        def sq_src(v):
            return lambda t: v[:, t:t + 2, :]

        RES = {"out": 0, "down": 16, "out2": 32, "down2": 48}

        @block.scalar
        def _(e):
            e.wait_ge(s_vecs, 16)
            for v, name in enumerate(("c", "c_ctx")):
                e.activation(csil[:, :, v], vec(name, 0, KT), ACT.Silu).then_inc(silu_c, 1)
            e.wait_ge(silu_c, 2)
            e.activation(csplit[:, :, 0:2], csil[:], ACT.Copy).then_inc(csplit_hi, 1)
            split_hi(e, 0, LEAD)
            for g in range(8):
                split_hi(e, LEAD + g * CPG, LEAD + (g + 1) * CPG)
                e.wait_ge(weights_used, (g + 1) * CPG)
                if g >= 2:
                    e.wait_ge(mod_turned, g - 1)
                e.activation(mrows[0:4, g % 2, :], ps[0:4, g % 2, :], ACT.Copy).then_inc(mod_rows, 1)
                if g == 0:
                    e.wait_ge(s_x, 16)
                    for s in range(8):
                        square(e, SQ["x"] + s, x[:, 2 * s:2 * s + 2, :])
                    root(e, "x")
                if g == 2:
                    e.wait_ge(s_ctx, 16)
                    for s in range(8):
                        square(e, SQ["ctx"] + s, ctx_x[:, 2 * s:2 * s + 2, :])
                    root(e, "ctx")
            norm_hi_part(e, "x", SRC["x"][2], SRC["x"][3])
            e_ctx = NORM["ctx"][0]
            for i in range(CPG):
                split_hi(e, BASE["cq"] + LEAD + i, BASE["cq"] + LEAD + i + 1)
                for t in (2 * i, 2 * i + 1):
                    e.wait_ge(scaled, e_ctx + t + 1)
                    e.activation(ctxpair[:, t, 0, :], tmp[:, t % 4, :], ACT.Identity, bias=modv(1, SH1, t))\
                        .then_inc(norm_hi, 1)

            def upto(a, stage, n):
                b = BASE[stage] + n + LEAD
                split_hi(e, a, b)
                return b

            at = BASE["cq"] + LEAD + CPG
            at = upto(at, "ckv", CPG)
            e.wait_ge(sums_ready, SUMS["cq"] + 4)
            squares(e, "cq", sq_src(cq))
            norm_hi_part(e, "cq", SRC["cq"][2])
            at = upto(at, "kr", 2)
            at = upto(at, "qn", CPG)
            e.wait_ge(sums_ready, SUMS["ckv"] + 8)
            squares(e, "ckv", lambda t: ckv[:, t:t + 2, 0, :])
            norm_hi_part(e, "ckv", SRC["ckv"][2])
            squares(e, "ckvc", lambda t: ckv[:, t:t + 2, 1, :])
            norm_hi_part(e, "ckvc", SRC["ckvc"][2])
            at = upto(at, "kn", CPG)
            at = upto(at, "vn", CPG)
            e.wait_ge(weights_used, BASE["vn"] + CPG)
            for tt in range(4):
                e.activation(vn[:, tt, :], ps[:, 4 + tt, :], ACT.Copy).then_inc(rows_copied, 1)
            at = upto(at, "f", CPG)
            e.wait_ge(weights_used, BASE["f"] + CPG)
            for tt in range(2):
                e.activation(f_sb[:, tt, :], ps[:, tt, :], ACT.Copy).then_inc(rows_copied, 1)
            at = upto(at, "uq", 8)
            for g in range(FN_G):
                e.wait_ge(uv_done, g + 1)
                e.activation(uv[:, g, :], ps[:, 4 + g, :], ACT.Copy).then_inc(uv_copied, 1)
            for g in range(FN_G):
                e.wait_ge(fn_done, g + 1)
                e.activation(pair[:, HEADS + g, 0, :], ps[:, 4 + g, 0:T], ACT.Copy).then_inc(o_hi, 1)
            for g in range(4):
                at = upto(at, "ukv", 2 * (g + 1))
                e.wait_ge(weights_used, BASE["ukv"] + 2 * (g + 1))
                for tt in range(4):
                    e.activation(v_sb[:, tt, g * 2 * VD:(g + 1) * 2 * VD], ps[:, 4 + tt, 0:2 * VD], ACT.Copy)\
                        .then_inc(rows_copied, 1)
            for i in range(HEADS + 2):
                if 1 <= i <= HEADS:
                    h = i - 1
                    for t in range(2):
                        e.wait_ge(flipped, 2 * h + t + 1)
                        if h >= 2:
                            e.wait_ge(mixed, h - 1)
                        e.activation(probT[:, h % 2, :, t * P:(t + 1) * P],
                                     ps[:, 4 + t, :].rearrange("p (k q) -> p k q", k=4), ACT.Copy)\
                            .then_inc(flips_copied, 1)
                if i < HEADS:
                    for t in range(2):
                        n = 2 * i + t
                        e.wait_ge(negmax, n + 1)
                        if i >= 2:
                            e.wait_ge(flipped, n - 3)
                        src = ps[:, 2 * (i % 2) + t, :] if i < MLA_H else prob[:, i % 2, t, :]
                        e.activation(prob[:, i % 2, t, :], src, ACT.Exp, bias=small[:, 24 + n:25 + n],
                                     scale=MLA_SCALE if i < MLA_H else 1.0,
                                     accum_out=small[:, 48 + n:49 + n]).then_inc(exps, 1)
                if i >= 2:
                    h = i - 2
                    e.wait_ge(mixed, h + 1)
                    e.activation(pair[:, h, 0, :], ps[:, 6 + h % 2, 0:T], ACT.Copy).then_inc(o_hi, 1)
            for g in range(4):
                at = upto(at, "out", min((g + 1) * CPG + CPG, 4 * CPG))
                for i in range(2):
                    e.wait_ge(resid, RES["out"] + 4 * g + 2 * i + 2)
                    square(e, SQ["ffn"] + 2 * g + i, x[:, 4 * g + 2 * i:4 * g + 2 * i + 2, :])
            root(e, "ffn")
            norm_hi_part(e, "ffn", SRC["ffn"][2], SRC["ffn"][3])

            def ffn(s_up, s_down, n_ffn, conv):
                b = BASE[s_up]
                split_hi(e, b + LEAD, b + LEAD + CPG)
                with e.Fori(0, 11) as j:
                    def centre_tap(group, buf, m):
                        e.activation(buf[:, m, :], tmp[:, m, :], ACT.Identity,
                                     bias=vec("conv_b", FT * group + m, 1, j, 4),
                                     scale=vec("conv_w", 2 * FT + FT * group + m, 1, j, 4)).then_inc(centre, 1)

                    def hidden(m):
                        e.wait_ge(prod, plus(44 * n_ffn + m + 1, j, 4))
                        e.activation(hid[:, bass.ds(j * 4 + m, 1), 0, :].rearrange("p a t -> p (a t)"), val[:, m, :],
                                     ACT.Copy).then_inc(hid_hi, 1)

                    for m in range(4):
                        c = b + LEAD + CPG + 2 * m
                        split_hi(e, c, c + 2, j, 2 * CPG)
                        e.wait_ge(sums_ready, plus(SUMS[s_up] + m + 1, j, 8))
                        if conv:
                            centre_tap(0, gate, m)
                        else:
                            e.activation(gate[:, m, :], tmp[:, m, :], ACT.Silu).then_inc(silu_done, 1)
                    for m in range(4):
                        c = b + LEAD + 2 * CPG + 2 * m
                        split_hi(e, c, c + 2, j, 2 * CPG)
                        if conv:
                            e.wait_ge(sides, plus(2 * m + 2, j, 16))
                            e.activation(gate[:, m, :], gate[:, m, :], ACT.Silu).then_inc(silu_done, 1)
                            e.wait_ge(sums_ready, plus(SUMS[s_up] + 4 + m + 1, j, 8))
                            centre_tap(1, val, m)
                        if m >= 2:
                            hidden(m - 2)
                    hidden(2)
                    hidden(3)

            def resid_squares(stage, g, n):
                for i in range(2):
                    e.wait_ge(resid, RES[stage] + 4 * g + 2 * i + 2)
                    square(e, n + 2 * g + i, x[:, 4 * g + 2 * i:4 * g + 2 * i + 2, :])

            def down_splits(stage, norm):
                at = BASE[stage] + LEAD + CPG
                end = BASE[stage] + 4 * (FT // 2) + LEAD
                for g in range(4):
                    e_g = BASE[stage] + (g + 1) * (FT // 2) + LEAD
                    to = min(e_g + CPG, end)
                    split_hi(e, at, to)
                    at = to
                    if norm != "fin":
                        resid_squares(stage, g, SQ[norm] )
                        continue
                    for i in range(2):
                        e.wait_ge(resid, RES[stage] + 4 * g + 2 * i + 2)
                        t = 4 * g + 2 * i
                        square(e, SQ[norm] + 2 * (2 * g + i), x[:, t:t + 2, :])
                        square(e, SQ[norm] + 2 * (2 * g + i) + 1, x[:, t:t + 2, :], vec("g_final", t, 2))

            ffn("up", "down", 0, True)
            down_splits("down", "fin")
            root(e, "fin")
            e.wait_ge(mix_ms, 2)
            e.activation(std[:], rinv[:, 1, :], ACT.Sqrt, bias=vec("eps")).then_inc(std_ready, 1)
            norm_hi_part(e, "mix2", SRC["mix2"][2])
            for g in range(2):
                b = BASE["qa"] + g * CPG + LEAD
                split_hi(e, b, b + CPG)
                for m in range(4):
                    e.wait_ge(sums_ready, SUMS["qa"] + 4 * g + m + 1)
                    e.activation(qa[:, 4 * g + m, :], tmp[:, m, :], ACT.Copy, scale=HD ** -0.5).then_inc(tmp_read, 1)
            b = BASE["kva"] + LEAD
            split_hi(e, b, b + CPG)
            e.wait_ge(weights_used, BASE["kva"] + CPG)
            for tt in range(2):
                e.activation(va[:, tt, :], ps[:, 2 + tt, 0:A_KV * HD], ACT.Copy).then_inc(rows_copied, 1)
            b = BASE["qkb"] + LEAD
            with e.Fori(0, 2) as j:
                split_hi(e, b, b + 2 * CPG, j, 2 * CPG)
            e.wait_ge(sums_ready, SUMS["qkb"] + 16)
            e.activation(qkb[:, 0:PAIRS, :], qkb[:, 0:PAIRS, :], ACT.Copy, scale=HD ** -0.5).then_inc(qb_scaled, 1)
            for g in range(2):
                b = BASE["vb"] + g * CPG + LEAD
                split_hi(e, b, b + CPG)
                e.wait_ge(weights_used, BASE["vb"] + (g + 1) * CPG)
                for tt in range(2):
                    e.activation(vb[:, tt, g * GW:(g + 1) * GW], ps[:, 4 * g + tt, :], ACT.Copy).then_inc(rows_copied, 1)
            b = BASE["gates"] + LEAD
            with e.Fori(0, 4) as j:
                for g in range(2):
                    split_hi(e, b + g * CPG, b + (g + 1) * CPG, j, 2 * CPG)
                    for m in range(4):
                        e.wait_ge(sums_ready, plus(SUMS["gates"] + 4 * g + m + 1, j, 8))
                        e.activation(gates[:, bass.ds(j * 8 + 4 * g + m, 1), :].rearrange("p a t -> p (a t)"),
                                     tmp[:, m, :], ACT.Sigmoid).then_inc(tmp_read, 1)
            e.wait_ge(tmp_read, 8 + 2 * KT)
            e.dma_start(dist[:], dist_tab).then_inc(s_dist, 16)
            for i in range(PAIRS + 2):
                if i < PAIRS:
                    e.wait_ge(sb_zb, i + 1)
                    if i >= 1:
                        e.wait_ge(sb_sp, i)
                    e.activation(lnb[:], zb[:, i % 3], ACT.Abs).then_inc(sb_step, 1)
                    e.wait_ge(sb_step, 2 * i + 1)
                    e.activation(lnb[:], lnb[:], ACT.Exp, scale=-1.0).then_inc(sb_step, 1)
                    e.wait_ge(sb_step, 2 * i + 2)
                    e.activation(lnb[:], lnb[:], ACT.Ln, bias=1.0).then_inc(sb_ln, 1)
                if 1 <= i <= PAIRS:
                    n = i - 1
                    e.wait_ge(sw_flip, i)
                    if n >= 2:
                        e.wait_ge(mixed2, 4 * (n - 1))
                    e.activation(saT[:, n % 2], ps[:, 0:2, 0:W3], ACT.Copy).then_inc(sw_flipc, 1)
                    e.wait_ge(sb_d, i)
                    e.activation(zb[:, n % 3], zb[:, n % 3], ACT.Exp).then_inc(sb_a, 1)
                if i < PAIRS:
                    e.wait_ge(sw_neg, 2 * (i + 1))
                    o = 4 * i
                    e.activation(small[:, 128:132], small[:, 132:136], ACT.Exp).then_inc(sw_exps, 1)
                    for h in range(2):
                        for b_ in range(2):
                            q = slice(0, P) if b_ == 0 else slice(P, W3)
                            k = 2 * h + b_
                            e.activation(sa[:, i % 2, h, q], sa[:, i % 2, h, q], ACT.Exp,
                                         bias=small[:, 136 + k:137 + k],
                                         accum_out=small[:, 140 + k:141 + k]).then_inc(sw_exps, 1)
                if i >= 2:
                    n = i - 2
                    for br in range(2):
                        e.wait_ge(mixed2, 2 * (2 * n + br + 1))
                        e.activation(pair[:, 8 * br + n, 0, :], ps[:, 6 + br, 0:T], ACT.Copy)\
                            .then_inc(o2_hi, 1)
            for g in range(4):
                b = BASE["bra"] + g * 4 + LEAD
                split_hi(e, b, b + 4)
            for g in range(4):
                b = BASE["brb"] + g * 4 + LEAD
                split_hi(e, b, b + 4)
                for m in range(4):
                    t = 4 * g + m
                    e.wait_ge(merged, t + 1)
                    e.activation(pair2[:, t, 0, :], gates[:, t, :], ACT.Copy).then_inc(m_hi, 1)
            at = BASE["out2"] + LEAD
            for g in range(4):
                at = upto(at, "out2", min((g + 2) * CPG, 4 * CPG))
                resid_squares("out2", g, SQ["ffn2"])
            root(e, "ffn2")
            norm_hi_part(e, "ffn2", SRC["ffn2"][2])
            ffn("up2", "down2", 1, False)
            down_splits("down2", "fin2")
            root(e, "fin2")

        @block.vector
        def _(e):
            e.wait_ge(s_vecs, 16)
            e.wait_ge(csplit_hi, 1)
            e.tensor_tensor(csplit[:, :, 2:4], csil[:], csplit[:, :, 0:2].bitcast(F32), ALU.subtract)\
                .then_inc(csplit_lo, 1)
            split_lo(e, 0, LEAD)
            for g in range(8):
                split_lo(e, LEAD + g * CPG + (4 if g else 0), LEAD + (g + 1) * CPG)
                if g in (0, 2):
                    name = "x" if g == 0 else "ctx"
                    for s in range(8):
                        add_square(e, SQ[name] + s, tmp[:, 0:2, :], s == 0)
                    inv_rms(e, name, g // 2)
                if g < 7:
                    split_lo(e, LEAD + (g + 1) * CPG, LEAD + (g + 1) * CPG + 4)
                e.wait_ge(mod_turned, g + 1)
                o = (KT + 4 * g) % (2 * KT)
                e.tensor_tensor(mod[:, :, o:o + 4], ps[:, 4 + g % 2, 0:8].rearrange("p (m v) -> p v m", v=2),
                                vec("b_mod", o, 4).unsqueeze(1).to_broadcast([P, 2, 4]), ALU.add)\
                    .then_inc(mod_ready, 1)
                if g == 3:
                    e.wait_ge(mod_ready, 4)
                    for w in range(2):
                        e.scalar_tensor_tensor(out=gain[:, w, :], in0=mod[:, w, SC1:SC1 + KT], scalar=1.0,
                                               in1=vec("g_attn", 0, KT), op0=ALU.add, op1=ALU.mult)\
                            .then_inc(gain_ready, 1)
            e.wait_ge(mod_ready, 8)
            e.wait_ge(gain_ready, 2)
            src, g_, dst, shift = SRC["x"]
            norm_apply(e, "x", src, g_, dst, shift)
            src, g_, dst, shift = SRC["ctx"]
            for i in range(CPG):
                split_lo(e, BASE["cq"] + LEAD + i, BASE["cq"] + LEAD + i + 1)
                for t in (2 * i, 2 * i + 1):
                    e.wait_ge(norm_lo, PAIRED["ctx"] + t - 3)
                    norm_scale(e, "ctx", t, src(t), g_(t), 1)
                for t in (2 * i, 2 * i + 1):
                    norm_lo_part(e, "ctx", t, dst, shift)

            def upto(a, stage, n):
                b = BASE[stage] + n + LEAD
                split_lo(e, a, b)
                return b

            def sum_out(bank, out):
                e.tensor_reduce(out, ps[:, bank, :].rearrange("p (s t) -> p t s", s=2), AX_X, ALU.add)\
                    .then_inc(sums_ready, 1)

            at = BASE["cq"] + LEAD + CPG
            e.wait_ge(weights_used, BASE["cq"] + CPG)
            for m in range(4):
                sum_out(m, cq[:, m, :])
            at = upto(at, "ckv", CPG)
            e.wait_ge(weights_used, BASE["ckv"] + CPG)
            for s in range(2):
                for m in range(4):
                    sum_out(4 * (1 - s) + m, ckv[:, m, s, :])
            inv_rms(e, "cq")
            norm_apply(e, "cq", SRC["cq"][0], SRC["cq"][1], SRC["cq"][2])
            at = upto(at, "kr", 2)
            e.wait_ge(weights_used, BASE["kr"] + 2)
            e.wait_ge(s_tabs, 32)
            e.wait_ge(zeroed, 2)
            sum_out(4, rinv[:, 1, :])
            sum_out(7, qn[:, 0, :])
            e.wait_ge(sums_ready, SUMS["kr"] + 2)
            e.tensor_copy(kre[0:64, 1, :], qn[0:64, 0, :]).then_inc(roped, 1)
            e.tensor_copy(kro[64:P, 1, :], qn[64:P, 0, :]).then_inc(roped, 1)
            at = upto(at, "qn", CPG)
            e.wait_ge(turned, 1)
            e.tensor_tensor(qn[:, 1, :], rinv[:, 1, :], cos, ALU.mult).then_inc(rope_mul, 1)
            e.tensor_tensor(qn[:, 2, :], ps[:, 7, 0:T], sin, ALU.mult).then_inc(rope_mul, 1)
            e.wait_ge(rope_mul, 2)
            e.tensor_tensor(kre[0:64, 0, :], qn[0:64, 1, :], qn[0:64, 2, :], ALU.add).then_inc(roped, 1)
            e.tensor_tensor(kro[64:P, 0, :], qn[64:P, 1, :], qn[64:P, 2, :], ALU.add).then_inc(roped, 1)
            e.wait_ge(roped, 4)
            e.wait_ge(weights_used, BASE["qn"] + CPG)
            for m in range(4):
                sum_out(m, qn[:, m, :])
            for name in ("ckv", "ckvc"):
                inv_rms(e, name)
                norm_apply(e, name, SRC[name][0], SRC[name][1], SRC[name][2])
            at = upto(at, "kn", CPG)
            e.wait_ge(weights_used, BASE["kn"] + CPG)
            for s in range(2):
                for m in range(4):
                    sum_out(4 * (1 - s) + m, kn[:, m, s, :])
            at = upto(at, "vn", CPG)
            at = upto(at, "f", CPG)
            for g in range(4):
                at = upto(at, "uq", 2 * (g + 1))
                e.wait_ge(weights_used, BASE["uq"] + 2 * (g + 1))
                b = 4 * (g % 2)
                sum_out(b, qnope[:, 2 * g, :])
                sum_out(b + 1, qnope[:, 2 * g + 1, :])
                sum_out(b + 2, qrope[:, g, :])
            late_bias(e, 1, 0, 8, 3)
            for g in range(4):
                e.wait_ge(turned, 2 + g)
                if g >= 2:
                    e.wait_ge(roped, 4 + 2 * (g - 1))
                e.tensor_tensor(tmp[:, g % 2, :], ps[:, g, 0:T], sin, ALU.mult).then_inc(rope_mul, 1)
                e.tensor_tensor(qrope[:, g, :], qrope[:, g, :], cos, ALU.mult).then_inc(roped, 1)
                e.wait_ge(rope_mul, 3 + g)
                e.wait_ge(roped, 5 + 2 * g)
                e.tensor_tensor(qrope[:, g, :], qrope[:, g, :], tmp[:, g % 2, :], ALU.add).then_inc(roped, 1)
            for g in range(FN_G):
                e.wait_ge(spec_done, g + 1)
                e.tensor_copy(spec[:, g, :], ps[:, g, 0:T]).then_inc(spec_copied, 1)
            for g in range(FN_G):
                e.wait_ge(o_hi, g + 1)
                e.tensor_tensor(pair[:, HEADS + g, 1, :], ps[:, 4 + g, 0:T], pair[:, HEADS + g, 0, :].bitcast(F32),
                                ALU.subtract).then_inc(o_lo, 1)
            for g in range(4):
                at = upto(at, "ukv", 2 * (g + 1))
                e.wait_ge(weights_used, BASE["ukv"] + 2 * (g + 1))
                for m in range(2):
                    for s in range(2):
                        sum_out(2 * m + s, knope[:, 2 * g + m, s, :])
            for i in range(HEADS + 2):
                if i == 1:
                    e.wait_ge(s_bias, 16 * NA_ROWS)
                    e.wait_ge(s_dft, 48)
                    for h in range(NA_H):
                        v = bias[:, h].rearrange("p t (a c) -> p (t a) c", c=GRID_W)
                        mk = tmp[:, 3, 0:GRID_W].unsqueeze(1).to_broadcast([P, 2 * NA_ROWS, GRID_W])
                        e.tensor_tensor(v, v, mk, ALU.add).then_inc(bias_masked, 1)
                if i < HEADS:
                    for t in range(2):
                        n = 2 * i + t
                        e.wait_ge(scores, n + 1)
                        if i >= MLA_H:
                            if i == MLA_H and t == 0:
                                e.wait_ge(bias_masked, NA_H)
                            e.wait_ge(flipped, n - 3)
                            pb, bk = prob[:, i % 2, t, :], ps[:, 2 * (i % 2) + t, :]
                            e.scalar_tensor_tensor(out=pb[:, 0:T], in0=bk[:, 0:T], scalar=NA_SCALE,
                                                   in1=bias[:, i - MLA_H, t, :], op0=ALU.mult, op1=ALU.add)\
                                .then_inc(biased, 1)
                            e.tensor_scalar(pb[:, T:2 * T], bk[:, T:2 * T], NA_SCALE, None, ALU.mult).then_inc(biased, 1)
                            e.wait_ge(biased, 2 * (n - 2 * MLA_H + 1))
                            e.tensor_reduce(small[:, n:n + 1], pb, AX_X, ALU.max).then_inc(maxed, 1)
                        else:
                            e.tensor_reduce(small[:, n:n + 1], ps[:, 2 * (i % 2) + t, :], AX_X, ALU.max)\
                                .then_inc(maxed, 1)
                        e.wait_ge(maxed, n + 1)
                        e.tensor_scalar(small[:, 24 + n:25 + n], small[:, n:n + 1],
                                        -(MLA_SCALE if i < MLA_H else 1.0), None, ALU.mult).then_inc(negmax, 1)
                if i >= 2:
                    h = i - 2
                    e.wait_ge(o_hi, FN_G + h + 1)
                    e.tensor_tensor(pair[:, h, 1, :], ps[:, 6 + h % 2, 0:T], pair[:, h, 0, :].bitcast(F32),
                                    ALU.subtract).then_inc(o_lo, 1)
                if i < HEADS:
                    for t in range(2):
                        n = 2 * i + t
                        e.wait_ge(exps, n + 1)
                        e.reciprocal(small[:, 72 + n:73 + n], small[:, 48 + n:49 + n]).then_inc(recips, 1)
                        e.wait_ge(recips, n + 1)
                        pb = prob[:, i % 2, t, :]
                        e.tensor_scalar(pb, pb, small[:, 72 + n:73 + n], None, ALU.mult).then_inc(probs, 1)
                if i < 8:
                    accumulate(e, 80 + 2 * i, 82 + 2 * i)
            late_bias(e, 2, 8, 12, 2)
            e.wait_ge(late_mod, 2)
            e.scalar_tensor_tensor(out=gain[:, 2, :], in0=mod[:, 0, SC2:SC2 + KT], scalar=1.0,
                                   in1=vec("g_ffn", 0, KT), op0=ALU.add, op1=ALU.mult).then_inc(gain_ready, 1)
            e.wait_ge(gain_ready, 3)

            def residual(stage, g, gt, it=None, per_t=0, tiles=range(4)):
                for m in tiles:
                    t = 4 * g + m
                    if it is None:
                        xt = x[:, t, :]
                        gv = None if gt is None else modv(0, gt, t)
                    else:
                        xt = x[:, bass.ds(it * per_t + t, 1), :].rearrange("p a t -> p (a t)")
                        gv = None if gt is None else mod[:, 0, bass.ds(it * per_t + gt + t, 1)]
                    e.wait_ge(sums_ready, plus(SUMS[stage] + t + 1, it, per_t))
                    e.scalar_tensor_tensor(out=xt, in0=tmp[:, m, :], scalar=1.0 if gv is None else gv, in1=xt,
                                           op0=ALU.mult, op1=ALU.add).then_inc(resid, 1)

            def onto_x(at, stage, size, gt, end, squared):
                b = BASE[stage]
                for g in range(4):
                    split_lo(e, at, b + (g + 1) * size + LEAD)
                    at = max(at, b + (g + 1) * size + LEAD)
                    e.wait_ge(weights_used, b + (g + 1) * size)
                    if stage == "out" and g == 0:
                        e.wait_ge(x_again, 16)
                    for m in range(4):
                        if g:
                            e.wait_ge(resid, RES[stage] + 4 * (g - 1) + m + 1)
                        sum_out(4 * (g % 2) + m, tmp[:, m, :])
                        if m:
                            residual(stage, g, gt, tiles=[m - 1])
                        split_lo(e, at, min(at + 2, end))
                        at = min(at + 2, end)
                    residual(stage, g, gt, tiles=[3])
                    squared(g)
                return at

            def squared(name):
                def add(g):
                    for i in range(2):
                        add_square(e, SQ[name] + 2 * g + i, sq_acc[:, 0], g == 0 and i == 0)
                return add

            at = onto_x(at, "out", CPG, GT1, BASE["up"] + LEAD, squared("ffn"))
            late_bias(e, 3, 12, 16, 2)
            e.wait_ge(late_mod, 3)
            inv_rms(e, "ffn")
            norm_apply(e, "ffn", *SRC["ffn"])

            def ffn(s_up, s_down, n_ffn, conv, gt, then):
                b, u = BASE[s_up], SUMS[s_up]
                split_lo(e, b + LEAD, b + LEAD + CPG)
                with e.Fori(0, 11) as j:
                    def taps(group, buf, m):
                        e.wait_ge(centre, plus(4 * group + m + 1, j, 8))
                        e.scalar_tensor_tensor(out=buf[:, m, 1:T], in0=tmp[:, m, 0:T - 1],
                                               scalar=vec("conv_w", FT * group + m, 1, j, 4),
                                               in1=buf[:, m, 1:T], op0=ALU.mult, op1=ALU.add).then_inc(sides, 1)
                        e.wait_ge(sides, plus(8 * group + 2 * m + 1, j, 16))
                        e.scalar_tensor_tensor(out=buf[:, m, 0:T - 1], in0=tmp[:, m, 1:T],
                                               scalar=vec("conv_w", 4 * FT + FT * group + m, 1, j, 4),
                                               in1=buf[:, m, 0:T - 1], op0=ALU.mult, op1=ALU.add)\
                            .then_inc(sides, 1)

                    def product(m):
                        if conv:
                            taps(1, val, m)
                            e.wait_ge(sides, plus(8 + 2 * m + 2, j, 16))
                            e.wait_ge(silu_done, plus(m + 1, j, 4))
                        else:
                            e.wait_ge(sums_ready, plus(u + 4 + m + 1, j, 8))
                        e.tensor_tensor(val[:, m, :], val[:, m, :] if conv else tmp[:, m, :], gate[:, m, :],
                                        ALU.mult).then_inc(prod, 1)

                    def hidden_low(m):
                        e.wait_ge(hid_hi, plus(44 * n_ffn + m + 1, j, 4))
                        hv = hid[:, bass.ds(j * 4 + m, 1), :, :].rearrange("p a s t -> p (a s) t")
                        e.tensor_tensor(hv[:, 1, :], val[:, m, :], hv[:, 0, :].bitcast(F32), ALU.subtract)\
                            .then_inc(hid_lo, 1)

                    e.wait_ge(weights_used, plus(b + CPG, j, 2 * CPG))
                    for m in range(4):
                        sum_out(m, tmp[:, m, :])
                        if conv and m:
                            taps(0, gate, m - 1)
                        c = b + LEAD + CPG + 2 * m
                        split_lo(e, c, c + 2, j, 2 * CPG)
                    if conv:
                        taps(0, gate, 3)
                        e.wait_ge(sides, plus(8, j, 16))
                    e.wait_ge(weights_used, plus(b + 2 * CPG, j, 2 * CPG))
                    for m in range(4):
                        if not conv:
                            e.wait_ge(silu_done, plus(44 * n_ffn + m + 1, j, 4))
                        sum_out(4 + m, tmp[:, m, :])
                        if m:
                            product(m - 1)
                        if m == 3:
                            hidden_low(0)
                        c = b + LEAD + 2 * CPG + 2 * m
                        split_lo(e, c, c + 2, j, 2 * CPG)
                    product(3)
                    for m in (1, 2, 3):
                        hidden_low(m)
                onto_x(BASE[s_down] + LEAD + CPG, s_down, FT // 2, gt, BASE[s_down] + 4 * (FT // 2) + LEAD, then)

            def squared_twice(g):
                for i in range(4):
                    add_square(e, SQ["fin"] + 4 * g + i, sq_acc[:, i % 2], g == 0 and i < 2, 2)

            ffn("up", "down", 0, True, GT2, squared_twice)
            inv_rms(e, "fin")
            e.tensor_tensor(rinv[:, 1, :], rinv[:, 0, :], rinv[:, 0, :], ALU.mult).then_inc(mix_ms, 1)
            e.wait_ge(mix_ms, 1)
            e.wait_ge(sq_sum, 5)
            e.scalar_tensor_tensor(out=rinv[:, 1, :], in0=ps[:, STAT["mix2"], 0:T], scalar=1.0 / D, in1=rinv[:, 1, :],
                                   op0=ALU.mult, op1=ALU.mult).then_inc(mix_ms, 1)

            def block1_out(t):
                e.scalar_tensor_tensor(out=x[:, t, :], in0=x[:, t, :], scalar=vec("g_final", t), in1=rinv[:, 0, :],
                                       op0=ALU.mult, op1=ALU.mult).then_inc(x_between, 1)
            for t in range(4):
                block1_out(t)
            inv_rms(e, "mix2", 1)
            for t in range(KT + 2):
                if t + 4 < KT:
                    block1_out(t + 4)
                if t < KT:
                    if t >= 4:
                        e.wait_ge(norm_lo, PAIRED["mix2"] + t - 3)
                    e.wait_ge(x_between, t + 1)
                    norm_scale(e, "mix2", t, x[:, t, :], vec("g_mix2", t), 1)
                if t >= 2:
                    norm_lo_part(e, "mix2", t - 2, SRC["mix2"][2])
            for g in range(2):
                b = BASE["qa"] + g * CPG + LEAD
                split_lo(e, b, b + CPG)
                e.wait_ge(weights_used, BASE["qa"] + (g + 1) * CPG)
                if g:
                    e.wait_ge(tmp_read, 4)
                for m in range(4):
                    sum_out(4 * g + m, tmp[:, m, :])
            b = BASE["kva"] + LEAD
            split_lo(e, b, b + CPG)
            e.wait_ge(weights_used, BASE["kva"] + CPG)
            for m in range(2):
                sum_out(m, ka[:, m, :])
            b = BASE["qkb"]
            with e.Fori(0, 2) as j:
                for g in range(2):
                    split_lo(e, b + LEAD + g * CPG, b + LEAD + (g + 1) * CPG, j, 2 * CPG)
                    e.wait_ge(weights_used, plus(b + (g + 1) * CPG, j, 2 * CPG))
                    for m in range(4):
                        sum_out(4 + m if g == 0 else m,
                                qkb[:, bass.ds(j * 8 + 4 * g + m, 1), :].rearrange("p a t -> p (a t)"))
            b = BASE["vb"] + LEAD
            split_lo(e, b, b + 2 * CPG)
            b = BASE["gates"]
            with e.Fori(0, 4) as j:
                for g in range(2):
                    split_lo(e, b + LEAD + g * CPG, b + LEAD + (g + 1) * CPG, j, 2 * CPG)
                    e.wait_ge(weights_used, plus(b + (g + 1) * CPG, j, 2 * CPG))
                    e.wait_ge(tmp_read, plus(8 + 4 * g, j, 8))
                    for m in range(4):
                        sum_out(4 * g + m, tmp[:, m, :])
            e.wait_ge(tmp_read, 8 + 2 * KT)
            e.wait_ge(s_dist, 16)
            e.wait_ge(s_stick, 16)
            for i in range(PAIRS + 2):
                if i < PAIRS:
                    e.wait_ge(sw_scores, 2 * (i + 1))
                    if i >= 2:
                        e.wait_ge(sw_flip, i - 1)
                    for h in range(2):
                        s = -SLOPES[2 * i + h]
                        o = sa[:, i % 2, h]
                        e.scalar_tensor_tensor(out=o[:, 0:P], in0=dist[:, P:2 * P], scalar=s, in1=ps[:, h, 0:P],
                                               op0=ALU.mult, op1=ALU.add).then_inc(sw_biased, 1)
                        e.scalar_tensor_tensor(out=o[:, P:W3], in0=dist[:], scalar=s, in1=ps[:, h, P:W3],
                                               op0=ALU.mult, op1=ALU.add).then_inc(sw_biased, 1)
                    e.wait_ge(sb_z, 2 * (i + 1))
                    if i >= 3:
                        e.wait_ge(mixed2, 4 * (i - 2))
                    mk = stick[:, 0:W3].unsqueeze(1).to_broadcast([P, 2, W3])
                    e.tensor_tensor(zb[:, i % 3], ps[:, 2:4, 0:W3], mk, ALU.add).then_inc(sb_zb, 1)
                if 1 <= i <= PAIRS:
                    n = i - 1
                    e.wait_ge(sb_suffix, i)
                    e.tensor_tensor(zb[:, n % 3], zb[:, n % 3], ps[:, 4:6, 0:W3], ALU.subtract).then_inc(sb_d, 1)
                if i < PAIRS:
                    e.wait_ge(sw_biased, 4 * (i + 1))
                    if i:
                        e.wait_ge(sw_probs, 4 * i)
                    mx = small[:, 144:148].rearrange("p (h b) -> p h b", b=2)
                    e.tensor_reduce(mx[:, :, 0], sa[:, i % 2, :, 0:P], AX_X, ALU.max).then_inc(sw_max, 1)
                    e.tensor_reduce(mx[:, :, 1], sa[:, i % 2, :, P:W3], AX_X, ALU.max).then_inc(sw_max, 1)
                    e.wait_ge(sw_max, 3 * i + 2)
                    sk = vec("sink", 4 * i, 4)
                    e.tensor_tensor(small[:, 144:148], small[:, 144:148], sk, ALU.max).then_inc(sw_max, 1)
                    e.wait_ge(sw_max, 3 * i + 3)
                    e.tensor_tensor(small[:, 132:136], sk, small[:, 144:148], ALU.subtract).then_inc(sw_neg, 1)
                    e.tensor_scalar(small[:, 136:140], small[:, 144:148], -1.0, None, ALU.mult).then_inc(sw_neg, 1)
                    e.wait_ge(sb_ln, i + 1)
                    if i >= 2:
                        e.wait_ge(sb_suffix, i - 1)
                    e.scalar_tensor_tensor(out=sp_[:, i % 2], in0=zb[:, i % 3], scalar=0.0, in1=lnb[:],
                                           op0=ALU.max, op1=ALU.add).then_inc(sb_sp, 1)
                    e.wait_ge(sw_exps, 5 * (i + 1))
                    e.tensor_tensor(small[:, 148:152], small[:, 140:144], small[:, 128:132], ALU.add).then_inc(sw_sum, 1)
                    e.wait_ge(sw_sum, 2 * i + 1)
                    e.reciprocal(small[:, 152:156], small[:, 148:152]).then_inc(sw_sum, 1)
                    e.wait_ge(sw_sum, 2 * i + 2)
                    for h in range(2):
                        for b_ in range(2):
                            q = slice(0, P) if b_ == 0 else slice(P, W3)
                            k = 2 * h + b_
                            e.tensor_scalar(sa[:, i % 2, h, q], sa[:, i % 2, h, q], small[:, 152 + k:153 + k], None,
                                            ALU.mult).then_inc(sw_probs, 1)
                if i >= 2:
                    n = i - 2
                    for br in range(2):
                        e.wait_ge(o2_hi, 2 * n + br + 1)
                        e.tensor_tensor(pair[:, 8 * br + n, 1, :], ps[:, 6 + br, 0:T],
                                        pair[:, 8 * br + n, 0, :].bitcast(F32), ALU.subtract).then_inc(o2_lo, 1)
            for br, stage in enumerate(("bra", "brb")):
                for g in range(4):
                    b = BASE[stage] + g * 4
                    split_lo(e, b + LEAD, b + LEAD + 4)
                    e.wait_ge(weights_used, b + 4)
                    if br or g:
                        e.wait_ge(gated, 16 * br + 4 * g)
                    for m in range(4):
                        sum_out(4 * (g % 2) + m, tmp[:, m, :])
                    for m in range(4):
                        t = 16 * br + 4 * g + m
                        e.wait_ge(sums_ready, SUMS[stage] + 4 * g + m + 1)
                        e.tensor_tensor(gates[:, t, :], gates[:, t, :], tmp[:, m, :], ALU.mult).then_inc(gated, 1)
                    if br:
                        for m in range(4):
                            t = 4 * g + m
                            e.wait_ge(gated, 16 + t + 1)
                            e.tensor_tensor(gates[:, t, :], gates[:, t, :], gates[:, 16 + t, :], ALU.add)\
                                .then_inc(merged, 1)
                        for m in range(4):
                            t = 4 * g + m
                            e.wait_ge(m_hi, t + 1)
                            e.tensor_tensor(pair2[:, t, 1, :], gates[:, t, :], pair2[:, t, 0, :].bitcast(F32),
                                            ALU.subtract).then_inc(m_lo, 1)
            onto_x(BASE["out2"] + LEAD, "out2", CPG, None, BASE["up2"] + LEAD, squared("ffn2"))
            inv_rms(e, "ffn2")
            norm_apply(e, "ffn2", SRC["ffn2"][0], SRC["ffn2"][1], SRC["ffn2"][2])
            ffn("up2", "down2", 1, False, None, squared("fin2"))
            inv_rms(e, "fin2")
            for t in range(KT):
                norm_scale(e, "fin2", t, x[:, t, :], vec("g_final2", t), out=x[:, t, :])

        @block.tensor
        def _(e):
            e.wait_ge(s_tabs, 32)
            e.wait_ge(csplit_lo, 1)

            def turn_mod(g):
                e.wait_ge(mod_rows, g + 1)
                if g >= 2:
                    e.wait_ge(mod_ready, g - 1)
                for m in range(4):
                    r = e.matmul(ps[:, 4 + g % 2, 2 * m:2 * m + 2], mrows[0:4, g % 2, m * P:(m + 1) * P], pick,
                                 start=True, stop=True)
                r.then_inc(mod_turned, 1)

            for g in range(8):
                def mod_jobs(kt, whi, wlo, first, last):
                    e.matmul(ps[0:4, g % 2, :], csplit[:, kt, :], whi, start=first, stop=False)
                    return e.matmul(ps[0:4, g % 2, :], csplit[:, kt, :], wlo, start=False, stop=last)

                def between(kt):
                    if kt == 0 and g >= 2:
                        e.wait_ge(mod_rows, g - 1)
                    if kt == 8 and g >= 1:
                        turn_mod(g - 1)
                group(e, g * CPG, CPG, 2, GW, mod_jobs, need=between)
                if g == 0:
                    sum_squares(e, 8, tmp[:, 0:2, :], STAT["x"])
                if g == 2:
                    sum_squares(e, 16, tmp[:, 0:2, :], STAT["ctx"])
            turn_mod(7)

            def wide(banks, acts, n=4):
                def jobs(kt, whi, wlo, first, last):
                    for m in range(n):
                        for bk, act in zip(banks, acts):
                            r = features(e, bk + m, whi[:, m * P:(m + 1) * P], wlo[:, m * P:(m + 1) * P], act(kt),
                                         first, last)
                    return r
                return jobs

            def px(kt):
                return pair[:, kt]

            def pc(kt):
                return ctxpair[:, kt]

            def normed(name):
                return lambda kt: e.wait_ge(norm_lo, PAIRED[name] + kt + 1)

            e.wait_ge(std_ready, 2)
            e.wait_ge(mod_rows, 8)
            e.wait_ge(mod_ready, 8)
            group(e, BASE["cq"], CPG, 2, GW, wide([0], [px]), need=normed("x"))
            e.wait_ge(sums_ready, SUMS["cq"] + 4)
            group(e, BASE["ckv"], CPG, 2, GW, wide([4, 0], [px, pc]), need=normed("ctx"))
            e.wait_ge(sums_ready, SUMS["ckv"] + 8)
            stats(e, "cq")
            def kr_jobs(kt, whi, wlo, first, last):
                features(e, 4, whi, wlo, px(kt), first, last)
                return features(e, 7, whi, wlo, pc(kt), first, last)
            group(e, BASE["kr"], 2, 8, P, kr_jobs)
            e.wait_ge(std_ready, 3)
            group(e, BASE["qn"], CPG, 2, GW, wide([0], [px]))
            stats(e, "ckv")
            e.wait_ge(sums_ready, SUMS["kr"] + 2)
            e.matmul(ps[:, 7, 0:T], rot, rinv[:, 1, :], start=True, stop=True).then_inc(turned, 1)
            stats(e, "ckvc")
            e.wait_ge(sums_ready, SUMS["qn"] + 4)
            e.wait_ge(std_ready, 5)
            e.wait_ge(roped, 4)
            group(e, BASE["kn"], CPG, 2, GW, wide([4, 0], [px, pc]))
            e.wait_ge(sums_ready, SUMS["kn"] + 8)

            def vn_jobs(kt, whi, wlo, first, last):
                for tt in range(4):
                    r = tokens(e, ps[:, 4 + tt, :], whi, wlo, px(kt) if tt < 2 else pc(kt), tt % 2, first, last)
                return r
            group(e, BASE["vn"], CPG, 2, GW, vn_jobs)

            def f_jobs(kt, whi, wlo, first, last):
                for tt in range(2):
                    r = tokens(e, ps[:, tt, :], whi, wlo, px(kt), tt, first, last)
                return r
            group(e, BASE["f"], CPG, 2, GW, f_jobs)
            e.wait_ge(norm_lo, PAIRED["cq"] + RT)
            e.wait_ge(rows_copied, ROWS["f"] + 2)
            for g in range(4):
                if g >= 2:
                    e.wait_ge(sums_ready, SUMS["uq"] + 3 * (g - 1))

                def uq_jobs(kt, whi, wlo, first, last, b=4 * (g % 2)):
                    for m in range(2):
                        s = slice(m * NOPE, (m + 1) * NOPE)
                        features(e, b + m, whi[:, s], wlo[:, s], cqn[:, kt], first, last)
                    s = slice(2 * NOPE, 2 * (NOPE + ROPE))
                    return features(e, b + 2, whi[:, s], wlo[:, s], cqn[:, kt], first, last)
                group(e, BASE["uq"] + 2 * g, 2, 2, 2 * (NOPE + ROPE), uq_jobs)
            late_sums(e, 0, 8, 3)
            e.wait_ge(sums_ready, SUMS["uq"] + 12)
            e.wait_ge(late_mod, 1)
            for g in range(4):
                e.matmul(ps[:, g, 0:T], rot, qrope[:, g, :], start=True, stop=True).then_inc(turned, 1)
            e.wait_ge(s_dft, 32)
            for g in range(FN_G):
                for tt in range(2):
                    m = e.matmul(ps[:, 4 + g, :], f_sb[:, tt, g * P:(g + 1) * P], dft[:, 2 * T * tt:2 * T * (tt + 1)],
                                 start=(tt == 0), stop=(tt == 1))
                m.then_inc(uv_done, 1)
            e.wait_ge(roped, 12)
            for g in range(FN_G):
                e.wait_ge(uv_copied, g + 1)
                for s in range(2):
                    m = e.matmul(ps[:, g, 0:T], dft[:, 4 * T + s * P:4 * T + (s + 1) * P], uv[:, g, s * T:(s + 1) * T],
                                 start=(s == 0), stop=(s == 1))
                m.then_inc(spec_done, 1)
            for g in range(FN_G):
                e.wait_ge(spec_copied, g + 1)
                e.matmul(ps[:, 4 + g, 0:T], wfn[:, g, :], spec[:, g, :], start=True, stop=True).then_inc(fn_done, 1)
            e.wait_ge(o_lo, FN_G)
            e.wait_ge(norm_lo, PAIRED["ckvc"] + RT)
            for g in range(4):
                if g:
                    e.wait_ge(sums_ready, SUMS["ukv"] + 4 * g)
                    e.wait_ge(rows_copied, ROWS["ukv"] + 4 * g)

                def ukv_jobs(kt, whi, wlo, first, last):
                    for m in range(2):
                        s = slice(m * (NOPE + VD), m * (NOPE + VD) + NOPE)
                        for st in range(2):
                            features(e, 2 * m + st, whi[:, s], wlo[:, s], ckvn[:, st, kt], first, last)
                    wv = [w.rearrange("p (m n) -> p m n", m=2)[:, :, NOPE:] for w in (whi, wlo)]
                    for tt in range(4):
                        out = ps[:, 4 + tt, 0:2 * VD].rearrange("p (m n) -> p m n", m=2)
                        r = tokens(e, out, wv[0], wv[1], ckvn[:, tt // 2, kt], tt % 2, first, last)
                    return r
                group(e, BASE["ukv"] + 2 * g, 2, 2, GW, ukv_jobs)
            e.wait_ge(sums_ready, SUMS["ukv"] + 16)
            e.wait_ge(rows_copied, ROWS["ukv"] + 16)
            for i in range(HEADS + 2):
                if i == HEADS + 1:
                    e.wait_ge(exps, 2 * HEADS)
                    late_sums(e, 8, 12, 2)
                if i < HEADS:
                    if i >= 2:
                        e.wait_ge(exps, 2 * (i - 1))
                    for t in range(2):
                        q, out = slice(t * P, (t + 1) * P), ps[:, 2 * (i % 2) + t, :]
                        if i < MLA_H:
                            e.matmul(out, qnope[:, i, q], knope[:, i].rearrange("p s t -> p (s t)"), start=True,
                                     stop=False)
                            kr = kro if i % 2 else kre
                            m = e.matmul(out, qrope[:, i // 2, q], kr[:].rearrange("p s t -> p (s t)"), start=False,
                                         stop=True)
                        else:
                            h = i - MLA_H
                            m = e.matmul(out, qn[:, h, q], kn[:, h].rearrange("p s t -> p (s t)"), start=True,
                                         stop=True)
                        m.then_inc(scores, 1)
                if 1 <= i <= HEADS:
                    h = i - 1
                    for t in range(2):
                        e.wait_ge(probs, 2 * h + t + 1)
                        if h >= 1:
                            e.wait_ge(flips_copied, 2 * h + t - 1)
                        for k in range(4):
                            m = e.transpose(ps[:, 4 + t, k * P:(k + 1) * P], prob[:, h % 2, t, k * P:(k + 1) * P],
                                            ident)
                        m.then_inc(flipped, 1)
                if i >= 2:
                    h = i - 2
                    e.wait_ge(flips_copied, 2 * h + 2)
                    if h >= 2:
                        e.wait_ge(o_lo, FN_G + h - 1)
                    for k in range(4):
                        v = v_sb[:, k, h * VD:(h + 1) * VD] if h < MLA_H else vn[:, k, (h - MLA_H) * P:(h - MLA_H + 1) * P]
                        m = e.matmul(ps[:, 6 + h % 2, 0:T], v, probT[:, h % 2, k, :], start=(k == 0), stop=(k == 3))
                    m.then_inc(mixed, 1)
            e.wait_ge(o_lo, FN_G + HEADS)
            e.wait_ge(late_mod, 2)
            for g in range(4):
                if g >= 2:
                    e.wait_ge(sums_ready, SUMS["out"] + 4 * (g - 1))
                group(e, BASE["out"] + g * CPG, CPG, 2, GW, wide([4 * (g % 2)], [px]))
            e.wait_ge(sums_ready, SUMS["out"] + 12)
            late_sums(e, 12, 16, 2)
            sum_squares(e, 24, sq_acc[:, 0], STAT["ffn"])
            e.wait_ge(late_mod, 3)

            def ffn(s_up, s_down, n_ffn, name, stat_no):
                e.wait_ge(std_ready, stat_no)
                e.wait_ge(norm_lo, PAIRED[name] + KT)
                with e.Fori(0, 11) as j:
                    for g in range(2):
                        e.wait_ge(sums_ready, plus(SUMS[s_up] - 4 + 4 * g, j, 8))
                        group(e, BASE[s_up] + g * CPG, CPG, 2, GW, wide([4 * g], [px]), j, 2 * CPG)
                def hidden(kt):
                    e.wait_ge(hid_lo, 44 * n_ffn + kt + 1)
                with e.Fori(0, 2) as j:
                    for g in range(2):
                        e.wait_ge(sums_ready, plus(SUMS[s_down] - 4 + 4 * g, j, 8))
                        group(e, BASE[s_down] + g * FT // 2, FT // 2, 2, GW,
                              wide([4 * g], [lambda kt: hid[:, kt]]), j, FT, need=hidden)
                e.wait_ge(sums_ready, SUMS[s_down] + 16)

            ffn("up", "down", 0, "ffn", NORM["ffn"][2] + 1)
            sum_squares(e, 40, sq_acc[:, 0], STAT["fin"])
            sum_squares(e, 40, sq_acc[:, 1], STAT["mix2"])
            e.wait_ge(norm_lo, PAIRED["mix2"] + KT)
            for g in range(2):
                group(e, BASE["qa"] + g * CPG, CPG, 2, GW, wide([4 * g], [px]))
            e.wait_ge(sums_ready, SUMS["qa"] + 4)

            def kva_jobs(kt, whi, wlo, first, last):
                for m in range(2):
                    features(e, m, whi[:, m * P:(m + 1) * P], wlo[:, m * P:(m + 1) * P], px(kt), first, last)
                for tt in range(2):
                    r = tokens(e, ps[:, 2 + tt, 0:T], whi[:, T:2 * T], wlo[:, T:2 * T], px(kt), tt, first, last)
                return r
            group(e, BASE["kva"], CPG, 2, GW, kva_jobs)
            e.wait_ge(rows_copied, ROWS["kva"] + 2)
            e.wait_ge(sums_ready, SUMS["kva"] + 2)
            with e.Fori(0, 2) as j:
                for g in range(2):
                    e.wait_ge(sums_ready, plus(SUMS["qkb"] - 4 + 4 * g, j, 8))
                    group(e, BASE["qkb"] + g * CPG, CPG, 2, GW, wide([4 - 4 * g], [px]), j, 2 * CPG)
            e.wait_ge(sums_ready, SUMS["qkb"] + 16)
            for g in range(2):
                def vb_jobs(kt, whi, wlo, first, last, g=g):
                    for tt in range(2):
                        r = tokens(e, ps[:, 4 * g + tt, :], whi, wlo, px(kt), tt, first, last)
                    return r
                group(e, BASE["vb"] + g * CPG, CPG, 2, GW, vb_jobs)
            e.wait_ge(rows_copied, ROWS["vb"] + 4)
            with e.Fori(0, 4) as j:
                for g in range(2):
                    e.wait_ge(sums_ready, plus(SUMS["gates"] - 4 + 4 * g, j, 8))
                    group(e, BASE["gates"] + g * CPG, CPG, 2, GW, wide([4 * g], [px]), j, 2 * CPG)
            e.wait_ge(sums_ready, SUMS["gates"] + 32)
            e.wait_ge(qb_scaled, 1)
            e.wait_ge(s_stick, 16)
            tri = stick[:, W3:W3 + P]
            for i in range(PAIRS + 2):
                if i < PAIRS:
                    if i == 1:
                        e.wait_ge(sw_biased, 4)
                    if i >= 2:
                        e.wait_ge(sw_flipc, i - 1)
                    for h in range(2):
                        hq = 2 * i + h
                        kv = hq // 4
                        r = slice(HD * (kv % 2), HD * (kv % 2 + 1))
                        qt = qa[r, 4 * (kv // 2) + hq % 4, :]
                        kt_ = ka[r, kv // 2, :]
                        e.matmul(ps[:, h, 0:P], qt[:, 0:P], kt_[:, 0:P], start=True, stop=True)
                        e.matmul(ps[:, h, P:W3], qt[:, P:2 * P], kt_, start=True, stop=True).then_inc(sw_scores, 1)
                    if i:
                        e.wait_ge(sb_zb, i)
                    for h in range(2):
                        r = slice(HD * h, HD * (h + 1))
                        q, k = qkb[r, i, :], qkb[r, PAIRS + i, :]
                        e.matmul(ps[:, 2 + h, 0:T], k[:, 0:P], q, start=True, stop=True)
                        e.matmul(ps[:, 2 + h, T:W3], k[:, P:2 * P], q[:, P:2 * P], start=True, stop=True)\
                            .then_inc(sb_z, 1)
                if 1 <= i <= PAIRS:
                    n = i - 1
                    e.wait_ge(sb_sp, i)
                    if n:
                        e.wait_ge(sb_d, n)
                    for h in range(2):
                        s = sp_[:, n % 2, h]
                        out = ps[:, 4 + h, :]
                        e.matmul(out[:, 0:P], tri, s[:, 0:P], start=True, stop=True)
                        e.matmul(out[:, P:T], tri, s[:, P:T], start=True, stop=False)
                        e.matmul(out[:, P:T], ones, s[:, T:W3], start=False, stop=True)
                        m = e.matmul(out[:, T:W3], tri, s[:, T:W3], start=True, stop=True)
                    m.then_inc(sb_suffix, 1)
                    e.wait_ge(sw_probs, 4 * i)
                    if i < PAIRS:
                        e.wait_ge(sw_biased, 4 * (i + 1))
                    if n:
                        e.wait_ge(sw_flipc, n)
                    for h in range(2):
                        for dst, src in ((0, 0), (1, 1), (2, 2)):
                            m = e.transpose(ps[:, h, dst * P:(dst + 1) * P], sa[:, n % 2, h, src * P:(src + 1) * P],
                                            ident)
                    m.then_inc(sw_flip, 1)
                if i >= 2:
                    n = i - 2
                    c0 = slice(0, P)
                    c1 = slice(P, T)
                    for br in range(2):
                        if br == 0:
                            e.wait_ge(sw_flipc, n + 1)
                        else:
                            e.wait_ge(sb_a, n + 1)
                        if n:
                            e.wait_ge(o2_lo, 2 * (n - 1) + br + 1)
                        for h in range(2):
                            hq = 2 * n + h
                            r = slice(HD * h, HD * (h + 1))
                            pt = saT[:, n % 2, h] if br == 0 else zb[:, n % 3, h]
                            vv = va if br == 0 else vb
                            hv = hq // 4 if br == 0 else hq
                            v = [vv[:, tt, hv * HD:(hv + 1) * HD] for tt in range(2)]
                            e.matmul(ps[r, 6 + br, c0], v[0], pt[:, 0:P], start=True, stop=True)
                            e.matmul(ps[r, 6 + br, c1], v[0], pt[:, P:T], start=True, stop=False)
                            e.matmul(ps[r, 6 + br, c1], v[1], pt[:, T:W3], start=False, stop=True)\
                                .then_inc(mixed2, 1)
            e.wait_ge(o2_lo, 2 * PAIRS)
            for br, stage in enumerate(("bra", "brb")):
                for g in range(4):
                    if br or g >= 2:
                        e.wait_ge(sums_ready, SUMS[stage] + 4 * (g - 1))
                    group(e, BASE[stage] + 4 * g, 4, 2, GW, wide([4 * (g % 2)], [lambda kt: pair[:, 8 * br + kt]]))
            e.wait_ge(m_lo, KT)
            with e.Fori(0, 2) as j:
                for g in range(2):
                    e.wait_ge(sums_ready, plus(SUMS["out2"] - 4 + 4 * g, j, 8))
                    group(e, BASE["out2"] + g * CPG, CPG, 2, GW, wide([4 * g], [lambda kt: pair2[:, kt]]), j, 2 * CPG)
            sum_squares(e, 48, sq_acc[:, 0], STAT["ffn2"])
            ffn("up2", "down2", 1, "ffn2", NORM["ffn2"][2] + 1)
            sum_squares(e, 56, sq_acc[:, 0], STAT["fin2"])


_ORDER = ("xT", "ctxT", "vecs", "w_mod", "w_in", "w_uq", "w_ukv", "rpb", "w_fnet", "w_out", "w_up", "w_down",
          "w_in2", "w_bra", "w_brb", "w_out2", "w_up2", "w_down2",
          "base_tab", "rope_tab", "dft_tab", "na_mask", "stick_tab", "dist_tab")


def toeplitz(rpb):
    wide = np.zeros(rpb.shape[:2] + (2 * GRID_W - 1,), rpb.dtype)
    o = GRID_W - NA_KW
    wide[:, :, o:o + 2 * NA_KW - 1] = rpb
    return np.stack([wide[:, :, GRID_W - 1 - w:2 * GRID_W - 1 - w] for w in range(GRID_W)])


def lay_out(inputs):
    g = {k: np.asarray(v) for k, v in inputs.items()}

    def cols(v):
        return np.ascontiguousarray(v.reshape(-1, P).T)

    vecs = np.zeros((P, NV), np.float32)

    def put(name, v):
        o, n = VEC[name]
        vecs[:, o:o + n] = v

    put("c", cols(g["c"]))
    put("c_ctx", cols(g["c_ctx"]))
    put("b_mod", cols(g["b_mod"]))
    put("g_attn", cols(g["g_attn"]))
    put("g_ffn", cols(g["g_ffn"]))
    put("g_q", cols(g["g_q"]))
    put("g_kv", cols(g["g_kv"]))
    put("conv_w", cols(g["conv_w"]))
    put("conv_b", cols(g["conv_b"]))
    put("g_final", cols(g["g_final"]))
    put("g_mix2", cols(g["norm_mix_g_2"]))
    put("g_ffn2", cols(g["norm_ffn_g_2"]))
    put("g_final2", cols(g["norm_final_g_2"]))
    put("sink", np.broadcast_to(np.repeat(g["sink_logits_2"].reshape(-1), 2), (P, 2 * A_H)))
    put("eps", np.float32(EPS))
    out = dict(
        xT=np.ascontiguousarray(g["x"][0].T), ctxT=np.ascontiguousarray(g["ctx"][0].T), vecs=vecs,
        w_mod=g["w_mod"][0], w_in=g["w_in"][0], w_uq=g["w_uq"][0], w_ukv=g["w_ukv"][0], rpb=toeplitz(g["na_rpb"][0]),
        w_fnet=g["w_fnet"][0], w_out=g["w_out"][0], w_up=g["w_up"][0], w_down=g["w_down"][0],
        w_in2=g["w_in_2"][0], w_bra=g["w_branch_a_2"][0], w_brb=g["w_branch_b_2"][0], w_out2=g["w_out_2"][0],
        w_up2=g["w_ffn_in_2"][0], w_down2=g["w_ffn_down_2"][0])
    out.update(host_tables())
    return out


def kernel(**inputs):
    import concourse.bacc as bacc
    from concourse.bass_utils import run_bass_kernel_spmd

    arrays = lay_out(inputs)
    nc = bacc.Bacc("TRN2", target_bir_lowering=False, num_devices=1)
    maps, args = {}, []
    for name in _ORDER:
        a = np.ascontiguousarray(arrays[name])
        maps[f"in_{name}"] = a
        args.append(nc.dram_tensor(f"in_{name}", a.shape, mybir.dt.from_np(a.dtype), kind="ExternalInput").ap())
    args.append(nc.dram_tensor("outT", (D, T), F32, kind="ExternalOutput").ap())
    two_blocks(nc, *args)
    r = run_bass_kernel_spmd(nc, [maps], core_ids=[0])
    return np.ascontiguousarray(r.results[0]["outT"].T)[None]
```

```python
from contextlib import ExitStack

import numpy as np

import concourse.bass as bass
from concourse import mybir

F32 = mybir.dt.float32
F32R = mybir.dt.float32r
ALU = mybir.AluOpType
ACT = mybir.ActivationFunctionType
AX_X = mybir.AxisListType.X

P = 128
D = 2048
T = 256
KT = D // P
FF = 5632
FT = FF // P
R = 4
LEAD = R
CH = 1024
GW = 512
CPG = KT // 2
EPS = 1e-6
BIG = 1e30

MLA_H, NOPE, ROPE, VD, RANK = 8, 128, 64, 128, 512
RT = RANK // P
MLA_SCALE = (NOPE + ROPE) ** -0.5
NA_H, NA_ROWS, GRID_W, NA_KH, NA_KW = 4, 4, 64, 8, 16
NA_SCALE = 128 ** -0.5
FN_G = 4
HEADS = MLA_H + NA_H

A_H, A_KV, B_H, HD = 16, 4, 16, 64
PAIRS = A_H // 2
SLOPES = [2.0 ** (-8.0 * (h + 1) / A_H) for h in range(A_H)]

VEC = {}


def _vec(name, n):
    VEC[name] = (VEC["_n"] if "_n" in VEC else 0, n)
    VEC["_n"] = VEC[name][0] + n


for _name, _n in (("c", KT), ("c_ctx", KT), ("b_mod", 6 * KT), ("g_attn", KT), ("g_ffn", KT),
                  ("g_q", RT), ("g_kv", RT), ("conv_w", 3 * 2 * FT), ("conv_b", 2 * FT),
                  ("g_final", KT), ("g_mix2", KT), ("g_ffn2", KT), ("g_final2", KT),
                  ("sink", 2 * A_H), ("eps", 1)):
    _vec(_name, _n)
NV = VEC["_n"]

STAGES = [("mod1", 8, CPG), ("cq", 1, CPG), ("ckv", 1, CPG), ("kr", 1, 2), ("qn", 1, CPG), ("kn", 1, CPG),
          ("vn", 1, CPG), ("f", 1, CPG), ("uq", 4, 2), ("ukv", 4, 2), ("out", 4, CPG),
          ("up", 22, CPG), ("down", 4, FT // 2),
          ("qa", 2, CPG), ("kva", 1, CPG), ("qkb", 4, CPG), ("vb", 2, CPG), ("gates", 8, CPG),
          ("bra", 4, 4), ("brb", 4, 4), ("out2", 4, CPG), ("up2", 22, CPG), ("down2", 4, FT // 2)]
BASE = {}
N_CHUNKS = 0
for _s, _g, _n in STAGES:
    BASE[_s] = N_CHUNKS
    N_CHUNKS += _g * _n
N_EXTRA = 4 * D // GW * CPG
EXTRA = {}
_pace = [t for _s, t in (("cq", 1.6), ("ckv", 3.2), ("kr", 6.4), ("qn", 1.6), ("kn", 3.2), ("vn", 3.2), ("f", 1.6))
         for _ in range(2 if _s == "kr" else CPG)]
_spare = 0.0
_left = 64
for _i in range(len(_pace) + 4):
    if _i >= 10 and _left:
        _spare += _pace[_i - 6] - 1
        _n = min(int(_spare), 3, _left)
        if _n:
            EXTRA[BASE["cq"] + _i] = _n
            _spare -= _n
            _left -= _n
assert _left == 0, _left
for _i in range(CPG):
    EXTRA[BASE["ukv"] + CPG // 2 + _i] = 2
for _i in range(16):
    EXTRA[BASE["out"] + 5 + _i * 3 // 2] = 1
IN_X = 10
TURN = 2 * CPG
UP_X = 8
for _j in range(UP_X):
    for _i in (2, 5, 8, 11):
        EXTRA[BASE["up"] + _j * TURN + _i] = 1
IN_TURN = 4
X_END = BASE["up"] + UP_X * TURN
SEQ = []
for _c in range(X_END):
    SEQ.append(("weights", _c))
    for _ in range(EXTRA.get(_c, 0)):
        SEQ.append(("extra", sum(q[0] == "extra" for q in SEQ)))
assert all(q[0] == "weights" for q in SEQ[-R:]) and len(SEQ) == X_END + N_EXTRA and N_EXTRA % R == 0
POS = {q: i for i, q in enumerate(SEQ)}


def position(c):
    return POS[("weights", c)] if c < X_END else c + N_EXTRA


def loads_per(c, per):
    return per + IN_TURN if BASE["up"] <= c < X_END else per


def extra_tile(i):
    n = 12 * CPG
    return (i // CPG, i % CPG) if i < n else (12 + (i - n) % 4, (i - n) // 4)


SUMS = {}
N_SUMS = 0
for _s, _n in (("cq", 4), ("ckv", 8), ("kr", 2), ("qn", 4), ("kn", 8), ("uq", 12), ("ukv", 16),
               ("out", 16), ("up", 88), ("down", 16), ("qa", 8), ("kva", 2), ("qkb", 16),
               ("gates", 32), ("bra", 16), ("brb", 16), ("out2", 16), ("up2", 88), ("down2", 16)):
    SUMS[_s] = N_SUMS
    N_SUMS += _n
ROWS = {}
N_ROWS = 0
for _s, _n in (("vn", 4), ("f", 2), ("ukv", 16), ("kva", 2), ("vb", 4)):
    ROWS[_s] = N_ROWS
    N_ROWS += _n

NORM = {}
_t = 0
for _i, (_s, _n) in enumerate((("x", KT), ("ctx", KT), ("ckv", RT), ("cq", RT),
                               ("ffn", KT), ("fin", KT), ("mix2", KT), ("ffn2", KT), ("fin2", KT))):
    NORM[_s] = (_t, 0, _i, _n)
    _t += 0 if _s == "fin" else _n


def plus(base, it, per):
    return base if it is None else it * per + base


def host_tables():
    f = np.float32
    n = ROPE // 4
    freqs = (f(10000.0) ** (-np.arange(n, dtype=f) / f(n))).astype(f)
    pos = np.arange(T)
    ang = np.zeros((ROPE, T), f)
    rot = np.zeros((ROPE, ROPE), f)
    for half, where in enumerate((pos // GRID_W, pos % GRID_W)):
        for i in range(n):
            a, b = half * 2 * n + i, half * 2 * n + n + i
            ang[a] = ang[b] = where.astype(f) * freqs[i]
            rot[b, a] = -1.0
            rot[a, b] = 1.0
    rope = np.zeros((P, 2 * T + P), f)
    for s in range(2):
        rope[s * ROPE:(s + 1) * ROPE, 0:T] = np.cos(ang)
        rope[s * ROPE:(s + 1) * ROPE, T:2 * T] = np.sin(ang)
        rope[s * ROPE:(s + 1) * ROPE, 2 * T + s * ROPE:2 * T + (s + 1) * ROPE] = rot
    pick = np.zeros((P, 2), f)
    pick[0:4] = np.tile(np.eye(2, dtype=f), (2, 1))
    base = np.concatenate([np.eye(P, dtype=f), np.ones((P, P), f), pick], axis=1)
    l = np.arange(T)
    angl = 2 * np.pi * ((l[:, None] * l[None, :]) % T) / T
    cl = np.concatenate([np.cos(angl), np.sin(angl)], axis=1)
    c = np.arange(P)
    angc = 2 * np.pi * ((c[:, None] * c[None, :]) % P) / P
    ortho = 1.0 / np.sqrt(T * P)
    dft = np.concatenate([cl[:P], cl[P:], np.cos(angc) * ortho, -np.sin(angc) * ortho], axis=1).astype(f)
    w = np.arange(P) % GRID_W
    start = np.clip(w - NA_KW // 2, 0, GRID_W - NA_KW)[:, None]
    col = np.arange(GRID_W)[None, :]
    na_mask = np.where((col >= start) & (col < start + NA_KW), 0.0, -BIG).astype(f)
    k, q = np.arange(P)[:, None], np.arange(P)[None, :]
    strict = np.where(k < q, 0.0, -BIG).astype(f)
    tri = (k >= q).astype(f)
    stick = np.concatenate([strict, np.zeros((P, P), f), strict, tri], axis=1)
    qi, ki = np.arange(P)[:, None], np.arange(2 * P)[None, :]
    dist = P + qi - ki
    dist = np.where((dist >= 0) & (dist < P), dist, BIG).astype(f)
    return dict(base_tab=base, rope_tab=rope, dft_tab=dft, na_mask=na_mask, stick_tab=stick, dist_tab=dist)


def two_blocks(nc, xT, ctxT, vecs_d, w_mod, w_in, w_uq, w_ukv, rpb, w_fnet, w_out, w_up, w_down,
               w_in2, w_bra, w_brb, w_out2, w_up2, w_down2,
               base_tab, rope_tab, dft_tab, na_mask, stick_tab, dist_tab, outT):
    ctx = ExitStack()
    with ctx:
        def sem(name):
            return ctx.enter_context(nc.semaphore(name))

        top = [-(-nc.sbuf_base // 32) * 32]

        def place(name, shape, dt=F32, at=None):
            size = 4 * int(np.prod(shape[1:]))
            if at is None:
                at = top[0]
                top[0] += -(-size // 32) * 32
            assert at + size <= nc.sbuf_usable_end, (name, at + size - nc.sbuf_usable_end)
            return nc.alloc_sbuf_tensor_at(name, shape, dt, offset=at), at

        raw, _ = place("raw", [P, R, CH])
        hi, _ = place("hi", [P, R, CH], F32R)
        lo, _ = place("lo", [P, R, CH], F32R)
        x, _ = place("x", [P, KT, T])
        pair, _ = place("pair", [P, KT, 2, T], F32R)
        tmp, tmp_at = place("tmp", [P, 4, T])
        base, _ = place("base", [P, 2 * P + 2])
        ident, ones, pick = base[:, 0:P], base[:, P:2 * P], base[0:4, 2 * P:2 * P + 2]
        vecs, _ = place("vecs", [P, NV])
        mod, _ = place("mod", [P, 2, 6 * KT])
        csil, _ = place("csil", [P, KT, 2])
        csplit, _ = place("csplit", [P, KT, 4], F32R)
        gain, _ = place("gain", [P, 3, KT])
        std, _ = place("std", [P, T])
        rinv, _ = place("rinv", [P, 2, T])
        small, _ = place("small", [P, 8 * 24])
        rope, rope_at = place("rope", [P, 2 * T + P])
        cos, sin, rot = rope[:, 0:T], rope[:, T:2 * T], rope[:, 2 * T:2 * T + P]
        reg = top[0]
        K1 = 1024
        ctxpair, _ = place("ctxpair", [P, KT, 2, T], F32R, reg)
        cq, _ = place("cq", [P, RT, T], at=reg + 32 * K1)
        mrows, _ = place("mrows", [P, 2, GW], at=reg + 32 * K1)
        ckv, _ = place("ckv", [P, RT, 2, T], at=reg + 36 * K1)
        cqn, _ = place("cqn", [P, RT, 2, T], F32R, reg + 44 * K1)
        ckvn, _ = place("ckvn", [P, 2, RT, 2, T], F32R, reg + 52 * K1)
        kre, _ = place("kre", [P, 2, T], at=reg + 68 * K1)
        kro, _ = place("kro", [P, 2, T], at=reg + 70 * K1)
        qn, _ = place("qn", [P, NA_H, T], at=reg + 72 * K1)
        kn, _ = place("kn", [P, NA_H, 2, T], at=reg + 76 * K1)
        vn, _ = place("vn", [P, 4, GW], at=reg + 84 * K1)
        f_sb, _ = place("f_sb", [P, 2, GW], at=reg + 92 * K1)
        ctx_x, _ = place("ctx_x", [P, KT, T], at=reg + 76 * K1)
        dft, _ = place("dft", [P, 4 * T + 2 * P], at=reg)
        wfn, _ = place("wfn", [P, FN_G, P], at=reg + 5 * K1)
        uv, _ = place("uv", [P, FN_G, 2 * T], at=reg + 7 * K1)
        spec, _ = place("spec", [P, FN_G, T], at=reg + 15 * K1)
        knope, _ = place("knope", [P, MLA_H, 2, T], at=reg)
        v_sb, _ = place("v_sb", [P, 4, MLA_H * VD], at=reg + 16 * K1)
        qnope, _ = place("qnope", [P, MLA_H, T], at=reg + 32 * K1)
        qrope, _ = place("qrope", [P, MLA_H // 2, T], at=reg + 40 * K1)
        prob, _ = place("prob", [P, 2, 2, 2 * T], at=reg + 44 * K1)
        probT, _ = place("probT", [P, 2, 4, T], at=reg + 52 * K1)
        bias, _ = place("bias", [P, NA_H, 2, T], at=reg + 60 * K1)
        late, _ = place("late", [P, 6, GW], at=reg + 76 * K1)
        hid, _ = place("hid", [P, FT, 2, T], F32R, reg)
        sq_acc, _ = place("sq_acc", [P, 2, 2, T], at=reg + 88 * K1)
        sq_slot, _ = place("sq_slot", [P, 2, 2, T], at=reg + 92 * K1)
        gate, _ = place("gate", [P, 4, T], at=reg + 88 * K1)
        val, _ = place("val", [P, 4, T], at=reg + 92 * K1)
        qa, _ = place("qa", [P, PAIRS, T], at=reg)
        ka, _ = place("ka", [P, 2, T], at=reg + 8 * K1)
        va, _ = place("va", [P, 2, A_KV * HD], at=reg + 10 * K1)
        qkb, _ = place("qkb", [P, 2 * PAIRS, T], at=reg + 12 * K1)
        vb, _ = place("vb", [P, 2, B_H * HD], at=reg + 28 * K1)
        gates, _ = place("gates", [P, 2 * KT, T], at=reg + 36 * K1)
        W3 = 3 * P
        sa, _ = place("sa", [P, 2, 2, W3], at=reg + 68 * K1)
        saT, _ = place("saT", [P, 2, 2, W3], at=reg + 74 * K1)
        sp_, _ = place("sp_", [P, 2, 2, W3], at=reg + 80 * K1)
        zb, _ = place("zb", [P, 3, 2, W3], at=reg + 86 * K1)
        lnb, _ = place("lnb", [P, 2, W3], at=tmp_at)
        dist, _ = place("dist", [P, 2 * P], at=tmp_at + 3 * K1)
        stick, _ = place("stick", [P, 4 * P], at=rope_at)
        pair2, _ = place("pair2", [P, KT, 2, T], F32R, reg)

        ps = ctx.enter_context(nc.psum_tensor("ps", [P, 8, 512], F32))

        def vec(name, i=0, n=1, it=None, per=0):
            o = VEC[name][0] + i
            if it is None:
                return vecs[:, o:o + n]
            return vecs[:, bass.ds(it * per + o, n)]

        landed = [sem(f"landed{i}") for i in range(R)]
        s_x, s_ctx, s_vecs, s_tabs = sem("x_landed"), sem("ctx_landed"), sem("vecs_landed"), sem("tabs_landed")
        s_dft, s_bias, s_stick, s_dist = sem("dft_landed"), sem("bias_landed"), sem("stick_landed"), sem("dist_landed")
        mod_rows, mod_turned, hi_ready, lo_ready, weights_used = sem("mod_rows"), sem("mod_turned"), sem("hi_ready"), sem("lo_ready"), sem("weights_used")
        sums_ready, rows_copied = sem("sums_ready"), sem("rows_copied")
        late_zero = sem("late_zero")
        csplit_hi, csplit_lo = sem("csplit_hi"), sem("csplit_lo")
        extra_used, mod_sum, late_mod, x_again = sem("extra_used"), sem("mod_sum"), sem("late_mod"), sem("x_again")
        silu_c, mod_ready, gain_ready = sem("silu_c"), sem("mod_ready"), sem("gain_ready")
        sq_ready, sq_used, std_ready, rinv_ready = sem("sq_ready"), sem("sq_used"), sem("std_ready"), sem("rinv_ready")
        scaled, norm_hi, norm_lo = sem("scaled"), sem("norm_hi"), sem("norm_lo")
        zeroed = sem("zeroed")
        turned, rope_mul, roped = sem("turned"), sem("rope_mul"), sem("roped")
        uv_done, uv_copied, spec_done, spec_copied, fn_done = (sem("uv_done"), sem("uv_copied"), sem("spec_done"),
                                                              sem("spec_copied"), sem("fn_done"))
        o_hi, o_lo = sem("o_hi"), sem("o_lo")
        scores, biased, maxed, negmax = sem("scores"), sem("biased"), sem("maxed"), sem("negmax")
        exps, recips, probs = sem("exps"), sem("recips"), sem("probs")
        flipped, flips_copied, mixed = sem("flipped"), sem("flips_copied"), sem("mixed")
        bias_masked = sem("bias_masked")
        resid = sem("resid")
        centre, sides, silu_done, prod = sem("centre"), sem("sides"), sem("silu_done"), sem("prod")
        hid_hi, hid_lo = sem("hid_hi"), sem("hid_lo")
        tmp_read, qb_scaled, gated, merged = (sem("tmp_read"), sem("qb_scaled"),
                                                         sem("gated"), sem("merged"))
        m_hi, m_lo = sem("m_hi"), sem("m_lo")
        sw_scores, sw_biased, sw_max, sw_neg = sem("sw_scores"), sem("sw_biased"), sem("sw_max"), sem("sw_neg")
        sw_exps, sw_sum, sw_probs, sw_flip, sw_flipc = (sem("sw_exps"), sem("sw_sum"), sem("sw_probs"),
                                                       sem("sw_flip"), sem("sw_flipc"))
        sb_z, sb_zb, sb_ln, sb_sp, sb_suffix, sb_d, sb_a = (sem("sb_z"), sem("sb_zb"), sem("sb_ln"), sem("sb_sp"),
                                                           sem("sb_suffix"), sem("sb_d"), sem("sb_a"))
        sb_step = sem("sb_step")
        sq_piece, sq_added, sq_sum, mix_ms, x_between = (sem("sq_piece"), sem("sq_added"), sem("sq_sum"), sem("mix_ms"),
                                                         sem("x_between"))
        mixed2, o2_hi, o2_lo = sem("mixed2"), sem("o2_hi"), sem("o2_lo")
        stored = sem("stored")

        block = ctx.enter_context(nc.Block())

        def hid_tile(j, j0, m):
            if j is None:
                return hid[:, 4 * j0 + m]
            return hid[:, bass.ds(j * 4 + (4 * j0 + m), 1), :, :].rearrange("p a s t -> p (a s) t")

        def for_turns(e, stage, turn):
            if stage == "up":
                with e.Fori(0, UP_X - 1) as j:
                    turn(j, 0)
                turn(None, UP_X - 1)
                with e.Fori(0, 11 - UP_X) as j:
                    turn(j, UP_X)
            else:
                with e.Fori(0, 11) as j:
                    turn(j, 0)

        def slot(c):
            return position(c) % R

        def load(e, p, dst, src, it=None, per=0):
            prev = p - R
            if prev >= len(SEQ):
                e.wait_ge(lo_ready, plus(prev - N_EXTRA + 1, it, per))
            elif prev >= 0:
                kind, i = SEQ[prev]
                if kind == "weights":
                    e.wait_ge(lo_ready, plus(i + 1, it, per))
                else:
                    e.wait_ge(extra_used, plus(2 * (i + 1), it, 2 * IN_TURN))
            e.dma_start(dst, src).then_inc(landed[p % R], 16)

        def raw_view(p, k, n):
            return raw[:, p % R, 0:k * n].rearrange("p (k n) -> p k n", k=k)

        def split_view(part, c, k, n):
            return part[:, c % R, 0:k * n].rearrange("p (k n) -> p k n", k=k)

        def pieces(c, *parts):
            r = raw[:, slot(c), :]
            ds = [p[:, c % R, :] for p in parts]
            if BASE["kr"] <= c < BASE["kr"] + 2:
                src = r[:, 0:CH // 2].rearrange("p (k n) -> p k n", n=ROPE)
                ds = [d.rearrange("p (k j n) -> p k j n", j=2, n=ROPE) for d in ds]
                return [[d[:, :, j] for d in ds] + [src] for j in range(2)]
            if BASE["uq"] <= c < BASE["ukv"]:
                n = 2 * 2 * (NOPE + ROPE)
                src = r[:, 0:n].rearrange("p (k m n) -> p k m n", k=2, m=2)
                ds = [d[:, 0:n].rearrange("p (k n) -> p k n", k=2) for d in ds]
                plain = [d[:, :, 0:2 * NOPE].rearrange("p k (m n) -> p k m n", m=2) for d in ds]
                rotary = [d[:, :, 2 * NOPE:].rearrange("p k (m n) -> p k m n", m=2) for d in ds]
                return [plain + [src[:, :, :, 0:NOPE]], rotary + [src[:, :, :, NOPE:]]]
            if BASE["qa"] <= c < BASE["kva"]:
                return [[d[:, k * GW:(k + 1) * GW].rearrange("p (i a d) -> p i a d", i=4, a=2) for d in ds]
                        + [r[:, k * GW:(k + 1) * GW].rearrange("p (a i d) -> p i a d", i=4, a=2)] for k in range(2)]
            return [ds + [r]]

        def split_hi(e, a, b, it=None, per=0):
            for c in range(a, min(b, N_CHUNKS)):
                e.wait_ge(landed[slot(c)], plus(16 * (position(c) // R + 1), it, 16 * loads_per(c, per) // R))
                if c >= R:
                    e.wait_ge(weights_used, plus(c - R + 1, it, per))
                for h, r in pieces(c, hi):
                    m = e.activation(h, r, ACT.Copy)
                m.then_inc(hi_ready, 1)

        def split_lo(e, a, b, it=None, per=0):
            for c in range(a, min(b, N_CHUNKS)):
                e.wait_ge(hi_ready, plus(c + 1, it, per))
                for l, h, r in pieces(c, lo, hi):
                    m = e.tensor_tensor(l, r, h.bitcast(F32), ALU.subtract)
                m.then_inc(lo_ready, 1)
                if EXTRA.get(c, 0):
                    i = SEQ[position(c) + 1][1]
                    accumulate(e, i, i + EXTRA[c], it)

        def late_acc(g):
            if g < IN_X:
                return x[:, 2 * (g % 8):2 * (g % 8) + 2, :].rearrange("p a t -> p (a t)")
            return late[:, g - 12 if g >= 12 else 4 + g - IN_X, :]

        def accumulate(e, a, b, it=None):
            for i in range(a, b):
                p = POS[("extra", i)]
                e.wait_ge(landed[p % R], plus(16 * (p // R + 1), it, 16 * (TURN + IN_TURN) // R))
                g, ch = extra_tile(i)
                acc = late_acc(g)
                for k in range(2):
                    kt = 2 * ch + k
                    w = raw_view(p, 2, GW)[:, k, :]
                    c = csil[:, kt, 0:1] if it is None else \
                        csil[:, bass.ds(it * 2 + kt, 1), 0:1].rearrange("p a b -> p (a b)")
                    if kt == 0 and g < 12:
                        if 8 <= g < IN_X:
                            e.wait_ge(mod_sum, 1)
                        e.tensor_scalar(acc, w, c, None, ALU.mult).then_inc(extra_used, 1)
                    else:
                        e.wait_ge(extra_used, plus(2 * i + k if g < 12 or k else 2 * i - 6, it, 2 * IN_TURN))
                        e.scalar_tensor_tensor(out=acc, in0=w, scalar=c, in1=acc, op0=ALU.mult, op1=ALU.add)\
                            .then_inc(extra_used, 1)

        def late_sums(e, a, b, bank):
            e.wait_ge(extra_used, 2 * CPG * b)
            for i in range(a, b):
                for m in range(4):
                    col = 4 * (i - a) + m
                    r = e.matmul(ps[:, bank, col:col + 1], late_acc(i)[:, m * P:(m + 1) * P], ones[:, 0:1],
                                 start=True, stop=True)
            r.then_inc(mod_sum, 1)

        def late_bias(e, n, a, b, bank):
            e.wait_ge(mod_sum, n)
            o = 2 * KT + 4 * a
            k = 4 * (b - a)
            e.tensor_tensor(mod[:, 0, o:o + k], ps[:, bank, 0:k], vec("b_mod", o, k), ALU.add).then_inc(late_mod, 1)

        def group(e, c0, n_chunks, kpc, w, jobs, it=None, per=0, need=None):
            for ch in range(n_chunks):
                c = c0 + ch
                e.wait_ge(lo_ready, plus(c + 1, it, per))
                for k in range(kpc):
                    kt = ch * kpc + k
                    if need is not None:
                        need(kt)
                    last = jobs(kt, split_view(hi, c, kpc, w)[:, k], split_view(lo, c, kpc, w)[:, k],
                                kt == 0, kt == n_chunks * kpc - 1)
                last.then_inc(weights_used, 1)

        def features(e, bank, whi, wlo, act, first, last):
            out = ps[:, bank, :]
            both = act.rearrange("p s t -> p (s t)")
            if first:
                e.matmul(out, whi, both, start=True, stop=False)
                return e.matmul(out[:, T:2 * T], wlo, act[:, 0, :], start=False, stop=False)
            m = e.matmul(out[:, T:2 * T], wlo, act[:, 0, :], start=False, stop=False)
            return e.matmul(out, whi, both, start=False, stop=last)

        def tokens(e, out, whi, wlo, act, tt, first, last):
            ahi, alo = act[:, 0, tt * P:(tt + 1) * P], act[:, 1, tt * P:(tt + 1) * P]
            e.matmul(out, alo, whi, start=first, stop=False)
            e.matmul(out, ahi, wlo, start=False, stop=False)
            return e.matmul(out, ahi, whi, start=False, stop=last)

        @block.sync
        def _(e):
            e.dma_start(vecs[:], vecs_d).then_inc(s_vecs, 16)
            wm = w_mod.rearrange("(t p) n -> p t n", p=P)

            def extras(p, it=None, per=0):
                while p + 1 < len(SEQ) and SEQ[p + 1][0] == "extra":
                    p += 1
                    i = SEQ[p][1]
                    g, ch = extra_tile(i)
                    col = 2 * D + g * GW
                    rows = slice(2 * ch, 2 * ch + 2) if it is None else bass.ds(it * 2 + 2 * ch, 2)
                    load(e, p, raw_view(p, 2, GW), wm[:, rows, col:col + GW], it, per)

            for c in range(8 * CPG):
                g, ch = c // CPG, c % CPG
                col = (D + g * GW) % (2 * D)
                load(e, c, raw_view(c, 2, GW), wm[:, 2 * ch:2 * ch + 2, col:col + GW])
                if c == 6:
                    e.dma_start(x[:], xT.rearrange("(t p) n -> p t n", p=P)).then_inc(s_x, 16)
                if c == 22:
                    e.dma_start(ctx_x[:], ctxT.rearrange("(t p) n -> p t n", p=P)).then_inc(s_ctx, 16)

            def stream(w, stage, col, g=0, it=None, per=0, col_per=0, kts=2, n=GW, chunks=CPG):
                wv = w.rearrange("(t p) n -> p t n", p=P)
                for ch in range(chunks):
                    p = position(BASE[stage] + g * chunks + ch)
                    cols = slice(col, col + n) if it is None else bass.ds(it * col_per + col, n)
                    load(e, p, raw_view(p, kts, n), wv[:, kts * ch:kts * (ch + 1), cols], it, per)
                    extras(p, it, per)

            for stage, col in (("cq", 0), ("ckv", 512), ("kr", 1024), ("qn", 1088), ("kn", 1600), ("vn", 2112),
                               ("f", 2624)):
                if stage == "kr":
                    stream(w_in, stage, col, kts=8, n=ROPE, chunks=2)
                else:
                    stream(w_in, stage, col)
            for g in range(4):
                stream(w_uq, "uq", g * 384, g, n=384, chunks=2)
            for g in range(4):
                stream(w_ukv, "ukv", g * GW, g, chunks=2)
            for g in range(4):
                stream(w_out, "out", g * GW, g)

            def ffn_stream(up, down, s_up, s_down):
                def turn(j, j0):
                    stream(up, s_up, j0 * GW, 2 * j0, j, TURN, GW)
                    stream(up, s_up, FF + j0 * GW, 2 * j0 + 1, j, TURN, GW)
                for_turns(e, s_up, turn)
                with e.Fori(0, 2) as j:
                    for g in range(2):
                        stream(down, s_down, g * GW, g, j, FT, 2 * GW, chunks=FT // 2)

            ffn_stream(w_up, w_down, "up", "down")
            for g in range(2):
                stream(w_in2, "qa", g * GW, g)
            stream(w_in2, "kva", 1024)
            with e.Fori(0, 2) as j:
                for g in range(2):
                    stream(w_in2, "qkb", 1536 + g * GW, g, j, 2 * CPG, 2 * GW)
            for g in range(2):
                stream(w_in2, "vb", 3584 + g * GW, g)
            with e.Fori(0, 4) as j:
                for g in range(2):
                    stream(w_in2, "gates", 4608 + g * GW, g, j, 2 * CPG, 2 * GW)
            for g in range(4):
                stream(w_bra, "bra", g * GW, g, chunks=4)
            for g in range(4):
                stream(w_brb, "brb", g * GW, g, chunks=4)
            with e.Fori(0, 2) as j:
                for g in range(2):
                    stream(w_out2, "out2", g * GW, g, j, 2 * CPG, 2 * GW)
            ffn_stream(w_up2, w_down2, "up2", "down2")

            ov = outT.rearrange("(t p) n -> p t n", p=P)
            for i in range(4):
                e.wait_ge(scaled, NORM["fin2"][0] + 4 * (i + 1))
                e.dma_start(ov[:, 4 * i:4 * i + 4, :], x[:, 4 * i:4 * i + 4, :]).then_inc(stored, 16)
            e.wait_ge(stored, 64)

        @block.gpsimd
        def _(e):
            e.dma_start(base[:], base_tab).then_inc(s_tabs, 16)
            e.dma_start(rope[:], rope_tab).then_inc(s_tabs, 16)
            e.memset(kre[64:P, :, :], 0.0).then_inc(zeroed, 1)
            e.memset(kro[0:64, :, :], 0.0).then_inc(zeroed, 1)
            e.wait_ge(weights_used, BASE["f"])
            e.dma_start(dft[:], dft_tab).then_inc(s_dft, 16)
            e.dma_start(wfn[:], w_fnet.rearrange("g c d -> c g d")).then_inc(s_dft, 16)
            e.wait_ge(weights_used, BASE["out"])
            e.dma_start(tmp[:, 3, 0:GRID_W], na_mask).then_inc(s_dft, 16)
            for r in range(NA_ROWS):
                a0 = NA_KH - 1 - r
                src = rpb[:, :, a0:a0 + NA_ROWS, :].rearrange("w h a c -> w h (a c)")
                e.dma_start(bias[(r % 2) * GRID_W:(r % 2 + 1) * GRID_W, :, r // 2, :], src).then_inc(s_bias, 16)
            e.wait_ge(mod_sum, 2)
            e.dma_start(x[:], xT.rearrange("(t p) n -> p t n", p=P)).then_inc(x_again, 16)
            e.wait_ge(weights_used, BASE["gates"])
            e.dma_start(stick[:], stick_tab).then_inc(s_stick, 16)

        def squares(e, name, src, bank_free=None):
            t0, s0, idx, n = NORM[name]
            if name not in ("x", "ctx"):
                e.wait_ge(norm_lo, sum(NORM[q][3] for q in PAIRED if NORM[q][2] < idx))
            for s in range(n // 2):
                if s0 + s >= 2:
                    e.wait_ge(sq_used, s0 + s - 1)
                e.activation(tmp[:, 2 * ((s0 + s) % 2):2 * ((s0 + s) % 2) + 2, :], src(2 * s), ACT.Square)\
                    .then_inc(sq_ready, 1)
            e.wait_ge(sq_used, s0 + n // 2)
            if idx >= 1:
                e.wait_ge(rinv_ready, idx)
            e.activation(std[:], ps[:, STAT[name], 0:T], ACT.Sqrt, bias=vec("eps"), scale=1.0 / (n * P))\
                .then_inc(std_ready, 1)

        STAT = {"x": 2, "ctx": 3, "cq": 5, "ckv": 5, "ffn": 0, "fin": 0, "mix2": 1, "ffn2": 0, "fin2": 0}

        def stats(e, name):
            t0, s0, idx, n = NORM[name]
            for s in range(n // 2):
                e.wait_ge(sq_ready, s0 + s + 1)
                for k in range(2):
                    last = e.matmul(ps[:, STAT[name], 0:T], ones, tmp[:, 2 * ((s0 + s) % 2) + k, :],
                                    start=(s == 0 and k == 0), stop=(s == n // 2 - 1 and k == 1))
                last.then_inc(sq_used, 1)

        SQ = {"x": 0, "ctx": 8, "ckv": 16, "ffn": 20, "fin": 28, "ffn2": 44, "fin2": 52}

        def square(e, n, src, scale=None):
            if n >= 2:
                e.wait_ge(sq_added, n - 1)
            if scale is None:
                e.activation(sq_slot[:, n % 2], src, ACT.Square).then_inc(sq_piece, 1)
            else:
                e.activation(sq_slot[:, n % 2, 0], src[:, 0], ACT.Square, scale=scale[:, 0:1])
                e.activation(sq_slot[:, n % 2, 1], src[:, 1], ACT.Square, scale=scale[:, 1:2]).then_inc(sq_piece, 1)

        def add_square(e, n, acc, first, apart=1):
            e.wait_ge(sq_piece, n + 1)
            if first:
                e.tensor_copy(acc, sq_slot[:, n % 2]).then_inc(sq_added, 1)
            else:
                e.wait_ge(sq_added, n + 1 - apart)
                e.tensor_tensor(acc, acc, sq_slot[:, n % 2], ALU.add).then_inc(sq_added, 1)

        def sum_squares(e, n, acc, bank):
            e.wait_ge(sq_added, n)
            for k in range(2):
                m = e.matmul(ps[:, bank, 0:T], ones, acc[:, k, :], start=(k == 0), stop=(k == 1))
            m.then_inc(sq_sum, 1)

        def root(e, name):
            t0, s0, idx, n = NORM[name]
            e.wait_ge(sq_sum, {"x": 1, "ctx": 2, "ffn": 4, "fin": 5, "ffn2": 7, "fin2": 8}[name])
            if idx >= 1:
                e.wait_ge(rinv_ready, idx)
            e.activation(std[:], ps[:, STAT[name], 0:T], ACT.Sqrt, bias=vec("eps"), scale=1.0 / (n * P))\
                .then_inc(std_ready, 1)

        def inv_rms(e, name, slot=0):
            idx = NORM[name][2]
            e.wait_ge(std_ready, idx + 1)
            e.reciprocal(rinv[:, slot, :], std[:]).then_inc(rinv_ready, 1)
            e.wait_ge(rinv_ready, idx + 1)

        def norm_scale(e, name, t, src, g, slot=0, out=None):
            n = NORM[name][0] + t
            if out is None:
                out = tmp[:, t % 4, :]
            e.scalar_tensor_tensor(out=out, in0=src, scalar=g, in1=rinv[:, slot, :], op0=ALU.mult, op1=ALU.mult)\
                .then_inc(scaled, 1)

        PAIRED = {}
        _n = 0
        for _s in ("x", "ctx", "ckv", "cq", "ffn", "mix2", "ffn2"):
            PAIRED[_s] = _n
            _n += NORM[_s][3]

        AFTER_NORM = {"ffn": "up", "mix2": "qa", "ffn2": "up2"}

        def next_split(e, name, t, split):
            if name in AFTER_NORM and t >= 5 and t % 2:
                c = BASE[AFTER_NORM[name]] + LEAD + (t - 5) // 2
                split(e, c, c + (1 if t < KT - 1 else 3))

        def norm_hi_part(e, name, dst, shift=None):
            for t in range(NORM[name][3]):
                if t:
                    next_split(e, name, t - 1, split_hi)
                e.wait_ge(scaled, NORM[name][0] + t + 1)
                b = 0.0 if shift is None else shift(t)
                e.activation(dst(t)[:, 0, :], tmp[:, t % 4, :], ACT.Copy if shift is None else ACT.Identity, bias=b)\
                    .then_inc(norm_hi, 1)
            next_split(e, name, NORM[name][3] - 1, split_hi)

        def norm_lo_part(e, name, t, dst, shift=None):
            e.wait_ge(norm_hi, PAIRED[name] + t + 1)
            h = dst(t)[:, 0, :].bitcast(F32)
            if shift is None:
                e.tensor_tensor(dst(t)[:, 1, :], tmp[:, t % 4, :], h, ALU.subtract).then_inc(norm_lo, 1)
            else:
                e.scalar_tensor_tensor(out=dst(t)[:, 1, :], in0=tmp[:, t % 4, :], scalar=shift(t), in1=h,
                                       op0=ALU.add, op1=ALU.subtract).then_inc(norm_lo, 1)

        def norm_apply(e, name, src, g, dst, shift=None, slot=0):
            n = NORM[name][3]
            for t in range(n + 2):
                if t < n:
                    if t >= 4:
                        e.wait_ge(norm_lo, PAIRED[name] + t - 3)
                    norm_scale(e, name, t, src(t), g(t), slot)
                if t >= 2:
                    norm_lo_part(e, name, t - 2, dst, shift)
                    next_split(e, name, t - 2, split_lo)

        SH1, SC1, GT1, SH2, SC2, GT2 = (KT * i for i in range(6))

        def modv(which, off, t, n=1):
            return mod[:, which, off + t:off + t + n]

        SRC = {
            "x": (lambda t: x[:, t, :], lambda t: gain[:, 0, t:t + 1], lambda t: pair[:, t], lambda t: modv(0, SH1, t)),
            "ctx": (lambda t: ctx_x[:, t, :], lambda t: gain[:, 1, t:t + 1], lambda t: ctxpair[:, t],
                    lambda t: modv(1, SH1, t)),
            "cq": (lambda t: cq[:, t, :], lambda t: vec("g_q", t), lambda t: cqn[:, t], None),
            "ffn": (lambda t: x[:, t, :], lambda t: gain[:, 2, t:t + 1], lambda t: pair[:, t], lambda t: modv(0, SH2, t)),
            "mix2": (lambda t: x[:, t, :], lambda t: vec("g_mix2", t), lambda t: pair[:, t], None),
            "ffn2": (lambda t: x[:, t, :], lambda t: vec("g_ffn2", t), lambda t: pair[:, t], None),
        }

        def sq_src(v):
            return lambda t: v[:, t:t + 2, :]

        RES = {"out": 0, "down": 16, "out2": 32, "down2": 48}

        @block.scalar
        def _(e):
            e.wait_ge(s_vecs, 16)
            for v, name in enumerate(("c", "c_ctx")):
                e.activation(csil[:, :, v], vec(name, 0, KT), ACT.Silu).then_inc(silu_c, 1)
            e.wait_ge(silu_c, 2)
            e.activation(csplit[:, :, 0:2], csil[:], ACT.Copy).then_inc(csplit_hi, 1)
            split_hi(e, 0, LEAD)
            for g in range(8):
                for i in range(CPG):
                    split_hi(e, LEAD + g * CPG + i, LEAD + g * CPG + i + 1)
                    if g in (1, 3):
                        if i == 0:
                            e.wait_ge(s_x if g == 1 else s_ctx, 16)
                        square(e, SQ["x" if g == 1 else "ctx"] + i, (x if g == 1 else ctx_x)[:, 2 * i:2 * i + 2, :])
                e.wait_ge(weights_used, (g + 1) * CPG)
                if g >= 2:
                    e.wait_ge(mod_turned, g - 1)
                e.activation(mrows[0:4, g % 2, :], ps[0:4, g % 2, :], ACT.Copy).then_inc(mod_rows, 1)
                if g == 2:
                    root(e, "x")
                if g == 4:
                    root(e, "ctx")
            norm_hi_part(e, "x", SRC["x"][2], SRC["x"][3])
            e_ctx = NORM["ctx"][0]
            for i in range(CPG):
                split_hi(e, BASE["cq"] + LEAD + i, BASE["cq"] + LEAD + i + 1)
                for t in (2 * i, 2 * i + 1):
                    e.wait_ge(scaled, e_ctx + t + 1)
                    e.activation(ctxpair[:, t, 0, :], tmp[:, t % 4, :], ACT.Identity, bias=modv(1, SH1, t))\
                        .then_inc(norm_hi, 1)

            def upto(a, stage, n):
                b = BASE[stage] + n + LEAD
                split_hi(e, a, b)
                return b

            at = BASE["cq"] + LEAD + CPG
            at = upto(at, "ckv", CPG - 1)
            e.wait_ge(sums_ready, SUMS["ckv"] + 8)
            for t in range(RT):
                square(e, SQ["ckv"] + t, ckv[:, t])
            at = upto(at, "ckv", CPG)
            e.wait_ge(sq_sum, 3)
            e.wait_ge(rinv_ready, NORM["ckv"][2])
            e.activation(rinv[:].rearrange("p s t -> p (s t)"), ps[:, STAT["ckv"], :], ACT.Sqrt, bias=vec("eps"),
                         scale=1.0 / RANK).then_inc(std_ready, 1)
            at = upto(at, "kr", 1)
            for t in range(RT):
                e.wait_ge(scaled, NORM["ckv"][0] + t + 1)
                e.activation(ckvn[:, :, t, 0, :], tmp[:, 2 * (t % 2):2 * (t % 2) + 2, :], ACT.Copy).then_inc(norm_hi, 1)
            at = upto(at, "kr", 2)
            squares(e, "cq", sq_src(cq))
            norm_hi_part(e, "cq", SRC["cq"][2])
            at = upto(at, "qn", CPG)
            at = upto(at, "kn", CPG)
            at = upto(at, "vn", CPG - 1)
            e.wait_ge(weights_used, BASE["vn"] + CPG)
            for tt in range(4):
                e.activation(vn[:, tt, :], ps[:, 4 + tt, :], ACT.Copy).then_inc(rows_copied, 1)
            at = upto(at, "f", CPG - 1)
            e.wait_ge(weights_used, BASE["f"] + CPG)
            for tt in range(2):
                e.activation(f_sb[:, tt, :], ps[:, tt, :], ACT.Copy).then_inc(rows_copied, 1)
            at = upto(at, "uq", 8)
            for g in range(FN_G):
                e.wait_ge(uv_done, g + 1)
                e.activation(uv[:, g, :], ps[:, 4 + g, :], ACT.Copy).then_inc(uv_copied, 1)
            for g in range(FN_G):
                e.wait_ge(fn_done, g + 1)
                e.activation(pair[:, HEADS + g, 0, :], ps[:, 4 + g, 0:T], ACT.Copy).then_inc(o_hi, 1)
            for g in range(4):
                e.wait_ge(weights_used, BASE["ukv"] + 2 * (g + 1))
                for tt in range(4):
                    e.activation(v_sb[:, tt, g * 2 * VD:(g + 1) * 2 * VD], ps[:, 4 + tt, 0:2 * VD], ACT.Copy)\
                        .then_inc(rows_copied, 1)
                at = upto(at, "ukv", 2 * (g + 1))
            for i in range(HEADS + 2):
                if 1 <= i <= HEADS:
                    h = i - 1
                    for t in range(2):
                        e.wait_ge(flipped, 2 * h + t + 1)
                        if h >= 2:
                            e.wait_ge(mixed, h - 1)
                        e.activation(probT[:, h % 2, :, t * P:(t + 1) * P],
                                     ps[:, 4 + t, :].rearrange("p (k q) -> p k q", k=4), ACT.Copy)\
                            .then_inc(flips_copied, 1)
                if i < HEADS:
                    for t in range(2):
                        n = 2 * i + t
                        e.wait_ge(negmax, n + 1)
                        if i >= 2:
                            e.wait_ge(flipped, n - 3)
                        src = ps[:, 2 * (i % 2) + t, :] if i < MLA_H else prob[:, i % 2, t, :]
                        e.activation(prob[:, i % 2, t, :], src, ACT.Exp, bias=small[:, 24 + n:25 + n],
                                     scale=MLA_SCALE if i < MLA_H else 1.0,
                                     accum_out=small[:, 48 + n:49 + n]).then_inc(exps, 1)
                if i >= 2:
                    h = i - 2
                    e.wait_ge(mixed, h + 1)
                    e.activation(pair[:, h, 0, :], ps[:, 6 + h % 2, 0:T], ACT.Copy).then_inc(o_hi, 1)
            for g in range(4):
                at = upto(at, "out", min((g + 1) * CPG + CPG, 4 * CPG))
                for i in range(2):
                    e.wait_ge(resid, RES["out"] + 4 * g + 2 * i + 2)
                    square(e, SQ["ffn"] + 2 * g + i, x[:, 4 * g + 2 * i:4 * g + 2 * i + 2, :])
            root(e, "ffn")
            norm_hi_part(e, "ffn", SRC["ffn"][2], SRC["ffn"][3])

            def ffn(s_up, s_down, n_ffn, conv):
                b = BASE[s_up]

                def turn(j, j0):
                    b = BASE[s_up] + TURN * j0

                    def centre_tap(group, buf, m):
                        e.activation(buf[:, m, :], tmp[:, m, :], ACT.Identity,
                                     bias=vec("conv_b", FT * group + m + 4 * j0, 1, j, 4),
                                     scale=vec("conv_w", 2 * FT + FT * group + m + 4 * j0, 1, j, 4)).then_inc(centre, 1)

                    def hidden(m):
                        e.wait_ge(prod, plus(44 * n_ffn + m + 1 + 4 * j0, j, 4))
                        e.activation(hid_tile(j, j0, m)[:, 0, :], val[:, m, :],
                                     ACT.Copy).then_inc(hid_hi, 1)

                    for m in range(4):
                        c = b + LEAD + CPG + 2 * m
                        split_hi(e, c, c + 2, j, 2 * CPG)
                        e.wait_ge(sums_ready, plus(SUMS[s_up] + m + 1 + 8 * j0, j, 8))
                        if conv:
                            centre_tap(0, gate, m)
                        else:
                            e.activation(gate[:, m, :], tmp[:, m, :], ACT.Silu).then_inc(silu_done, 1)
                    for m in range(4):
                        c = b + LEAD + 2 * CPG + 2 * m
                        split_hi(e, c, c + 2, j, 2 * CPG)
                        if conv:
                            e.wait_ge(sides, plus(2 * m + 2 + 16 * j0, j, 16))
                            e.activation(gate[:, m, :], gate[:, m, :], ACT.Silu).then_inc(silu_done, 1)
                            e.wait_ge(sums_ready, plus(SUMS[s_up] + 4 + m + 1 + 8 * j0, j, 8))
                            centre_tap(1, val, m)
                        if m >= 2:
                            hidden(m - 2)
                    hidden(2)
                    hidden(3)

                for_turns(e, s_up, turn)

            def resid_squares(stage, g, n):
                for i in range(2):
                    e.wait_ge(resid, RES[stage] + 4 * g + 2 * i + 2)
                    square(e, n + 2 * g + i, x[:, 4 * g + 2 * i:4 * g + 2 * i + 2, :])

            def down_splits(stage, norm):
                at = BASE[stage] + LEAD + CPG
                end = BASE[stage] + 4 * (FT // 2) + LEAD
                for g in range(4):
                    e_g = BASE[stage] + (g + 1) * (FT // 2) + LEAD
                    to = min(e_g + CPG, end)
                    split_hi(e, at, to)
                    at = to
                    if norm != "fin":
                        resid_squares(stage, g, SQ[norm] )
                        continue
                    for i in range(2):
                        e.wait_ge(resid, RES[stage] + 4 * g + 2 * i + 2)
                        t = 4 * g + 2 * i
                        square(e, SQ[norm] + 2 * (2 * g + i), x[:, t:t + 2, :])
                        square(e, SQ[norm] + 2 * (2 * g + i) + 1, x[:, t:t + 2, :], vec("g_final", t, 2))

            ffn("up", "down", 0, True)
            down_splits("down", "fin")
            root(e, "fin")
            e.wait_ge(mix_ms, 2)
            e.activation(std[:], rinv[:, 1, :], ACT.Sqrt, bias=vec("eps")).then_inc(std_ready, 1)
            norm_hi_part(e, "mix2", SRC["mix2"][2])
            for g in range(2):
                for m in range(4):
                    e.wait_ge(sums_ready, SUMS["qa"] + 4 * g + m + 1)
                    e.activation(qa[:, 4 * g + m, :], tmp[:, m, :], ACT.Copy, scale=HD ** -0.5).then_inc(tmp_read, 1)
                if g == 0:
                    b = BASE["qa"] + CPG + LEAD
                    split_hi(e, b, b + CPG)
            b = BASE["kva"] + LEAD
            split_hi(e, b, b + CPG)
            e.wait_ge(weights_used, BASE["kva"] + CPG)
            for tt in range(2):
                e.activation(va[:, tt, :], ps[:, 2 + tt, 0:A_KV * HD], ACT.Copy).then_inc(rows_copied, 1)
            b = BASE["qkb"] + LEAD
            with e.Fori(0, 2) as j:
                split_hi(e, b, b + 2 * CPG, j, 2 * CPG)
            e.wait_ge(sums_ready, SUMS["qkb"] + 16)
            e.activation(qkb[:, 0:PAIRS, :], qkb[:, 0:PAIRS, :], ACT.Copy, scale=HD ** -0.5).then_inc(qb_scaled, 1)
            for g in range(2):
                b = BASE["vb"] + g * CPG + LEAD
                split_hi(e, b, b + CPG)
                e.wait_ge(weights_used, BASE["vb"] + (g + 1) * CPG)
                for tt in range(2):
                    e.activation(vb[:, tt, g * GW:(g + 1) * GW], ps[:, 4 * g + tt, :], ACT.Copy).then_inc(rows_copied, 1)
            b = BASE["gates"] + LEAD
            with e.Fori(0, 4) as j:
                for g in range(2):
                    split_hi(e, b + g * CPG, b + (g + 1) * CPG, j, 2 * CPG)
                    for m in range(4):
                        e.wait_ge(sums_ready, plus(SUMS["gates"] + 4 * g + m + 1, j, 8))
                        e.activation(gates[:, bass.ds(j * 8 + 4 * g + m, 1), :].rearrange("p a t -> p (a t)"),
                                     tmp[:, m, :], ACT.Sigmoid).then_inc(tmp_read, 1)
            e.wait_ge(tmp_read, 8 + 2 * KT)
            e.dma_start(dist[:], dist_tab).then_inc(s_dist, 16)
            for i in range(PAIRS + 2):
                if i < PAIRS:
                    e.wait_ge(sb_zb, i + 1)
                    if i >= 1:
                        e.wait_ge(sb_sp, i)
                    e.activation(lnb[:], zb[:, i % 3], ACT.Abs).then_inc(sb_step, 1)
                    e.wait_ge(sb_step, 2 * i + 1)
                    e.activation(lnb[:], lnb[:], ACT.Exp, scale=-1.0).then_inc(sb_step, 1)
                    e.wait_ge(sb_step, 2 * i + 2)
                    e.activation(lnb[:], lnb[:], ACT.Ln, bias=1.0).then_inc(sb_ln, 1)
                if 1 <= i <= PAIRS:
                    n = i - 1
                    e.wait_ge(sw_flip, i)
                    if n >= 2:
                        e.wait_ge(mixed2, 4 * (n - 1))
                    e.activation(saT[:, n % 2], ps[:, 0:2, 0:W3], ACT.Copy).then_inc(sw_flipc, 1)
                    e.wait_ge(sb_d, i)
                    e.activation(zb[:, n % 3], zb[:, n % 3], ACT.Exp).then_inc(sb_a, 1)
                if i < PAIRS:
                    e.wait_ge(sw_neg, 2 * (i + 1))
                    o = 4 * i
                    e.activation(small[:, 128:132], small[:, 132:136], ACT.Exp).then_inc(sw_exps, 1)
                    for h in range(2):
                        for b_ in range(2):
                            q = slice(0, P) if b_ == 0 else slice(P, W3)
                            k = 2 * h + b_
                            e.activation(sa[:, i % 2, h, q], sa[:, i % 2, h, q], ACT.Exp,
                                         bias=small[:, 136 + k:137 + k],
                                         accum_out=small[:, 140 + k:141 + k]).then_inc(sw_exps, 1)
                if i >= 2:
                    n = i - 2
                    for br in range(2):
                        e.wait_ge(mixed2, 2 * (2 * n + br + 1))
                        e.activation(pair[:, 8 * br + n, 0, :], ps[:, 6 + br, 0:T], ACT.Copy)\
                            .then_inc(o2_hi, 1)
            for g in range(4):
                b = BASE["bra"] + g * 4 + LEAD
                split_hi(e, b, b + 4)
            for g in range(4):
                b = BASE["brb"] + g * 4 + LEAD
                split_hi(e, b, b + 4)
                for m in range(4):
                    t = 4 * g + m
                    e.wait_ge(merged, t + 1)
                    e.activation(pair2[:, t, 0, :], gates[:, t, :], ACT.Copy).then_inc(m_hi, 1)
            at = BASE["out2"] + LEAD
            for g in range(4):
                at = upto(at, "out2", min((g + 2) * CPG, 4 * CPG))
                resid_squares("out2", g, SQ["ffn2"])
            root(e, "ffn2")
            norm_hi_part(e, "ffn2", SRC["ffn2"][2])
            ffn("up2", "down2", 1, False)
            down_splits("down2", "fin2")
            root(e, "fin2")

        @block.vector
        def _(e):
            e.wait_ge(s_vecs, 16)
            e.wait_ge(csplit_hi, 1)
            e.tensor_tensor(csplit[:, :, 2:4], csil[:], csplit[:, :, 0:2].bitcast(F32), ALU.subtract)\
                .then_inc(csplit_lo, 1)
            split_lo(e, 0, LEAD)
            for g in range(8):
                for i in range(4 if g else 0, CPG):
                    split_lo(e, LEAD + g * CPG + i, LEAD + g * CPG + i + 1)
                    if g in (1, 3):
                        add_square(e, SQ["x" if g == 1 else "ctx"] + i, tmp[:, 0:2, :], i == 0)
                if g == 3:
                    inv_rms(e, "x", 0)
                if g == 5:
                    inv_rms(e, "ctx", 1)
                if g < 7:
                    for i in range(4):
                        split_lo(e, LEAD + (g + 1) * CPG + i, LEAD + (g + 1) * CPG + i + 1)
                        if g in (0, 2):
                            add_square(e, SQ["x" if g == 0 else "ctx"] + i, tmp[:, 0:2, :], i == 0)
                e.wait_ge(mod_turned, g + 1)
                o = (KT + 4 * g) % (2 * KT)
                e.tensor_tensor(mod[:, :, o:o + 4], ps[:, 4 + g % 2, 0:8].rearrange("p (m v) -> p v m", v=2),
                                vec("b_mod", o, 4).unsqueeze(1).to_broadcast([P, 2, 4]), ALU.add)\
                    .then_inc(mod_ready, 1)
                if g == 3:
                    e.wait_ge(mod_ready, 4)
                    for w in range(2):
                        e.scalar_tensor_tensor(out=gain[:, w, :], in0=mod[:, w, SC1:SC1 + KT], scalar=1.0,
                                               in1=vec("g_attn", 0, KT), op0=ALU.add, op1=ALU.mult)\
                            .then_inc(gain_ready, 1)
            e.wait_ge(mod_ready, 8)
            e.wait_ge(gain_ready, 2)
            src, g_, dst, shift = SRC["x"]
            norm_apply(e, "x", src, g_, dst, shift)
            src, g_, dst, shift = SRC["ctx"]
            for i in range(CPG):
                split_lo(e, BASE["cq"] + LEAD + i, BASE["cq"] + LEAD + i + 1)
                for t in (2 * i, 2 * i + 1):
                    e.wait_ge(norm_lo, PAIRED["ctx"] + t - 3)
                    norm_scale(e, "ctx", t, src(t), g_(t), 1)
                for t in (2 * i, 2 * i + 1):
                    norm_lo_part(e, "ctx", t, dst, shift)

            def upto(a, stage, n):
                b = BASE[stage] + n + LEAD
                split_lo(e, a, b)
                return b

            def sum_out(bank, out):
                e.tensor_reduce(out, ps[:, bank, :].rearrange("p (s t) -> p t s", s=2), AX_X, ALU.add)\
                    .then_inc(sums_ready, 1)

            at = BASE["cq"] + LEAD + CPG
            e.wait_ge(weights_used, BASE["cq"] + CPG)
            for m in range(4):
                sum_out(m, cq[:, m, :])
            at = upto(at, "ckv", CPG - 1)
            e.wait_ge(weights_used, BASE["ckv"] + CPG)
            for s in range(2):
                for m in range(4):
                    sum_out(4 * (1 - s) + m, ckv[:, m, s, :])
            for t in range(RT):
                add_square(e, SQ["ckv"] + t, sq_acc[:, 0], t == 0)
            at = upto(at, "ckv", CPG)
            at = upto(at, "kr", 1)
            e.wait_ge(std_ready, NORM["ckv"][2] + 1)
            e.reciprocal(rinv[:], rinv[:]).then_inc(rinv_ready, 1)
            e.wait_ge(rinv_ready, NORM["ckv"][2] + 1)
            for t in range(RT + 1):
                if t < RT:
                    if t >= 2:
                        e.wait_ge(norm_lo, PAIRED["ckv"] + t - 1)
                    e.scalar_tensor_tensor(out=tmp[:, 2 * (t % 2):2 * (t % 2) + 2, :], in0=ckv[:, t],
                                           scalar=vec("g_kv", t), in1=rinv[:], op0=ALU.mult, op1=ALU.mult)\
                        .then_inc(scaled, 1)
                if t:
                    u = t - 1
                    e.wait_ge(norm_hi, PAIRED["ckv"] + u + 1)
                    e.tensor_tensor(ckvn[:, :, u, 1, :], tmp[:, 2 * (u % 2):2 * (u % 2) + 2, :],
                                    ckvn[:, :, u, 0, :].bitcast(F32), ALU.subtract).then_inc(norm_lo, 1)
            e.wait_ge(weights_used, BASE["kr"] + 2)
            e.wait_ge(s_tabs, 32)
            e.wait_ge(zeroed, 2)
            sum_out(4, qn[:, 3, :])
            sum_out(7, qn[:, 0, :])
            at = upto(at, "kr", 2)
            e.wait_ge(sums_ready, SUMS["kr"] + 2)
            e.tensor_copy(kre[0:64, 1, :], qn[0:64, 0, :]).then_inc(roped, 1)
            e.tensor_copy(kro[64:P, 1, :], qn[64:P, 0, :]).then_inc(roped, 1)
            inv_rms(e, "cq")
            norm_apply(e, "cq", SRC["cq"][0], SRC["cq"][1], SRC["cq"][2])
            at = upto(at, "qn", CPG)
            e.wait_ge(turned, 1)
            e.tensor_tensor(qn[:, 1, :], qn[:, 3, :], cos, ALU.mult).then_inc(rope_mul, 1)
            e.tensor_tensor(qn[:, 2, :], ps[:, 7, 0:T], sin, ALU.mult).then_inc(rope_mul, 1)
            e.wait_ge(rope_mul, 2)
            e.tensor_tensor(kre[0:64, 0, :], qn[0:64, 1, :], qn[0:64, 2, :], ALU.add).then_inc(roped, 1)
            e.tensor_tensor(kro[64:P, 0, :], qn[64:P, 1, :], qn[64:P, 2, :], ALU.add).then_inc(roped, 1)
            e.wait_ge(roped, 4)
            e.wait_ge(weights_used, BASE["qn"] + CPG)
            for m in range(4):
                sum_out(m, qn[:, m, :])
            at = upto(at, "kn", CPG - 1)
            e.wait_ge(weights_used, BASE["kn"] + CPG)
            for s in range(2):
                for m in range(4):
                    sum_out(4 * (1 - s) + m, kn[:, m, s, :])
            at = upto(at, "vn", CPG)
            at = upto(at, "f", CPG)
            for g in range(4):
                e.wait_ge(weights_used, BASE["uq"] + 2 * (g + 1))
                b = 4 * (g % 2)
                sum_out(b, qnope[:, 2 * g, :])
                sum_out(b + 1, qnope[:, 2 * g + 1, :])
                sum_out(b + 2, qrope[:, g, :])
                at = upto(at, "uq", 2 * (g + 1))
            late_bias(e, 1, 0, 8, 3)
            for g in range(4):
                e.wait_ge(turned, 2 + g)
                if g >= 2:
                    e.wait_ge(roped, 4 + 2 * (g - 1))
                e.tensor_tensor(tmp[:, g % 2, :], ps[:, g, 0:T], sin, ALU.mult).then_inc(rope_mul, 1)
                e.tensor_tensor(qrope[:, g, :], qrope[:, g, :], cos, ALU.mult).then_inc(roped, 1)
                e.wait_ge(rope_mul, 3 + g)
                e.wait_ge(roped, 5 + 2 * g)
                e.tensor_tensor(qrope[:, g, :], qrope[:, g, :], tmp[:, g % 2, :], ALU.add).then_inc(roped, 1)
            for g in range(FN_G):
                e.wait_ge(spec_done, g + 1)
                e.tensor_copy(spec[:, g, :], ps[:, g, 0:T]).then_inc(spec_copied, 1)
            for g in range(FN_G):
                e.wait_ge(o_hi, g + 1)
                e.tensor_tensor(pair[:, HEADS + g, 1, :], ps[:, 4 + g, 0:T], pair[:, HEADS + g, 0, :].bitcast(F32),
                                ALU.subtract).then_inc(o_lo, 1)
            for g in range(4):
                e.wait_ge(weights_used, BASE["ukv"] + 2 * (g + 1))
                for m in range(2):
                    for s in range(2):
                        sum_out(2 * m + s, knope[:, 2 * g + m, s, :])
                at = upto(at, "ukv", 2 * (g + 1))
            for i in range(HEADS + 2):
                if i == 1:
                    e.wait_ge(s_bias, 16 * NA_ROWS)
                    e.wait_ge(s_dft, 48)
                    for h in range(NA_H):
                        v = bias[:, h].rearrange("p t (a c) -> p (t a) c", c=GRID_W)
                        mk = tmp[:, 3, 0:GRID_W].unsqueeze(1).to_broadcast([P, 2 * NA_ROWS, GRID_W])
                        e.tensor_tensor(v, v, mk, ALU.add).then_inc(bias_masked, 1)
                if i < HEADS:
                    for t in range(2):
                        n = 2 * i + t
                        e.wait_ge(scores, n + 1)
                        if i >= MLA_H:
                            if i == MLA_H and t == 0:
                                e.wait_ge(bias_masked, NA_H)
                            e.wait_ge(flipped, n - 3)
                            pb, bk = prob[:, i % 2, t, :], ps[:, 2 * (i % 2) + t, :]
                            e.scalar_tensor_tensor(out=pb[:, 0:T], in0=bk[:, 0:T], scalar=NA_SCALE,
                                                   in1=bias[:, i - MLA_H, t, :], op0=ALU.mult, op1=ALU.add)\
                                .then_inc(biased, 1)
                            e.tensor_scalar(pb[:, T:2 * T], bk[:, T:2 * T], NA_SCALE, None, ALU.mult).then_inc(biased, 1)
                            e.wait_ge(biased, 2 * (n - 2 * MLA_H + 1))
                            e.tensor_reduce(small[:, n:n + 1], pb, AX_X, ALU.max).then_inc(maxed, 1)
                        else:
                            e.tensor_reduce(small[:, n:n + 1], ps[:, 2 * (i % 2) + t, :], AX_X, ALU.max)\
                                .then_inc(maxed, 1)
                        e.wait_ge(maxed, n + 1)
                        e.tensor_scalar(small[:, 24 + n:25 + n], small[:, n:n + 1],
                                        -(MLA_SCALE if i < MLA_H else 1.0), None, ALU.mult).then_inc(negmax, 1)
                if i >= 2:
                    h = i - 2
                    e.wait_ge(o_hi, FN_G + h + 1)
                    e.tensor_tensor(pair[:, h, 1, :], ps[:, 6 + h % 2, 0:T], pair[:, h, 0, :].bitcast(F32),
                                    ALU.subtract).then_inc(o_lo, 1)
                if i < HEADS:
                    for t in range(2):
                        n = 2 * i + t
                        e.wait_ge(exps, n + 1)
                        e.reciprocal(small[:, 72 + n:73 + n], small[:, 48 + n:49 + n]).then_inc(recips, 1)
                        e.wait_ge(recips, n + 1)
                        pb = prob[:, i % 2, t, :]
                        e.tensor_scalar(pb, pb, small[:, 72 + n:73 + n], None, ALU.mult).then_inc(probs, 1)
            late_bias(e, 2, 8, IN_X, 4)

            def residual(stage, g, gt, it=None, per_t=0, tiles=range(4)):
                for m in tiles:
                    t = 4 * g + m
                    if it is None:
                        xt = x[:, t, :]
                        gv = None if gt is None else modv(0, gt, t)
                    else:
                        xt = x[:, bass.ds(it * per_t + t, 1), :].rearrange("p a t -> p (a t)")
                        gv = None if gt is None else mod[:, 0, bass.ds(it * per_t + gt + t, 1)]
                    e.wait_ge(sums_ready, plus(SUMS[stage] + t + 1, it, per_t))
                    e.scalar_tensor_tensor(out=xt, in0=tmp[:, m, :], scalar=1.0 if gv is None else gv, in1=xt,
                                           op0=ALU.mult, op1=ALU.add).then_inc(resid, 1)

            def onto_x(at, stage, size, gt, end, squared):
                b = BASE[stage]
                for g in range(4):
                    split_lo(e, at, b + (g + 1) * size + LEAD)
                    at = max(at, b + (g + 1) * size + LEAD)
                    e.wait_ge(weights_used, b + (g + 1) * size)
                    if stage == "out" and g == 0:
                        e.wait_ge(x_again, 16)
                    for m in range(4):
                        if g:
                            e.wait_ge(resid, RES[stage] + 4 * (g - 1) + m + 1)
                        sum_out(4 * (g % 2) + m, tmp[:, m, :])
                        if m:
                            residual(stage, g, gt, tiles=[m - 1])
                        split_lo(e, at, min(at + 2, end))
                        at = min(at + 2, end)
                    residual(stage, g, gt, tiles=[3])
                    squared(g)
                return at

            def squared(name):
                def add(g):
                    for i in range(2):
                        add_square(e, SQ[name] + 2 * g + i, sq_acc[:, 0], g == 0 and i == 0)
                return add

            e.memset(late[:, 0:4, :], 0.0).then_inc(late_zero, 1)
            e.wait_ge(late_zero, 1)
            at = onto_x(at, "out", CPG, GT1, BASE["up"] + LEAD, squared("ffn"))
            late_bias(e, 3, IN_X, 12, 2)
            e.wait_ge(late_mod, 3)
            e.scalar_tensor_tensor(out=gain[:, 2, :], in0=mod[:, 0, SC2:SC2 + KT], scalar=1.0,
                                   in1=vec("g_ffn", 0, KT), op0=ALU.add, op1=ALU.mult).then_inc(gain_ready, 1)
            e.wait_ge(gain_ready, 3)
            inv_rms(e, "ffn")
            norm_apply(e, "ffn", *SRC["ffn"])

            def ffn(s_up, s_down, n_ffn, conv, gt, then):
                u = SUMS[s_up]

                def turn(j, j0):
                    b = BASE[s_up] + TURN * j0

                    def taps(group, buf, m):
                        e.wait_ge(centre, plus(4 * group + m + 1 + 8 * j0, j, 8))
                        e.scalar_tensor_tensor(out=buf[:, m, 1:T], in0=tmp[:, m, 0:T - 1],
                                               scalar=vec("conv_w", FT * group + m + 4 * j0, 1, j, 4),
                                               in1=buf[:, m, 1:T], op0=ALU.mult, op1=ALU.add).then_inc(sides, 1)
                        e.wait_ge(sides, plus(8 * group + 2 * m + 1 + 16 * j0, j, 16))
                        e.scalar_tensor_tensor(out=buf[:, m, 0:T - 1], in0=tmp[:, m, 1:T],
                                               scalar=vec("conv_w", 4 * FT + FT * group + m + 4 * j0, 1, j, 4),
                                               in1=buf[:, m, 0:T - 1], op0=ALU.mult, op1=ALU.add)\
                            .then_inc(sides, 1)

                    def product(m):
                        if conv:
                            taps(1, val, m)
                            e.wait_ge(sides, plus(8 + 2 * m + 2 + 16 * j0, j, 16))
                            e.wait_ge(silu_done, plus(m + 1 + 4 * j0, j, 4))
                        else:
                            e.wait_ge(sums_ready, plus(u + 4 + m + 1 + 8 * j0, j, 8))
                        e.tensor_tensor(val[:, m, :], val[:, m, :] if conv else tmp[:, m, :], gate[:, m, :],
                                        ALU.mult).then_inc(prod, 1)

                    def hidden_low(m):
                        e.wait_ge(hid_hi, plus(44 * n_ffn + m + 1 + 4 * j0, j, 4))
                        hv = hid_tile(j, j0, m)
                        e.tensor_tensor(hv[:, 1, :], val[:, m, :], hv[:, 0, :].bitcast(F32), ALU.subtract)\
                            .then_inc(hid_lo, 1)

                    e.wait_ge(weights_used, plus(b + CPG, j, 2 * CPG))
                    for m in range(4):
                        sum_out(m, tmp[:, m, :])
                        if conv and m:
                            taps(0, gate, m - 1)
                        c = b + LEAD + CPG + 2 * m
                        split_lo(e, c, c + 2, j, 2 * CPG)
                    if conv:
                        taps(0, gate, 3)
                        e.wait_ge(sides, plus(8 + 16 * j0, j, 16))
                    e.wait_ge(weights_used, plus(b + 2 * CPG, j, 2 * CPG))
                    if conv and j is None:
                        late_bias(e, 4, 12, 16, 0)
                    for m in range(4):
                        if not conv:
                            e.wait_ge(silu_done, plus(44 * n_ffn + m + 1 + 4 * j0, j, 4))
                        sum_out(4 + m, tmp[:, m, :])
                        if m:
                            product(m - 1)
                        if m == 3:
                            hidden_low(0)
                        c = b + LEAD + 2 * CPG + 2 * m
                        split_lo(e, c, c + 2, j, 2 * CPG)
                    product(3)
                    for m in (1, 2, 3):
                        hidden_low(m)
                for_turns(e, s_up, turn)
                onto_x(BASE[s_down] + LEAD + CPG, s_down, FT // 2, gt, BASE[s_down] + 4 * (FT // 2) + LEAD, then)

            def squared_twice(g):
                for i in range(4):
                    add_square(e, SQ["fin"] + 4 * g + i, sq_acc[:, i % 2], g == 0 and i < 2, 2)

            ffn("up", "down", 0, True, GT2, squared_twice)
            inv_rms(e, "fin")
            e.tensor_tensor(rinv[:, 1, :], rinv[:, 0, :], rinv[:, 0, :], ALU.mult).then_inc(mix_ms, 1)
            e.wait_ge(mix_ms, 1)
            e.wait_ge(sq_sum, 6)
            e.scalar_tensor_tensor(out=rinv[:, 1, :], in0=ps[:, STAT["mix2"], 0:T], scalar=1.0 / D, in1=rinv[:, 1, :],
                                   op0=ALU.mult, op1=ALU.mult).then_inc(mix_ms, 1)

            def block1_out(t):
                e.scalar_tensor_tensor(out=x[:, t, :], in0=x[:, t, :], scalar=vec("g_final", t), in1=rinv[:, 0, :],
                                       op0=ALU.mult, op1=ALU.mult).then_inc(x_between, 1)
            for t in range(4):
                block1_out(t)
            inv_rms(e, "mix2", 1)
            for t in range(KT + 2):
                if t + 4 < KT:
                    block1_out(t + 4)
                if t < KT:
                    if t >= 4:
                        e.wait_ge(norm_lo, PAIRED["mix2"] + t - 3)
                    e.wait_ge(x_between, t + 1)
                    norm_scale(e, "mix2", t, x[:, t, :], vec("g_mix2", t), 1)
                if t >= 2:
                    norm_lo_part(e, "mix2", t - 2, SRC["mix2"][2])
                    next_split(e, "mix2", t - 2, split_lo)
            for g in range(2):
                if g:
                    b = BASE["qa"] + CPG + LEAD
                    split_lo(e, b, b + CPG)
                e.wait_ge(weights_used, BASE["qa"] + (g + 1) * CPG)
                if g:
                    e.wait_ge(tmp_read, 4)
                for m in range(4):
                    sum_out(4 * g + m, tmp[:, m, :])
            b = BASE["kva"] + LEAD
            split_lo(e, b, b + CPG)
            e.wait_ge(weights_used, BASE["kva"] + CPG)
            for m in range(2):
                sum_out(m, ka[:, m, :])
            b = BASE["qkb"]
            with e.Fori(0, 2) as j:
                for g in range(2):
                    split_lo(e, b + LEAD + g * CPG, b + LEAD + (g + 1) * CPG, j, 2 * CPG)
                    e.wait_ge(weights_used, plus(b + (g + 1) * CPG, j, 2 * CPG))
                    for m in range(4):
                        sum_out(4 + m if g == 0 else m,
                                qkb[:, bass.ds(j * 8 + 4 * g + m, 1), :].rearrange("p a t -> p (a t)"))
            b = BASE["vb"] + LEAD
            split_lo(e, b, b + 2 * CPG)
            b = BASE["gates"]
            with e.Fori(0, 4) as j:
                for g in range(2):
                    split_lo(e, b + LEAD + g * CPG, b + LEAD + (g + 1) * CPG, j, 2 * CPG)
                    e.wait_ge(weights_used, plus(b + (g + 1) * CPG, j, 2 * CPG))
                    e.wait_ge(tmp_read, plus(8 + 4 * g, j, 8))
                    for m in range(4):
                        sum_out(4 * g + m, tmp[:, m, :])
            e.wait_ge(tmp_read, 8 + 2 * KT)
            e.wait_ge(s_dist, 16)
            e.wait_ge(s_stick, 16)
            for i in range(PAIRS + 2):
                if i < PAIRS:
                    e.wait_ge(sw_scores, 2 * (i + 1))
                    if i >= 2:
                        e.wait_ge(sw_flip, i - 1)
                    for h in range(2):
                        s = -SLOPES[2 * i + h]
                        o = sa[:, i % 2, h]
                        e.scalar_tensor_tensor(out=o[:, 0:P], in0=dist[:, P:2 * P], scalar=s, in1=ps[:, h, 0:P],
                                               op0=ALU.mult, op1=ALU.add).then_inc(sw_biased, 1)
                        e.scalar_tensor_tensor(out=o[:, P:W3], in0=dist[:], scalar=s, in1=ps[:, h, P:W3],
                                               op0=ALU.mult, op1=ALU.add).then_inc(sw_biased, 1)
                    e.wait_ge(sb_z, 2 * (i + 1))
                    if i >= 3:
                        e.wait_ge(mixed2, 4 * (i - 2))
                    mk = stick[:, 0:W3].unsqueeze(1).to_broadcast([P, 2, W3])
                    e.tensor_tensor(zb[:, i % 3], ps[:, 2:4, 0:W3], mk, ALU.add).then_inc(sb_zb, 1)
                if 1 <= i <= PAIRS:
                    n = i - 1
                    e.wait_ge(sb_suffix, i)
                    e.tensor_tensor(zb[:, n % 3], zb[:, n % 3], ps[:, 4:6, 0:W3], ALU.subtract).then_inc(sb_d, 1)
                if i < PAIRS:
                    e.wait_ge(sw_biased, 4 * (i + 1))
                    if i:
                        e.wait_ge(sw_probs, 4 * i)
                    mx = small[:, 144:148].rearrange("p (h b) -> p h b", b=2)
                    e.tensor_reduce(mx[:, :, 0], sa[:, i % 2, :, 0:P], AX_X, ALU.max).then_inc(sw_max, 1)
                    e.tensor_reduce(mx[:, :, 1], sa[:, i % 2, :, P:W3], AX_X, ALU.max).then_inc(sw_max, 1)
                    e.wait_ge(sw_max, 3 * i + 2)
                    sk = vec("sink", 4 * i, 4)
                    e.tensor_tensor(small[:, 144:148], small[:, 144:148], sk, ALU.max).then_inc(sw_max, 1)
                    e.wait_ge(sw_max, 3 * i + 3)
                    e.tensor_tensor(small[:, 132:136], sk, small[:, 144:148], ALU.subtract).then_inc(sw_neg, 1)
                    e.tensor_scalar(small[:, 136:140], small[:, 144:148], -1.0, None, ALU.mult).then_inc(sw_neg, 1)
                    e.wait_ge(sb_ln, i + 1)
                    if i >= 2:
                        e.wait_ge(sb_suffix, i - 1)
                    e.scalar_tensor_tensor(out=sp_[:, i % 2], in0=zb[:, i % 3], scalar=0.0, in1=lnb[:],
                                           op0=ALU.max, op1=ALU.add).then_inc(sb_sp, 1)
                    e.wait_ge(sw_exps, 5 * (i + 1))
                    e.tensor_tensor(small[:, 148:152], small[:, 140:144], small[:, 128:132], ALU.add).then_inc(sw_sum, 1)
                    e.wait_ge(sw_sum, 2 * i + 1)
                    e.reciprocal(small[:, 152:156], small[:, 148:152]).then_inc(sw_sum, 1)
                    e.wait_ge(sw_sum, 2 * i + 2)
                    for h in range(2):
                        for b_ in range(2):
                            q = slice(0, P) if b_ == 0 else slice(P, W3)
                            k = 2 * h + b_
                            e.tensor_scalar(sa[:, i % 2, h, q], sa[:, i % 2, h, q], small[:, 152 + k:153 + k], None,
                                            ALU.mult).then_inc(sw_probs, 1)
                if i >= 2:
                    n = i - 2
                    for br in range(2):
                        e.wait_ge(o2_hi, 2 * n + br + 1)
                        e.tensor_tensor(pair[:, 8 * br + n, 1, :], ps[:, 6 + br, 0:T],
                                        pair[:, 8 * br + n, 0, :].bitcast(F32), ALU.subtract).then_inc(o2_lo, 1)
            for br, stage in enumerate(("bra", "brb")):
                for g in range(4):
                    b = BASE[stage] + g * 4
                    split_lo(e, b + LEAD, b + LEAD + 4)
                    e.wait_ge(weights_used, b + 4)
                    if br or g:
                        e.wait_ge(gated, 16 * br + 4 * g)
                    for m in range(4):
                        sum_out(4 * (g % 2) + m, tmp[:, m, :])
                    for m in range(4):
                        t = 16 * br + 4 * g + m
                        e.wait_ge(sums_ready, SUMS[stage] + 4 * g + m + 1)
                        e.tensor_tensor(gates[:, t, :], gates[:, t, :], tmp[:, m, :], ALU.mult).then_inc(gated, 1)
                    if br:
                        for m in range(4):
                            t = 4 * g + m
                            e.wait_ge(gated, 16 + t + 1)
                            e.tensor_tensor(gates[:, t, :], gates[:, t, :], gates[:, 16 + t, :], ALU.add)\
                                .then_inc(merged, 1)
                        for m in range(4):
                            t = 4 * g + m
                            e.wait_ge(m_hi, t + 1)
                            e.tensor_tensor(pair2[:, t, 1, :], gates[:, t, :], pair2[:, t, 0, :].bitcast(F32),
                                            ALU.subtract).then_inc(m_lo, 1)
            onto_x(BASE["out2"] + LEAD, "out2", CPG, None, BASE["up2"] + LEAD, squared("ffn2"))
            inv_rms(e, "ffn2")
            norm_apply(e, "ffn2", SRC["ffn2"][0], SRC["ffn2"][1], SRC["ffn2"][2])
            ffn("up2", "down2", 1, False, None, squared("fin2"))
            inv_rms(e, "fin2")
            for t in range(KT):
                norm_scale(e, "fin2", t, x[:, t, :], vec("g_final2", t), out=x[:, t, :])

        @block.tensor
        def _(e):
            e.wait_ge(s_tabs, 32)
            e.wait_ge(csplit_lo, 1)

            def turn_mod(g):
                e.wait_ge(mod_rows, g + 1)
                if g >= 2:
                    e.wait_ge(mod_ready, g - 1)
                for m in range(4):
                    r = e.matmul(ps[:, 4 + g % 2, 2 * m:2 * m + 2], mrows[0:4, g % 2, m * P:(m + 1) * P], pick,
                                 start=True, stop=True)
                r.then_inc(mod_turned, 1)

            for g in range(8):
                def mod_jobs(kt, whi, wlo, first, last):
                    e.matmul(ps[0:4, g % 2, :], csplit[:, kt, :], whi, start=first, stop=False)
                    return e.matmul(ps[0:4, g % 2, :], csplit[:, kt, :], wlo, start=False, stop=last)

                def between(kt):
                    if kt == 0 and g >= 2:
                        e.wait_ge(mod_rows, g - 1)
                    if kt == 8 and g >= 1:
                        turn_mod(g - 1)
                group(e, g * CPG, CPG, 2, GW, mod_jobs, need=between)
                if g == 2:
                    sum_squares(e, 8, tmp[:, 0:2, :], STAT["x"])
                if g == 4:
                    sum_squares(e, 16, tmp[:, 0:2, :], STAT["ctx"])
            turn_mod(7)

            def wide(banks, acts, n=4):
                def jobs(kt, whi, wlo, first, last):
                    for m in range(n):
                        for bk, act in zip(banks, acts):
                            r = features(e, bk + m, whi[:, m * P:(m + 1) * P], wlo[:, m * P:(m + 1) * P], act(kt),
                                         first, last)
                    return r
                return jobs

            def px(kt):
                return pair[:, kt]

            def pc(kt):
                return ctxpair[:, kt]

            def normed(name):
                return lambda kt: e.wait_ge(norm_lo, PAIRED[name] + kt + 1)

            e.wait_ge(std_ready, 2)
            e.wait_ge(mod_rows, 8)
            e.wait_ge(mod_ready, 8)
            group(e, BASE["cq"], CPG, 2, GW, wide([0], [px]), need=normed("x"))
            e.wait_ge(sums_ready, SUMS["cq"] + 4)
            group(e, BASE["ckv"], CPG, 2, GW, wide([4, 0], [px, pc]), need=normed("ctx"))
            e.wait_ge(sums_ready, SUMS["ckv"] + 4)

            def kr_jobs(kt, whi, wlo, first, last):
                features(e, 4, whi, wlo, px(kt), first, last)
                return features(e, 7, whi, wlo, pc(kt), first, last)

            def ckv_squares(kt):
                if kt == 8:
                    e.wait_ge(sq_added, SQ["ckv"] + RT)
                    e.matmul(ps[:, STAT["ckv"], :], ones, sq_acc[:, 0].rearrange("p s t -> p (s t)"), start=True,
                             stop=True).then_inc(sq_sum, 1)
            group(e, BASE["kr"], 2, 8, P, kr_jobs, need=ckv_squares)
            e.wait_ge(std_ready, NORM["ckv"][2] + 1)
            stats(e, "cq")
            e.wait_ge(sums_ready, SUMS["ckv"] + 8)
            group(e, BASE["qn"], CPG, 2, GW, wide([0], [px]))
            e.wait_ge(sums_ready, SUMS["kr"] + 2)
            e.matmul(ps[:, 7, 0:T], rot, qn[:, 3, :], start=True, stop=True).then_inc(turned, 1)
            e.wait_ge(sums_ready, SUMS["qn"] + 4)
            e.wait_ge(std_ready, NORM["cq"][2] + 1)
            e.wait_ge(roped, 4)
            group(e, BASE["kn"], CPG, 2, GW, wide([4, 0], [px, pc]))
            e.wait_ge(sums_ready, SUMS["kn"] + 8)

            def vn_jobs(kt, whi, wlo, first, last):
                for tt in range(4):
                    r = tokens(e, ps[:, 4 + tt, :], whi, wlo, px(kt) if tt < 2 else pc(kt), tt % 2, first, last)
                return r
            group(e, BASE["vn"], CPG, 2, GW, vn_jobs)

            def f_jobs(kt, whi, wlo, first, last):
                for tt in range(2):
                    r = tokens(e, ps[:, tt, :], whi, wlo, px(kt), tt, first, last)
                return r
            group(e, BASE["f"], CPG, 2, GW, f_jobs)
            e.wait_ge(norm_lo, PAIRED["cq"] + RT)
            e.wait_ge(rows_copied, ROWS["f"] + 2)
            for g in range(4):
                if g >= 2:
                    e.wait_ge(sums_ready, SUMS["uq"] + 3 * (g - 1))

                def uq_jobs(kt, whi, wlo, first, last, b=4 * (g % 2)):
                    for m in range(2):
                        s = slice(m * NOPE, (m + 1) * NOPE)
                        features(e, b + m, whi[:, s], wlo[:, s], cqn[:, kt], first, last)
                    s = slice(2 * NOPE, 2 * (NOPE + ROPE))
                    return features(e, b + 2, whi[:, s], wlo[:, s], cqn[:, kt], first, last)
                group(e, BASE["uq"] + 2 * g, 2, 2, 2 * (NOPE + ROPE), uq_jobs)
            late_sums(e, 0, 8, 3)
            e.wait_ge(sums_ready, SUMS["uq"] + 12)
            e.wait_ge(late_mod, 1)
            for g in range(4):
                e.matmul(ps[:, g, 0:T], rot, qrope[:, g, :], start=True, stop=True).then_inc(turned, 1)
            e.wait_ge(s_dft, 32)
            for g in range(FN_G):
                for tt in range(2):
                    m = e.matmul(ps[:, 4 + g, :], f_sb[:, tt, g * P:(g + 1) * P], dft[:, 2 * T * tt:2 * T * (tt + 1)],
                                 start=(tt == 0), stop=(tt == 1))
                m.then_inc(uv_done, 1)
            e.wait_ge(roped, 12)
            for g in range(FN_G):
                e.wait_ge(uv_copied, g + 1)
                for s in range(2):
                    m = e.matmul(ps[:, g, 0:T], dft[:, 4 * T + s * P:4 * T + (s + 1) * P], uv[:, g, s * T:(s + 1) * T],
                                 start=(s == 0), stop=(s == 1))
                m.then_inc(spec_done, 1)
            for g in range(FN_G):
                e.wait_ge(spec_copied, g + 1)
                e.matmul(ps[:, 4 + g, 0:T], wfn[:, g, :], spec[:, g, :], start=True, stop=True).then_inc(fn_done, 1)
            e.wait_ge(o_lo, FN_G)
            e.wait_ge(norm_lo, PAIRED["ckv"] + RT)
            for g in range(4):
                if g:
                    e.wait_ge(sums_ready, SUMS["ukv"] + 4 * g)
                    e.wait_ge(rows_copied, ROWS["ukv"] + 4 * g)

                def ukv_jobs(kt, whi, wlo, first, last):
                    for m in range(2):
                        s = slice(m * (NOPE + VD), m * (NOPE + VD) + NOPE)
                        for st in range(2):
                            features(e, 2 * m + st, whi[:, s], wlo[:, s], ckvn[:, st, kt], first, last)
                    wv = [w.rearrange("p (m n) -> p m n", m=2)[:, :, NOPE:] for w in (whi, wlo)]
                    for tt in range(4):
                        out = ps[:, 4 + tt, 0:2 * VD].rearrange("p (m n) -> p m n", m=2)
                        r = tokens(e, out, wv[0], wv[1], ckvn[:, tt // 2, kt], tt % 2, first, last)
                    return r
                group(e, BASE["ukv"] + 2 * g, 2, 2, GW, ukv_jobs)
            e.wait_ge(sums_ready, SUMS["ukv"] + 16)
            e.wait_ge(rows_copied, ROWS["ukv"] + 16)
            def out_chunks(a, b):
                jobs = wide([0], [px])
                for c in range(a, b):
                    e.wait_ge(lo_ready, BASE["out"] + c + 1)
                    e.wait_ge(o_lo, FN_G + min(2 * c + 2, HEADS) if c < HEADS // 2 else FN_G + HEADS)
                    for k in range(2):
                        kt = 2 * c + k
                        last = jobs(kt, split_view(hi, BASE["out"] + c, 2, GW)[:, k],
                                    split_view(lo, BASE["out"] + c, 2, GW)[:, k], kt == 0, kt == KT - 1)
                    last.then_inc(weights_used, 1)

            for i in range(HEADS + 2):
                if i == HEADS:
                    e.wait_ge(biased, 2 * 2 * NA_H)
                    e.wait_ge(exps, 2 * HEADS - 2 * NA_H)
                    out_chunks(0, 2)
                if i == HEADS + 1:
                    out_chunks(2, 4)
                if i < HEADS:
                    if i >= 2:
                        e.wait_ge(exps, 2 * (i - 1))
                    for t in range(2):
                        q, out = slice(t * P, (t + 1) * P), ps[:, 2 * (i % 2) + t, :]
                        if i < MLA_H:
                            e.matmul(out, qnope[:, i, q], knope[:, i].rearrange("p s t -> p (s t)"), start=True,
                                     stop=False)
                            kr = kro if i % 2 else kre
                            m = e.matmul(out, qrope[:, i // 2, q], kr[:].rearrange("p s t -> p (s t)"), start=False,
                                         stop=True)
                        else:
                            h = i - MLA_H
                            m = e.matmul(out, qn[:, h, q], kn[:, h].rearrange("p s t -> p (s t)"), start=True,
                                         stop=True)
                        m.then_inc(scores, 1)
                if 1 <= i <= HEADS:
                    h = i - 1
                    for t in range(2):
                        e.wait_ge(probs, 2 * h + t + 1)
                        if h >= 1:
                            e.wait_ge(flips_copied, 2 * h + t - 1)
                        for k in range(4):
                            m = e.transpose(ps[:, 4 + t, k * P:(k + 1) * P], prob[:, h % 2, t, k * P:(k + 1) * P],
                                            ident)
                        m.then_inc(flipped, 1)
                if i >= 2:
                    h = i - 2
                    e.wait_ge(flips_copied, 2 * h + 2)
                    if h >= 2:
                        e.wait_ge(o_lo, FN_G + h - 1)
                    for k in range(4):
                        v = v_sb[:, k, h * VD:(h + 1) * VD] if h < MLA_H else vn[:, k, (h - MLA_H) * P:(h - MLA_H + 1) * P]
                        m = e.matmul(ps[:, 6 + h % 2, 0:T], v, probT[:, h % 2, k, :], start=(k == 0), stop=(k == 3))
                    m.then_inc(mixed, 1)
            late_sums(e, 8, IN_X, 4)
            out_chunks(4, CPG)
            e.wait_ge(o_lo, FN_G + HEADS)
            e.wait_ge(late_mod, 2)
            for g in range(1, 4):
                if g >= 2:
                    e.wait_ge(sums_ready, SUMS["out"] + 4 * (g - 1))
                group(e, BASE["out"] + g * CPG, CPG, 2, GW, wide([4 * (g % 2)], [px]))
            e.wait_ge(sums_ready, SUMS["out"] + 12)
            late_sums(e, IN_X, 12, 2)
            sum_squares(e, 28, sq_acc[:, 0], STAT["ffn"])
            e.wait_ge(late_mod, 3)

            def ffn(s_up, s_down, n_ffn, name, stat_no):
                e.wait_ge(std_ready, stat_no)
                def turn(j, j0):
                    for g in range(2):
                        e.wait_ge(sums_ready, plus(SUMS[s_up] - 4 + 4 * g + 8 * j0, j, 8))
                        group(e, BASE[s_up] + (2 * j0 + g) * CPG, CPG, 2, GW, wide([4 * g], [px]), j, TURN,
                              need=normed(name))
                    if s_up == "up" and j is None:
                        late_sums(e, 12, 16, 0)
                        e.wait_ge(late_mod, 4)
                for_turns(e, s_up, turn)

                def hidden(kt):
                    e.wait_ge(hid_lo, 44 * n_ffn + kt + 1)
                with e.Fori(0, 2) as j:
                    for g in range(2):
                        e.wait_ge(sums_ready, plus(SUMS[s_down] - 4 + 4 * g, j, 8))
                        group(e, BASE[s_down] + g * FT // 2, FT // 2, 2, GW,
                              wide([4 * g], [lambda kt: hid[:, kt]]), j, FT, need=hidden)
                e.wait_ge(sums_ready, SUMS[s_down] + 16)

            ffn("up", "down", 0, "ffn", NORM["ffn"][2] + 1)
            sum_squares(e, 44, sq_acc[:, 0], STAT["fin"])
            sum_squares(e, 44, sq_acc[:, 1], STAT["mix2"])
            for g in range(2):
                group(e, BASE["qa"] + g * CPG, CPG, 2, GW, wide([4 * g], [px]), need=normed("mix2"))
            e.wait_ge(sums_ready, SUMS["qa"] + 4)

            def kva_jobs(kt, whi, wlo, first, last):
                for m in range(2):
                    features(e, m, whi[:, m * P:(m + 1) * P], wlo[:, m * P:(m + 1) * P], px(kt), first, last)
                for tt in range(2):
                    r = tokens(e, ps[:, 2 + tt, 0:T], whi[:, T:2 * T], wlo[:, T:2 * T], px(kt), tt, first, last)
                return r
            group(e, BASE["kva"], CPG, 2, GW, kva_jobs)
            e.wait_ge(rows_copied, ROWS["kva"] + 2)
            e.wait_ge(sums_ready, SUMS["kva"] + 2)
            with e.Fori(0, 2) as j:
                for g in range(2):
                    e.wait_ge(sums_ready, plus(SUMS["qkb"] - 4 + 4 * g, j, 8))
                    group(e, BASE["qkb"] + g * CPG, CPG, 2, GW, wide([4 - 4 * g], [px]), j, 2 * CPG)
            e.wait_ge(sums_ready, SUMS["qkb"] + 16)
            for g in range(2):
                def vb_jobs(kt, whi, wlo, first, last, g=g):
                    for tt in range(2):
                        r = tokens(e, ps[:, 4 * g + tt, :], whi, wlo, px(kt), tt, first, last)
                    return r
                group(e, BASE["vb"] + g * CPG, CPG, 2, GW, vb_jobs)
            e.wait_ge(rows_copied, ROWS["vb"] + 4)
            with e.Fori(0, 4) as j:
                for g in range(2):
                    e.wait_ge(sums_ready, plus(SUMS["gates"] - 4 + 4 * g, j, 8))
                    group(e, BASE["gates"] + g * CPG, CPG, 2, GW, wide([4 * g], [px]), j, 2 * CPG)
            e.wait_ge(sums_ready, SUMS["gates"] + 32)
            e.wait_ge(qb_scaled, 1)
            e.wait_ge(s_stick, 16)
            tri = stick[:, W3:W3 + P]
            def bra_chunk(c):
                jobs = wide([0], [px])
                e.wait_ge(lo_ready, BASE["bra"] + c + 1)
                e.wait_ge(o2_lo, 4 * c + 3)
                for k in range(2):
                    kt = 2 * c + k
                    last = jobs(kt, split_view(hi, BASE["bra"] + c, 2, GW)[:, k],
                                split_view(lo, BASE["bra"] + c, 2, GW)[:, k], kt == 0, kt == PAIRS - 1)
                last.then_inc(weights_used, 1)

            for i in range(PAIRS + 2):
                if i < PAIRS:
                    if i == 1:
                        e.wait_ge(sw_biased, 4)
                    if i >= 2:
                        e.wait_ge(sw_flipc, i - 1)
                    for h in range(2):
                        hq = 2 * i + h
                        kv = hq // 4
                        r = slice(HD * (kv % 2), HD * (kv % 2 + 1))
                        qt = qa[r, 4 * (kv // 2) + hq % 4, :]
                        kt_ = ka[r, kv // 2, :]
                        e.matmul(ps[:, h, 0:P], qt[:, 0:P], kt_[:, 0:P], start=True, stop=True)
                        e.matmul(ps[:, h, P:W3], qt[:, P:2 * P], kt_, start=True, stop=True).then_inc(sw_scores, 1)
                    if i:
                        e.wait_ge(sb_zb, i)
                    for h in range(2):
                        r = slice(HD * h, HD * (h + 1))
                        q, k = qkb[r, i, :], qkb[r, PAIRS + i, :]
                        e.matmul(ps[:, 2 + h, 0:T], k[:, 0:P], q, start=True, stop=True)
                        e.matmul(ps[:, 2 + h, T:W3], k[:, P:2 * P], q[:, P:2 * P], start=True, stop=True)\
                            .then_inc(sb_z, 1)
                if 1 <= i <= PAIRS:
                    n = i - 1
                    e.wait_ge(sb_sp, i)
                    if n:
                        e.wait_ge(sb_d, n)
                    for h in range(2):
                        s = sp_[:, n % 2, h]
                        out = ps[:, 4 + h, :]
                        e.matmul(out[:, 0:P], tri, s[:, 0:P], start=True, stop=True)
                        e.matmul(out[:, P:T], tri, s[:, P:T], start=True, stop=False)
                        e.matmul(out[:, P:T], ones, s[:, T:W3], start=False, stop=True)
                        m = e.matmul(out[:, T:W3], tri, s[:, T:W3], start=True, stop=True)
                    m.then_inc(sb_suffix, 1)
                    e.wait_ge(sw_probs, 4 * i)
                    if i < PAIRS:
                        e.wait_ge(sw_biased, 4 * (i + 1))
                    if n:
                        e.wait_ge(sw_flipc, n)
                    for h in range(2):
                        for dst, src in ((0, 0), (1, 1), (2, 2)):
                            m = e.transpose(ps[:, h, dst * P:(dst + 1) * P], sa[:, n % 2, h, src * P:(src + 1) * P],
                                            ident)
                    m.then_inc(sw_flip, 1)
                if i == PAIRS + 1:
                    e.wait_ge(sb_d, PAIRS)
                    for c in range(3):
                        e.wait_ge(sw_flipc, PAIRS)
                        e.wait_ge(sb_zb, PAIRS)
                        bra_chunk(c)
                if i >= 2:
                    n = i - 2
                    c0 = slice(0, P)
                    c1 = slice(P, T)
                    for br in range(2):
                        if br == 0:
                            e.wait_ge(sw_flipc, n + 1)
                        else:
                            e.wait_ge(sb_a, n + 1)
                        if n:
                            e.wait_ge(o2_lo, 2 * (n - 1) + br + 1)
                        for h in range(2):
                            hq = 2 * n + h
                            r = slice(HD * h, HD * (h + 1))
                            pt = saT[:, n % 2, h] if br == 0 else zb[:, n % 3, h]
                            vv = va if br == 0 else vb
                            hv = hq // 4 if br == 0 else hq
                            v = [vv[:, tt, hv * HD:(hv + 1) * HD] for tt in range(2)]
                            e.matmul(ps[r, 6 + br, c0], v[0], pt[:, 0:P], start=True, stop=True)
                            e.matmul(ps[r, 6 + br, c1], v[0], pt[:, P:T], start=True, stop=False)
                            e.matmul(ps[r, 6 + br, c1], v[1], pt[:, T:W3], start=False, stop=True)\
                                .then_inc(mixed2, 1)
            bra_chunk(3)
            e.wait_ge(o2_lo, 2 * PAIRS)
            for br, stage in enumerate(("bra", "brb")):
                for g in range(0 if br else 1, 4):
                    if br or g >= 2:
                        e.wait_ge(sums_ready, SUMS[stage] + 4 * (g - 1))
                    group(e, BASE[stage] + 4 * g, 4, 2, GW, wide([4 * (g % 2)], [lambda kt: pair[:, 8 * br + kt]]))
            e.wait_ge(m_lo, KT)
            with e.Fori(0, 2) as j:
                for g in range(2):
                    e.wait_ge(sums_ready, plus(SUMS["out2"] - 4 + 4 * g, j, 8))
                    group(e, BASE["out2"] + g * CPG, CPG, 2, GW, wide([4 * g], [lambda kt: pair2[:, kt]]), j, 2 * CPG)
            sum_squares(e, 52, sq_acc[:, 0], STAT["ffn2"])
            ffn("up2", "down2", 1, "ffn2", NORM["ffn2"][2] + 1)
            sum_squares(e, 60, sq_acc[:, 0], STAT["fin2"])


_ORDER = ("xT", "ctxT", "vecs", "w_mod", "w_in", "w_uq", "w_ukv", "rpb", "w_fnet", "w_out", "w_up", "w_down",
          "w_in2", "w_bra", "w_brb", "w_out2", "w_up2", "w_down2",
          "base_tab", "rope_tab", "dft_tab", "na_mask", "stick_tab", "dist_tab")


def toeplitz(rpb):
    wide = np.zeros(rpb.shape[:2] + (2 * GRID_W - 1,), rpb.dtype)
    o = GRID_W - NA_KW
    wide[:, :, o:o + 2 * NA_KW - 1] = rpb
    return np.stack([wide[:, :, GRID_W - 1 - w:2 * GRID_W - 1 - w] for w in range(GRID_W)])


def lay_out(inputs):
    g = {k: np.asarray(v) for k, v in inputs.items()}

    def cols(v):
        return np.ascontiguousarray(v.reshape(-1, P).T)

    vecs = np.zeros((P, NV), np.float32)

    def put(name, v):
        o, n = VEC[name]
        vecs[:, o:o + n] = v

    put("c", cols(g["c"]))
    put("c_ctx", cols(g["c_ctx"]))
    put("b_mod", cols(g["b_mod"]))
    put("g_attn", cols(g["g_attn"]))
    put("g_ffn", cols(g["g_ffn"]))
    put("g_q", cols(g["g_q"]))
    put("g_kv", cols(g["g_kv"]))
    put("conv_w", cols(g["conv_w"]))
    put("conv_b", cols(g["conv_b"]))
    put("g_final", cols(g["g_final"]))
    put("g_mix2", cols(g["norm_mix_g_2"]))
    put("g_ffn2", cols(g["norm_ffn_g_2"]))
    put("g_final2", cols(g["norm_final_g_2"]))
    put("sink", np.broadcast_to(np.repeat(g["sink_logits_2"].reshape(-1), 2), (P, 2 * A_H)))
    put("eps", np.float32(EPS))
    out = dict(
        xT=np.ascontiguousarray(g["x"][0].T), ctxT=np.ascontiguousarray(g["ctx"][0].T), vecs=vecs,
        w_mod=g["w_mod"][0], w_in=g["w_in"][0], w_uq=g["w_uq"][0], w_ukv=g["w_ukv"][0], rpb=toeplitz(g["na_rpb"][0]),
        w_fnet=g["w_fnet"][0], w_out=g["w_out"][0], w_up=g["w_up"][0], w_down=g["w_down"][0],
        w_in2=g["w_in_2"][0], w_bra=g["w_branch_a_2"][0], w_brb=g["w_branch_b_2"][0], w_out2=g["w_out_2"][0],
        w_up2=g["w_ffn_in_2"][0], w_down2=g["w_ffn_down_2"][0])
    out.update(host_tables())
    return out


def kernel(**inputs):
    import concourse.bacc as bacc
    from concourse.bass_utils import run_bass_kernel_spmd

    arrays = lay_out(inputs)
    nc = bacc.Bacc("TRN2", target_bir_lowering=False, num_devices=1)
    maps, args = {}, []
    for name in _ORDER:
        a = np.ascontiguousarray(arrays[name])
        maps[f"in_{name}"] = a
        args.append(nc.dram_tensor(f"in_{name}", a.shape, mybir.dt.from_np(a.dtype), kind="ExternalInput").ap())
    args.append(nc.dram_tensor("outT", (D, T), F32, kind="ExternalOutput").ap())
    two_blocks(nc, *args)
    r = run_bass_kernel_spmd(nc, [maps], core_ids=[0])
    return np.ascontiguousarray(r.results[0]["outT"].T)[None]
```
